# Optimizing a Trainium2 kernel written in Bass

```python
import math
import jax, jax.numpy as jnp
from jax import lax
import numpy as np

D_MODEL = 2048
BATCH = 1
SEQ = 256
DEPTH = 2

N_MIXERS = 2
N_S5 = (DEPTH + 1) // 2
N_DSA = DEPTH // 2
S5_GROUP = 16
S5_GROUPS = D_MODEL // S5_GROUP
S5_STATE = 64
DT_MIN = 0.001
DT_MAX = 0.1
N_HEADS = 16
HEAD_DIM = D_MODEL // N_HEADS
IDX_HEADS = 16
IDX_DIM = 64
TOPK_MAX = 256
Q_BLOCK = 128
ROPE_THETA = 10000.0
DSA_IN = 3 * D_MODEL + IDX_HEADS * IDX_DIM + IDX_HEADS + IDX_DIM
D_FF = ((8 * D_MODEL // 3 + 255) // 256) * 256
ALPHA = (2.0 * DEPTH) ** 0.25
BETA = (8.0 * DEPTH) ** -0.25
LN_EPS = 1e-5

kernel_name = "hybrid_s5_dsa_deepnorm_adaln"

def layer_norm(x, g, b):
    xf = x.astype(jnp.float32)
    mu = jnp.mean(xf, axis=-1, keepdims=True)
    var = jnp.mean(jnp.square(xf - mu), axis=-1, keepdims=True)
    y = (xf - mu) * lax.rsqrt(var + LN_EPS)
    return (y * g.astype(jnp.float32) + b.astype(jnp.float32)).astype(x.dtype)

def rope_tables(positions, dim):
    inv = 1.0 / (ROPE_THETA ** (jnp.arange(0, dim, 2, dtype=jnp.float32) / dim))
    ang = positions.astype(jnp.float32)[..., None] * inv
    return jnp.cos(ang), jnp.sin(ang)

def apply_rope(x, cos, sin):
    half = x.shape[-1] // 2
    xf = x.astype(jnp.float32)
    x1, x2 = xf[..., :half], xf[..., half:]
    cs, sn = cos[:, :, None, :], sin[:, :, None, :]
    return jnp.concatenate([x1 * cs - x2 * sn, x2 * cs + x1 * sn], axis=-1).astype(x.dtype)

def s5_mixer(h, in_w, a_re, a_im, log_dt, b_re, b_im, c_re, c_im, d_skip, glu_w, glu_b):
    Bsz, L, D = h.shape
    f32 = jnp.float32
    u = h @ in_w
    ug = u.reshape(Bsz, L, S5_GROUPS, S5_GROUP).astype(f32).astype(jnp.complex64)
    lam = lax.complex(a_re.astype(f32), a_im.astype(f32))
    dt = jnp.exp(log_dt.astype(f32))[:, None]
    lam_bar = jnp.exp(lam * dt)
    bmat = lax.complex(b_re.astype(f32), b_im.astype(f32))
    b_bar = ((lam_bar - 1.0) / lam)[..., None] * bmat
    bu = jnp.einsum('gnp,blgp->lbgn', b_bar, ug)
    a_seq = jnp.broadcast_to(lam_bar, (L,) + lam_bar.shape)

    def combine(left, right):
        a_l, b_l = left
        a_r, b_r = right
        return a_r * a_l, a_r[:, None] * b_l + b_r

    _, states = lax.associative_scan(combine, (a_seq, bu), axis=0)
    cmat = lax.complex(c_re.astype(f32), c_im.astype(f32))
    y = jnp.real(jnp.einsum('gpn,lbgn->blgp', cmat, states)).reshape(Bsz, L, D)
    y = y + d_skip.astype(f32) * u.astype(f32)
    g = jax.nn.gelu(y).astype(h.dtype)
    z = g @ glu_w + glu_b
    val, gate = jnp.split(z, 2, axis=-1)
    return val * jax.nn.sigmoid(gate)

def dsa_mixer(h, cos_h, sin_h, cos_i, sin_i, in_w, out_w):
    Bsz, L, D = h.shape
    f32 = jnp.float32
    k_top = min(TOPK_MAX, L // 4)
    proj = h @ in_w
    q, k, v, qi, wi, ki = jnp.split(
        proj, [D, 2 * D, 3 * D, 3 * D + IDX_HEADS * IDX_DIM, 3 * D + IDX_HEADS * IDX_DIM + IDX_HEADS], axis=-1)
    q = apply_rope(q.reshape(Bsz, L, N_HEADS, HEAD_DIM), cos_h, sin_h)
    k = apply_rope(k.reshape(Bsz, L, N_HEADS, HEAD_DIM), cos_h, sin_h)
    v = v.reshape(Bsz, L, N_HEADS, HEAD_DIM)
    qi = apply_rope(qi.reshape(Bsz, L, IDX_HEADS, IDX_DIM), cos_i, sin_i)
    ki = apply_rope(ki[:, :, None, :], cos_i, sin_i)[:, :, 0, :]
    wi = wi * (IDX_HEADS ** -0.5)
    key_pos = jnp.arange(L)
    gather = jax.vmap(lambda arr, idx: arr[idx])

    def block(i):
        start = i * Q_BLOCK
        qb = lax.dynamic_slice_in_dim(q, start, Q_BLOCK, axis=1)
        qib = lax.dynamic_slice_in_dim(qi, start, Q_BLOCK, axis=1)
        wib = lax.dynamic_slice_in_dim(wi, start, Q_BLOCK, axis=1)
        qpos = start + jnp.arange(Q_BLOCK)
        causal = key_pos[None, :] <= qpos[:, None]
        s_idx = jnp.einsum('bqhd,bsd->bqhs', qib, ki, preferred_element_type=f32) * (IDX_DIM ** -0.5)
        score = jnp.einsum('bqh,bqhs->bqs', wib.astype(f32), jax.nn.relu(s_idx))
        score = jnp.where(causal[None], score, -jnp.inf)
        _, sel = lax.top_k(score, k_top)
        valid = sel <= qpos[None, :, None]
        kg = gather(k, sel)
        vg = gather(v, sel)
        logits = jnp.einsum('bqhd,bqkhd->bhqk', qb, kg, preferred_element_type=f32) * (HEAD_DIM ** -0.5)
        logits = jnp.where(valid[:, None], logits, -jnp.inf)
        p = jax.nn.softmax(logits, axis=-1).astype(v.dtype)
        ob = jnp.einsum('bhqk,bqkhd->bqhd', p, vg)
        return ob.reshape(Bsz, Q_BLOCK, D)

    out = lax.map(block, jnp.arange(L // Q_BLOCK))
    out = jnp.transpose(out, (1, 0, 2, 3)).reshape(Bsz, L, D)
    return out @ out_w

def swiglu(h, w_in, w_out):
    g, u = jnp.split(h @ w_in, 2, axis=-1)
    return (jax.nn.silu(g) * u) @ w_out

def setup_inputs(seed: int = 0) -> dict:
    key = jax.random.key(seed)
    ks = jax.random.split(key, 24)
    f32 = jnp.float32
    D = D_MODEL

    def nrm(k, shape, scale):
        return jax.random.normal(k, shape, f32) * scale

    x = nrm(ks[0], (BATCH, SEQ, D), 1.0)
    c = nrm(ks[1], (BATCH, D), 1.0)
    positions = (jax.random.randint(ks[2], (BATCH, 1), 0, 4096) + jnp.arange(SEQ)[None, :]).astype(jnp.int32)
    ada_w = nrm(ks[3], (DEPTH, D, 6 * D), 0.1 * D ** -0.5)
    ada_b = nrm(ks[4], (DEPTH, 6 * D), 0.01)
    ln_g = 1.0 + nrm(ks[5], (DEPTH, 2, D), 0.02)
    ln_b = nrm(ks[6], (DEPTH, 2, D), 0.02)
    s5_in_w = nrm(ks[7], (N_S5, D, D), D ** -0.5)
    n_idx = jnp.arange(S5_STATE, dtype=f32)
    s5_a_re = -0.5 * jnp.exp(nrm(ks[8], (N_S5, S5_GROUPS, S5_STATE), 0.05))
    s5_a_im = math.pi * n_idx + nrm(ks[9], (N_S5, S5_GROUPS, S5_STATE), 0.05)
    s5_log_dt = jax.random.uniform(ks[10], (N_S5, S5_GROUPS), f32, math.log(DT_MIN), math.log(DT_MAX))
    s5_b_re = nrm(ks[11], (N_S5, S5_GROUPS, S5_STATE, S5_GROUP), (2 * S5_GROUP) ** -0.5)
    s5_b_im = nrm(ks[12], (N_S5, S5_GROUPS, S5_STATE, S5_GROUP), (2 * S5_GROUP) ** -0.5)
    s5_c_re = nrm(ks[13], (N_S5, S5_GROUPS, S5_GROUP, S5_STATE), S5_STATE ** -0.5)
    s5_c_im = nrm(ks[14], (N_S5, S5_GROUPS, S5_GROUP, S5_STATE), S5_STATE ** -0.5)
    s5_d = nrm(ks[15], (N_S5, D), 1.0)
    s5_glu_w = nrm(ks[16], (N_S5, D, 2 * D), D ** -0.5)
    s5_glu_w = s5_glu_w.at[:, :, :D].multiply(BETA)
    s5_glu_b = nrm(ks[17], (N_S5, 2 * D), 0.01)
    dsa_in_w = nrm(ks[18], (N_DSA, D, DSA_IN), D ** -0.5)
    dsa_out_w = nrm(ks[19], (N_DSA, D, D), BETA * D ** -0.5)
    ffn_w_in = nrm(ks[20], (DEPTH, D, 2 * D_FF), D ** -0.5)
    ffn_w_out = nrm(ks[21], (DEPTH, D_FF, D), BETA * D_FF ** -0.5)
    return {"x": x, "c": c, "positions": positions, "ada_w": ada_w, "ada_b": ada_b,
            "ln_g": ln_g, "ln_b": ln_b, "s5_in_w": s5_in_w, "s5_a_re": s5_a_re, "s5_a_im": s5_a_im,
            "s5_log_dt": s5_log_dt, "s5_b_re": s5_b_re, "s5_b_im": s5_b_im, "s5_c_re": s5_c_re,
            "s5_c_im": s5_c_im, "s5_d": s5_d, "s5_glu_w": s5_glu_w, "s5_glu_b": s5_glu_b,
            "dsa_in_w": dsa_in_w, "dsa_out_w": dsa_out_w, "ffn_w_in": ffn_w_in, "ffn_w_out": ffn_w_out}

def reference(x, c, positions, ada_w, ada_b, ln_g, ln_b, s5_in_w, s5_a_re, s5_a_im, s5_log_dt,
              s5_b_re, s5_b_im, s5_c_re, s5_c_im, s5_d, s5_glu_w, s5_glu_b, dsa_in_w, dsa_out_w,
              ffn_w_in, ffn_w_out):
    cos_h, sin_h = rope_tables(positions, HEAD_DIM)
    cos_i, sin_i = rope_tables(positions, IDX_DIM)
    c_act = jax.nn.silu(c)
    for i in range(DEPTH):
        mod = c_act @ ada_w[i] + ada_b[i]
        sh1, sc1, g1, sh2, sc2, g2 = [m[:, None, :] for m in jnp.split(mod, 6, axis=-1)]
        h = x * (1.0 + sc1) + sh1
        j = i // N_MIXERS
        if i % N_MIXERS == 0:
            y = s5_mixer(h, s5_in_w[j], s5_a_re[j], s5_a_im[j], s5_log_dt[j], s5_b_re[j], s5_b_im[j],
                         s5_c_re[j], s5_c_im[j], s5_d[j], s5_glu_w[j], s5_glu_b[j])
        else:
            y = dsa_mixer(h, cos_h, sin_h, cos_i, sin_i, dsa_in_w[j], dsa_out_w[j])
        x = layer_norm(ALPHA * x + (1.0 + g1) * y, ln_g[i, 0], ln_b[i, 0])
        h = x * (1.0 + sc2) + sh2
        x = layer_norm(ALPHA * x + (1.0 + g2) * swiglu(h, ffn_w_in[i], ffn_w_out[i]), ln_g[i, 1], ln_b[i, 1])
    return x


_drawn_inputs = setup_inputs


def setup_inputs(seed=0):
    import zlib

    import numpy as np

    out = dict(_drawn_inputs(seed))
    spreads = {}
    factors = {'ada_b': 4.95,
     's5_a_re': 64.0,
     's5_a_im': 36.584,
     's5_log_dt': 37.856,
     's5_b_re': 48.496,
     's5_b_im': 51.208,
     's5_c_re': 49.584,
     's5_c_im': 49.576,
     's5_glu_b': 8.0}
    for name, (base, spread) in spreads.items():
        noise = np.random.default_rng([zlib.crc32(name.encode()), seed]).standard_normal(out[name].shape)
        drawn = base * np.exp(spread * noise) if base else spread * noise
        out[name] = __import__('jax').numpy.asarray(drawn.astype(out[name].dtype))
    for name, factor in factors.items():
        out[name] = (out[name] * factor).astype(out[name].dtype)
    return out
```

```python
from contextlib import ExitStack

import numpy as np

import concourse.bass as bass
from concourse import mybir

F32 = mybir.dt.float32
F32R = mybir.dt.float32r
I32 = mybir.dt.int32
ALU = mybir.AluOpType
ACT = mybir.ActivationFunctionType
AXX = mybir.AxisListType.X
ds = bass.ds

P = 128
SEQ = 256
TOK = SEQ // P
D = 2048
KT = D // P
DEPTH = 2
HEADS = 16
HD = D // HEADS
IDX_HEADS = 16
IDX_DIM = 64
TOPK = min(256, SEQ // 4)
D_FF = 5632
GROUPS = 128
GSIZE = 16
STATE = 64
ALPHA = (2.0 * DEPTH) ** 0.25
LN_EPS = 1e-5
ROPE_THETA = 10000.0

NB = 512
UK = 2
RING = 4
AW = 1024
CHUNKS = 6 * D // AW
AU = D // P
TC = 64
PAIRS = GROUPS // 2
TWO_PI = 6.283185307179586
C1 = 6.28125
C2 = float(np.float32(int((TWO_PI - C1) * 2 ** 21) / 2 ** 21))
C3 = float(np.float32(TWO_PI - C1 - C2))
ROUND = 12582912.0
MASKED = -3.0e38
TAKEN = -3.3e38
UNSEEN = 1.0e30


def shape_constants():
    out = np.zeros((P, 98), np.float32)
    for at, dim in ((0, HD), (HD // 2, IDX_DIM)):
        power = np.arange(0, dim, 2, dtype=np.float32) / np.float32(dim)
        out[:, at:at + dim // 2] = np.float32(1.0) / np.power(np.float32(ROPE_THETA), power).astype(np.float32)
    odd = (np.arange(P) // GSIZE) % 2
    out[:, 96] = 1 - odd
    out[:, 97] = odd
    return out


def build(nc, x, c, positions, ada_w, ada_b, ln_g, ln_b, s5_in_w, s5_a_re, s5_a_im, s5_log_dt, s5_b_re, s5_b_im,
          s5_c_re, s5_c_im, s5_d, s5_glu_w, s5_glu_b, dsa_in_w, dsa_out_w, ffn_w_in, ffn_w_out, consts, out):
    ctx = ExitStack()
    with ctx:
        K = 1024
        MAP = {}
        top = [0]

        def region(name, size):
            MAP[name] = top[0]
            top[0] += size

        for name, size in (("xz", 16 * K), ("hT_hi", 16 * K), ("hT_lo", 16 * K), ("aT_hi", 16 * K), ("aT_lo", 16 * K),
                           ("w_raw", 16 * K), ("w_hi", 16 * K), ("w_lo", 16 * K), ("growA", 8 * K), ("growB", 8 * K),
                           ("ada_raw", 16 * K), ("ada_acc", 4 * K), ("brow", 4 * K), ("lnrow", 8 * K), ("stgA", 4 * K),
                           ("stgB", 4 * K), ("uT", 16 * K), ("ident", 512), ("ones", 512), ("parT", 512),
                           ("sin", 768), ("cos", 768), ("modcol", 768), ("phase", 3 * K), ("small", 768)):
            region(name, size)
        base = (nc.sbuf_base + 31) // 32 * 32
        ctx.enter_context(nc.sbuf_tensor("slab", [P, top[0] // 4], F32))

        def at(name, where, shape, dtype=F32, plus=0):
            return nc.alloc_sbuf_tensor_at(name, shape, dtype, offset=base + MAP[where] + plus)

        xz = at("xz", "xz", [P, TOK, D])
        hT_hi = at("hT_hi", "hT_hi", [P, KT, SEQ], F32R)
        hT_lo = at("hT_lo", "hT_lo", [P, KT, SEQ], F32R)
        aT_hi = at("aT_hi", "aT_hi", [P, KT, SEQ], F32R)
        aT_lo = at("aT_lo", "aT_lo", [P, KT, SEQ], F32R)
        w_raw = at("w_raw", "w_raw", [P, RING, UK, NB])
        w_hi = at("w_hi", "w_hi", [P, RING, UK, NB], F32R)
        w_lo = at("w_lo", "w_lo", [P, RING, UK, NB], F32R)
        grow = at("grow", "growA", [P, 2 * D])
        ada_raw = at("ada_raw", "ada_raw", [P, RING, AW])
        ada_acc = at("ada_acc", "ada_acc", [P, AW])
        brow = at("brow", "brow", [1, AW])
        lnrow = at("lnrow", "lnrow", [P, 2, 2, NB])
        glub = at("glub", "lnrow", [1, 2, NB])
        stg = [at("stgA", "stgA", [P, TOK, NB]), at("stgB", "stgB", [P, TOK, NB])]
        ident = at("ident", "ident", [P, P])
        ones = at("ones", "ones", [P, P])
        parT = at("parT", "parT", [P, P])
        sin_t = at("sin_t", "sin", [P, 192])
        cos_t = at("cos_t", "cos", [P, 192])
        modcol = at("modcol", "modcol", [P, 2 * CHUNKS, 8])
        csil = at("csil", "small", [P, KT])
        dcol = at("dcol", "small", [P, KT], plus=64)
        scol = at("scol", "small", [P, KT], plus=128)
        bcol = at("bcol", "small", [P, KT], plus=192)
        stats = at("stats", "small", [P, TOK, 4, 6], plus=256)
        mv = at("mv", "small", [P, TOK, 2], plus=448)
        rstd = at("rstd", "small", [P, TOK, 2], plus=480)
        wic = at("wic", "small", [P, TOK, IDX_HEADS], plus=512)
        soft = at("soft", "small", [P, 4, 4], plus=640)

        uT = at("uT", "uT", [P, KT, SEQ])
        st = [at("st0", "w_hi", [P, TC, 2, PAIRS]), at("st1", "growB", [P, TC, 2, PAIRS])]
        uc = at("uc", "lnrow", [P, 2, KT, TC])
        y_in = at("y_in", "stgA", [P, KT, TC])
        y_act = at("y_act", "stgB", [P, KT, TC])
        Btab = [at("B_re_tab", "aT_hi", [P, KT, P]), at("B_im_tab", "aT_hi", [P, KT, P], plus=8 * K)]
        Ctab = [at("C_re_tab", "aT_lo", [P, KT, P]), at("C_im_tab", "aT_lo", [P, KT, P], plus=8 * K)]
        prod = at("prod", "phase", [P, 2, 2, PAIRS])
        tmp = at("tmp", "phase", [P, 2, PAIRS], plus=1024)
        carry = at("carry", "phase", [P, 2, PAIRS], plus=1536)
        lam4 = at("lam4", "phase", [P, 2, 2, PAIRS], plus=2048)
        Bnat = [at("Bnat_re", "w_hi", [P, STATE, GSIZE]), at("Bnat_im", "w_hi", [P, STATE, GSIZE], plus=4 * K)]
        Cnat = [at("Cnat_re", "w_hi", [P, KT, STATE], plus=8 * K), at("Cnat_im", "w_hi", [P, KT, STATE], plus=12 * K)]
        Bbar = [at("Bbar_re", "w_lo", [P, GSIZE, 2, STATE]), at("Bbar_im", "w_lo", [P, GSIZE, 2, STATE], plus=8 * K)]
        Btmp = [at("Btmp0", "aT_hi", [P, STATE, GSIZE]), at("Btmp1", "aT_hi", [P, STATE, GSIZE], plus=4 * K)]
        Bdiag = [at("Bdiag_re", "hT_hi", [P, PAIRS, 2, GSIZE]), at("Bdiag_im", "hT_hi", [P, PAIRS, 2, GSIZE], plus=8 * K)]
        Cmask = [at("Cmask_re", "hT_lo", [P, KT, 2, STATE]), at("Cmask_im", "hT_lo", [P, KT, 2, STATE], plus=8 * K)]
        scratch = [0]

        def pre(name, shape, dtype=F32):
            t = at(name, "uT", shape, dtype, plus=scratch[0])
            n = 4
            for s in shape[1:]:
                n *= s
            scratch[0] += (n + 31) // 32 * 32
            return t

        cst = pre("cst", [P, 98])
        parn = pre("parn", [P, P])
        cdn = pre("cdn", [2 * KT, P])
        pos_i = pre("pos_i", [P, TOK], I32)
        pos_f = pre("pos_f", [P, TOK])
        a_re = pre("a_re", [P, STATE])
        a_im = pre("a_im", [P, STATE])
        ldt = pre("ldt", [P, 1])
        dt = pre("dt", [P, 1])
        decay = pre("decay", [P, STATE])
        mag = pre("mag", [P, STATE])
        ang = pre("ang", [P, 256])
        turns = pre("turns", [P, 256])
        quarter = pre("quarter", [P, 256])
        sinv = pre("sinv", [P, 256])
        cosv = pre("cosv", [P, 256])
        lam = [pre("lam_re", [P, STATE]), pre("lam_im", [P, STATE])]
        lam_twice = [pre("lam_re_twice", [P, 2, STATE]), pre("lam_im_twice", [P, 2, STATE])]
        num = pre("num", [P, STATE])
        den = pre("den", [P, STATE])
        q0 = pre("q0", [P, STATE])
        q1 = pre("q1", [P, STATE])
        coef = [pre("coef_re", [P, STATE]), pre("coef_im", [P, STATE])]
        assert scratch[0] <= 16 * K

        qkT = at("qkT", "aT_hi", [P, 2 * HEADS, SEQ])
        v = at("v", "uT", [P, TOK, D])
        qiT = at("qiT", "lnrow", [P, IDX_HEADS // 2, SEQ])
        kiT = at("kiT", "phase", [P, SEQ], plus=2048)
        selb = at("selb", "phase", [P, TOK, SEQ])
        rt = at("rt", "phase", [P, NB])
        causal = at("causal", "hT_hi", [P, TOK, SEQ])
        score = at("score", "hT_hi", [P, 2, SEQ], plus=2 * K)
        relu = at("relu", "hT_hi", [P, 2, SEQ], plus=4 * K)
        off = at("off", "hT_hi", [P, TOK, SEQ], plus=6 * K)
        best = at("best", "hT_hi", [P, 8], plus=8 * K)
        logit = at("logit", "stgA", [P, 2, SEQ])
        prob = at("prob", "stgA", [P, 2, SEQ], plus=2 * K)
        probT = at("probT", "stgB", [P, 2, SEQ])

        PS = [ctx.enter_context(nc.psum_tensor("psA", [P, TOK, NB], F32)),
              ctx.enter_context(nc.psum_tensor("psB", [P, TOK, NB], F32))]
        T = ctx.enter_context(nc.psum_tensor("psT", [P, 2, NB], F32))
        M = ctx.enter_context(nc.psum_tensor("psM", [P, 2, NB], F32))

        def sem(name):
            return ctx.enter_context(nc.semaphore(name))

        w_landed = [sem(f"w_landed{n}") for n in range(RING)]
        w_hi_ready, w_lo_ready, w_used = sem("w_hi_ready"), sem("w_lo_ready"), sem("w_used")
        ada_landed = [sem(f"ada_landed{n}") for n in range(RING)]
        ada_used, brow_landed, chunk_summed, mod_ready = (sem("ada_used"), sem("brow_landed"), sem("chunk_summed"),
                                                          sem("mod_ready"))
        ps_free = [sem("psA_free"), sem("psB_free")]
        T_full, T_hi, T_free = sem("T_full"), sem("T_hi"), sem("T_free")
        rope_ready, rows_landed, row_used = sem("rope_ready"), [sem("rows_landed0"), sem("rows_landed1")], sem("row_used")
        glub_landed = sem("glub_landed")
        xn_ready, scale_ready, h_hi, h_ready = sem("xn_ready"), sem("scale_ready"), sem("h_hi"), sem("h_ready")
        var_ready, std_ready = sem("var_ready"), sem("std_ready")
        dve = sem("dve")
        const_ready, constants = sem("const_ready"), sem("constants")
        x_landed, in_landed, b_landed, cm_landed = sem("x_landed"), sem("in_landed"), sem("b_landed"), sem("cm_landed")
        pe_prep, act_prep, dve_prep = sem("pe_prep"), sem("act_prep"), sem("dve_prep")
        uT_ready, uc_ready, bu_full, bu_read = sem("uT_ready"), sem("uc_ready"), sem("bu_full"), sem("bu_read")
        rec, states_ready, y_full, y_ready, g_ready, g_hi, s5_done = (
            sem("rec"), sem("states_ready"), sem("y_full"), sem("y_ready"), sem("g_ready"), sem("g_hi"), sem("s5_done"))
        idx_full, idx_relu, idx_read, sel_ready = sem("idx_full"), sem("idx_relu"), sem("idx_read"), sem("sel_ready")
        lg_full, lg_ready, exp_done, p_ready, pT_full, pT_ready, o_full, o_hi, o_ready = (
            sem("lg_full"), sem("lg_ready"), sem("exp_done"), sem("p_ready"), sem("pT_full"), sem("pT_ready"),
            sem("o_full"), sem("o_hi"), sem("o_ready"))
        out_ready, out_landed = sem("out_ready"), sem("out_landed")

        class Run:
            def __init__(self, kind, n, w, col, row=0, units=KT // UK, layer=0, part=0, ada=(), before=None):
                self.kind, self.n, self.w, self.row, self.units = kind, n, w, row, units
                self.col = col
                self.step = 2 * NB if col[1] - col[0] == NB else NB
                self.layer, self.part, self.before = layer, part, before
                self.ada = list(ada)
                self.blocks = 1 if kind == "ki" else 2
                self.per = self.blocks * units
                self.width = IDX_HEADS + IDX_DIM if kind == "ki" else NB

        s5_in = Run("u", 2, s5_in_w[0], (0, NB), ada=[(0, 2, 4)], before="x")
        glu = Run("glu", 4, s5_glu_w[0], (D, 0), ada=[(0, 4, 6)], before="s5")
        runs = [s5_in, glu]
        parts = [4, 4, 3]
        for layer in range(DEPTH):
            if layer == 1:
                runs += [Run("rope", 4, dsa_in_w[0], (0, NB), layer=1, ada=[(0, 1, 21)], before="ln"),
                         Run("v", 2, dsa_in_w[0], (2 * D, 2 * D + NB), layer=1, ada=[(0, 2, 22)]),
                         Run("idx", 1, dsa_in_w[0], (3 * D, 3 * D + NB), layer=1),
                         Run("ki", 1, dsa_in_w[0], (3 * D + IDX_HEADS * IDX_DIM, 0), layer=1),
                         Run("z", 2, dsa_out_w[0], (0, NB), layer=1, part=2, before="attention")]
            done = 0
            for part, n in enumerate(parts):
                ada = [[(0, 2, 10), (2, 4, 12)], [(0, 2, 14), (2, 4, 16)], [(0, 3, 18)]][part] if layer == 0 else []
                runs += [Run("ff", n, ffn_w_in[layer], (done * NB, D_FF + done * NB), layer=layer, part=part, ada=ada,
                             before="ln" if part == 0 else None),
                         Run("z", 2, ffn_w_out[layer], (0, NB), row=done * NB, units=2 * n, layer=layer, part=part)]
                done += n
        attn_out = next(r for r in runs if r.before == "attention")
        unit = turn = hs = aT_parts = norms = 0
        roped = 1
        use = [0, 0]
        for r in runs:
            r.h0 = hs
            r.norm = norms
            if r.before in ("x", "ln"):
                r.hturn = turn
                turn += 4
                hs += 4
                norms += r.before == "ln"
            r.unit, r.turn, r.use, r.roped, r.aT0 = unit, turn, list(use), roped, aT_parts
            unit += r.per * r.n
            r.turns = {"u": 2, "rope": 2, "idx": 2, "ff": 1, "ki": 1}.get(r.kind, 0)
            turn += r.turns * r.n
            use[0] += r.n
            use[1] += r.n if r.blocks == 2 else 0
            roped += r.n * r.blocks if r.kind in ("rope", "idx", "ki") else 0
            aT_parts += r.n if r.kind == "ff" else 0
        runs[-1].final = True
        UNITS, TURNS, NORMS = unit, turn, norms
        AHEAD = RING - 1

        def iterations(eng, r):
            cuts = sorted({0, r.n} | {a for a, b, q in r.ada} | {b for a, b, q in r.ada})
            for lo, hi in zip(cuts[:-1], cuts[1:]):
                q = next((q + lo - a for a, b, q in r.ada if a <= lo < b), None)
                layer = None if q is None else q // CHUNKS
                if hi - lo == 1 or r is runs[0] or r is runs[-1]:
                    for i in range(lo, hi):
                        yield i, (None if q is None else q + i - lo), layer, q
                else:
                    with eng.Fori(lo, hi) as i:
                        yield i, (None if q is None else i + (q - lo)), layer, q

        def is_gate(q):
            return q % CHUNKS // 2 in (2, 5)

        def gate_column(q, q_first):
            kind = q_first % CHUNKS
            return (kind - 4 if kind < 6 else kind - 10 + 2) * AW + (q - q_first) * AW

        def ada_at(n, per):
            return [k for k in range(AU) if 2 + k * (per - 4) // AU == n]

        def product(r, i, s):
            return r.unit + i * r.per + (s + 1) * r.units

        def cols(i, s):
            return ds(i * (2 * NB) + s * NB, NB)

        block = ctx.enter_context(nc.Block())

        @block.sync
        def _(sp):
            sp.dma_start(cst[:], consts).then_inc(in_landed, 16)
            sp.dma_start(cdn[0:KT], c.rearrange("b (t p) -> (b t) p", p=P)).then_inc(in_landed, 16)
            sp.dma_start(cdn[KT:2 * KT], s5_d.rearrange("b (t p) -> (b t) p", p=P)).then_inc(in_landed, 16)
            sp.dma_start(parn[0:64], ln_g.rearrange("i j (t p) -> (i j t) p", p=P)).then_inc(in_landed, 16)
            sp.dma_start(parn[64:128], ln_b.rearrange("i j (t p) -> (i j t) p", p=P)).then_inc(in_landed, 16)
            sp.dma_start(a_re[:], s5_a_re[0]).then_inc(in_landed, 16)
            sp.dma_start(a_im[:], s5_a_im[0]).then_inc(in_landed, 16)
            sp.dma_start(ldt[:], s5_log_dt[0].rearrange("(g o) -> g o", o=1)).then_inc(in_landed, 16)
            sp.dma_start(pos_i[:], positions.rearrange("b (a p) -> p (b a)", p=P), allow_slow_non_contiguous=True).then_inc(in_landed, 16)

            def column(first, i, step):
                at_ = first + i * step
                return at_ if isinstance(at_, int) else sp.snap(at_)

            def ada_unit(first, k, layer, col):
                if not (isinstance(first, int) and first + k < RING):
                    sp.wait_ge(ada_used, first + (k - RING + 1))
                sp.dma_start(ada_raw[:, k % RING], ada_w[layer, k * P:(k + 1) * P, ds(col, AW)]
                             ).then_inc(ada_landed[k % RING], 16)

            for k in range(AU):
                ada_unit(0, k, 0, 0)
                if k == 3:
                    sp.dma_start(Bnat[0][:], s5_b_re[0]).then_inc(b_landed, 16)
                    sp.dma_start(Bnat[1][:], s5_b_im[0]).then_inc(b_landed, 16)
                if k == 5:
                    for ri, src in ((0, s5_c_re), (1, s5_c_im)):
                        sp.dma_start(Cnat[ri][:], src[0].rearrange("(t g) q n -> (g q) t n", g=8)).then_inc(cm_landed, 16)
            with sp.Fori(1, 4) as q:
                col, first = column(0, q, AW), column(0, q, AU)
                for k in range(AU):
                    ada_unit(first, k, 0, col)
            sp.dma_start(xz[:], x.rearrange("b (a p) d -> p (b a) d", p=P)).then_inc(x_landed, 16)
            for r in runs:
                for i, q, layer, _q in iterations(sp, r):
                    col = [column(r.col[s], i, r.step) for s in range(r.blocks)]
                    u = column(r.unit, i, r.per)
                    if q is not None:
                        ada_col, ada_first = column(-layer * CHUNKS * AW, q, AW), column(0, q, AU)
                    for n in range(r.per):
                        s, k = divmod(n, r.units)
                        early = r is glu and n == r.units - 1
                        if not (r is runs[0] and isinstance(i, int) and i == 0 and n < RING) and not (r is glu and n == r.units):
                            sp.wait_ge(w_lo_ready, u + (n - RING + 1 + early))
                        row = r.row + k * UK * P
                        sp.dma_start(w_raw[:, n % RING, :, 0:r.width],
                                     r.w[row:row + UK * P, ds(col[s], r.width)].rearrange("(k p) n -> p k n", p=P)
                                     ).then_inc(w_landed[n % RING], 16)
                        if q is not None:
                            if r is glu and n == 2:
                                sp.wait_ge(s5_done, SEQ // TC)
                            for k in ada_at(n, r.per):
                                ada_unit(ada_first, k, layer, ada_col)
            for chunk in range(4):
                sp.wait_ge(out_ready, chunk + 1)
                sp.dma_start(out.rearrange("b (a p) d -> p (b a) d", p=P)[:, :, chunk * NB:(chunk + 1) * NB],
                             xz[:, :, chunk * NB:(chunk + 1) * NB]).then_inc(out_landed, 16)
            sp.wait_ge(out_landed, 64)

        @block.gpsimd
        def _(pool):
            nc.gpsimd.memset(ident[:], 0.0).then_inc(const_ready, 1)
            nc.gpsimd.memset(ones[:], 1.0).then_inc(constants, 1)
            pool.wait_ge(const_ready, 1)
            nc.gpsimd.affine_select(out=ident[:], in_=ident[:], compare_op=ALU.not_equal, fill=1.0, base=0,
                                    pattern=[[-1, P]], channel_multiplier=1).then_inc(constants, 1)
            for ri in range(2):
                nc.gpsimd.memset(Bdiag[ri][:], 0.0).then_inc(constants, 1)
            nc.gpsimd.memset(carry[:], 0.0).then_inc(constants, 1)

            def load_brow(q, layer):
                if not (isinstance(q, int) and q == 0):
                    pool.wait_ge(chunk_summed, q)
                pool.dma_start(brow[:], ada_b[layer:layer + 1, ds((q - layer * CHUNKS) * AW, AW)]).then_inc(brow_landed, 16)

            def load_rows(norm, chunk):
                if norm == NORMS and chunk >= 2:
                    pool.wait_ge(out_ready, chunk - 1)
                elif 4 * norm + chunk >= 2:
                    pool.wait_ge(row_used, 4 * norm + chunk - 1)
                for which, src in ((0, ln_g), (1, ln_b)):
                    pool.dma_start(lnrow[:, chunk % 2, which],
                                   src[norm // 2, norm % 2:norm % 2 + 1, chunk * NB:(chunk + 1) * NB].to_broadcast([P, NB])
                                   ).then_inc(rows_landed[chunk % 2], 16)

            load_brow(0, 0)
            with pool.Fori(1, 4) as q:
                load_brow(q, 0)
            for r in runs:
                if r.before == "ln":
                    if r.norm == 0:
                        pool.wait_ge(w_used, glu.unit + glu.n * glu.per)
                    if r.norm == 2:
                        pool.wait_ge(idx_full, TOK * IDX_HEADS)
                    for chunk in range(4):
                        load_rows(r.norm, chunk)
                if r is glu:
                    pool.wait_ge(s5_done, SEQ // TC)
                if r is attn_out:
                    pool.wait_ge(w_used, r.unit)
                    nc.gpsimd.memset(causal[:], 1.0).then_inc(const_ready, 1)
                    pool.wait_ge(const_ready, 2)
                    nc.gpsimd.affine_select(out=causal[:], in_=causal[:], compare_op=ALU.is_ge, fill=0.0, base=0,
                                            pattern=[[P, TOK], [-1, SEQ]], channel_multiplier=1).then_inc(constants, 1)
                if not r.ada and r.kind != "glu":
                    continue
                for i, q, layer, _q in iterations(pool, r):
                    if r.kind == "glu":
                        pool.wait_ge(w_used, r.unit + i * r.per)
                        for which, c0 in ((0, D), (1, 0)):
                            pool.dma_start(glub[:, which], s5_glu_b[0:1, ds(i * NB + c0, NB)]).then_inc(glub_landed, 16)
                    if q is not None:
                        load_brow(q, layer)
            for chunk in range(4):
                load_rows(NORMS, chunk)

        @block.scalar
        def _(act):
            def hi_unit(u, n):
                act.wait_ge(w_landed[n % RING], u * (16 // RING) + (n // RING + 1) * 16)
                if not (isinstance(u, int) and u + n < RING):
                    act.wait_ge(w_used, u + (n - RING + 1))
                nc.scalar.activation(w_hi[:, n % RING], w_raw[:, n % RING], ACT.Copy).then_inc(w_hi_ready, 1)

            act.wait_ge(in_landed, 16 * 9)
            nc.scalar.activation(dt[:], ldt[:], ACT.Exp).then_inc(act_prep, 1)
            act.wait_ge(dve_prep, 1)
            nc.scalar.activation(mag[:], decay[:], ACT.Exp).then_inc(act_prep, 1)
            act.wait_ge(pe_prep, 1)
            nc.scalar.activation(csil[:], M[:, 0, 0:KT], ACT.Silu).then_inc(act_prep, 1)
            nc.scalar.activation(dcol[:], M[:, 0, KT:2 * KT], ACT.Copy)
            nc.scalar.activation(parT[:], M[:, 0, P:2 * P], ACT.Copy).then_inc(act_prep, 1)
            act.wait_ge(dve_prep, 2)
            nc.scalar.activation(sinv[:], turns[:], ACT.Sin)
            nc.scalar.activation(cosv[:], quarter[:], ACT.Sin).then_inc(act_prep, 1)
            for n in range(16):
                act.wait_ge(pe_prep, 12 + n)
                tab = (Btab if n < 8 else Ctab)[n % 8 // 4]
                j = n % 4
                nc.scalar.activation(tab[:, 4 * j:4 * j + 4, :], PS[n % 2][:, n // 2 % 2].rearrange("p (j m) -> p j m", m=P),
                                     ACT.Copy).then_inc(act_prep, 1)

            def make_h(r):
                act.wait_ge(scale_ready, r.h0 // 4 + 1)
                for g in range(4):
                    act.wait_ge(T_full, r.hturn + g + 1)
                    if g >= 2:
                        act.wait_ge(h_ready, r.h0 + g - 1)
                    h32 = stg[g % 2][:].rearrange("p a (b t) -> p (a b) t", t=SEQ)
                    for j in range(4):
                        k = 4 * g + j
                        ins = nc.scalar.activation(h32[:, j], T[:].rearrange("p a (b t) -> p (a b) t", t=SEQ)[:, j],
                                                   ACT.Identity, scale=scol[:, k:k + 1], bias=bcol[:, k:k + 1])
                    ins.then_inc(T_free, 1)
                    act.wait_ge(T_free, r.hturn + g + 1)
                    nc.scalar.activation(hT_hi[:, 4 * g:4 * g + 4], h32, ACT.Copy).then_inc(h_hi, 1)

            def std(norm):
                act.wait_ge(var_ready, norm + 1)
                nc.scalar.activation(rstd[:, :, 1], rstd[:, :, 0], ACT.Sqrt).then_inc(std_ready, 1)

            def read_T(r, i, k, dst, hi=False):
                act.wait_ge(T_full, r.turn + i * r.turns + (k + 1))
                n = dst.shape[1] if len(dst.shape) > 2 else 1
                src = T[:].rearrange("p a (b t) -> p (a b) t", t=SEQ)
                src = src[:, 0:n] if len(dst.shape) > 2 else src[:, 0]
                ins = nc.scalar.activation(dst, src, ACT.Copy)
                ins.then_inc(T_hi if hi else T_free, 1)

            def s5():
                for ch in range(SEQ // TC):
                    b = ch % 2
                    if ch == 0:
                        act.wait_ge(T_free, s5_in.turn + 4)
                        act.wait_ge(w_used, glu.unit)
                        act.wait_ge(mod_ready, 6)
                    if ch >= 2:
                        act.wait_ge(y_ready, ch - 1)
                    nc.scalar.activation(uc[:, b], uT[:, :, ch * TC:(ch + 1) * TC], ACT.Copy).then_inc(uc_ready, 1)
                    if ch >= 2:
                        act.wait_ge(y_full, ch - 1)
                    for j4 in range(4):
                        act.wait_ge(bu_full, 4 * ch + j4 + 1)
                        for g in range(4):
                            dst = st[b][:, :, :, 16 * j4 + g:16 * j4 + g + 13:4].rearrange("p t r f -> p f r t")
                            src = PS[g // 2][:, g % 2].rearrange("p (f r t) -> p f r t", f=4, r=2)
                            for f in range(4):
                                ins = nc.scalar.activation(dst[:, f], src[:, f], ACT.Copy)
                        ins.then_inc(bu_read, 1)
                    if ch >= 1:
                        gelu(ch - 1)
                gelu(SEQ // TC - 1)

            def gelu(ch):
                act.wait_ge(y_ready, ch + 1)
                if ch >= 1:
                    act.wait_ge(s5_done, ch)
                nc.scalar.activation(y_act[:], y_in[:], ACT.Gelu_apprx_tanh).then_inc(g_ready, 1)
                act.wait_ge(g_ready, ch + 1)
                nc.scalar.activation(hT_hi[:, :, ch * TC:(ch + 1) * TC], y_act[:], ACT.Copy).then_inc(g_hi, 1)

            def attention():
                n = 0
                for t in range(TOK):
                    for h in range(IDX_HEADS):
                        act.wait_ge(idx_full, n + 1)
                        if n >= 2:
                            act.wait_ge(idx_read, n - 1)
                        else:
                            act.wait_ge(w_used, attn_out.unit)
                        nc.scalar.activation(relu[:, n % 2, 0:(t + 1) * P], PS[h % 2][:, h // 2 % 2, 0:(t + 1) * P],
                                             ACT.Relu, scale=IDX_DIM ** -0.5).then_inc(idx_relu, 1)
                        n += 1
                for a in range(TOK * HEADS + 2):
                    if a < TOK * HEADS:
                        N = (a // HEADS + 1) * P
                        act.wait_ge(lg_ready, a + 1)
                        if a >= 2:
                            act.wait_ge(pT_full, a - 1)
                        nc.scalar.activation(prob[:, a % 2, 0:N], logit[:, a % 2, 0:N], ACT.Exp, bias=soft[:, a % 4, 1:2],
                                             accum_out=soft[:, a % 4, 2:3]).then_inc(exp_done, 1)
                    if 1 <= a <= TOK * HEADS:
                        b = a - 1
                        N = (b // HEADS + 1) * P
                        act.wait_ge(pT_full, b + 1)
                        nc.scalar.activation(probT[:, b % 2, 0:N], T[:, b % 2, 0:N], ACT.Copy).then_inc(pT_ready, 1)
                    if a >= 5 and a % 4 == 1:
                        g = a // 4 - 1
                        t, h = divmod(4 * g, HEADS)
                        act.wait_ge(o_full, g + 1)
                        nc.scalar.activation(hT_hi[:, h:h + 4, t * P:(t + 1) * P],
                                             M[:, g % 2].rearrange("p (h t) -> p h t", t=P), ACT.Copy).then_inc(o_hi, 1)

            for r in runs:
                if r.before == "ln":
                    std(r.norm)
                if r.before in ("x", "ln"):
                    make_h(r)
                elif r.before == "s5":
                    s5()
                    act.wait_ge(y_full, SEQ // TC)
                    act.wait_ge(g_hi, SEQ // TC)
                elif r.before == "attention":
                    attention()
                if r is runs[0]:
                    act.wait_ge(dve_prep, 4)
                if r is runs[0] or r is glu:
                    for n in range(AHEAD):
                        hi_unit(r.unit, n)
                for i, q, layer, _q in iterations(act, r):
                    u = r.unit + i * r.per
                    stop = isinstance(i, int) and i == r.n - 1 and (r is runs[0] or r is runs[-1])

                    def finish(s, i=i, r=r):
                        if r.kind in ("u", "v") or (r.kind in ("glu", "ff") and s == 0):
                            act.wait_ge(w_used, product(r, i, s))
                        if r.kind == "u":
                            nc.scalar.activation(stg[s][:], PS[s][:], ACT.Copy).then_inc(ps_free[s], 1)
                        if r.kind in ("glu", "ff") and s == 0:
                            act.wait_ge(ps_free[1], r.use[1] + i)
                            nc.scalar.activation(stg[0][:], PS[0][:], ACT.Sigmoid if r.kind == "glu" else ACT.Silu
                                                 ).then_inc(ps_free[0], 1)
                        if r.kind == "v":
                            nc.scalar.activation(v[:, :, cols(i, s)], PS[s][:], ACT.Copy).then_inc(ps_free[s], 1)

                    def turned(s, i=i, r=r):
                        if r.kind == "u":
                            read_T(r, i, s, uT[:, ds(i * 8 + s * 4, 4)])
                        if r.kind == "rope":
                            read_T(r, i, s, qkT[:, ds(i * 8 + s * 4, 4)])
                        if r.kind == "idx":
                            if s == 0:
                                act.wait_ge(row_used, 4 * (NORMS - 1))
                            read_T(r, i, s, qiT[:, 4 * s:4 * s + 4])
                        if r.kind == "ff" and s == 1:
                            read_T(r, i, 0, aT_hi[:, ds(i * 4, 4)], hi=True)
                        if r.kind == "ki" and s == 0:
                            read_T(r, i, 0, kiT[:])

                    for n in range(r.per):
                        if not (stop and n + AHEAD >= r.per):
                            hi_unit(u, n + AHEAD)
                        if r.blocks == 2 and n == r.units:
                            finish(0)
                        if r.blocks == 2 and n == r.units + 3:
                            turned(0)
                    finish(r.blocks - 1)
                    turned(r.blocks - 1)
            std(NORMS)

        @block.vector
        def _(vec):
            V = nc.vector
            chain = [0]

            def link(ins):
                chain[0] += 1
                ins.then_inc(dve, 1)
                vec.wait_ge(dve, chain[0])

            def lo_unit(u, n):
                vec.wait_ge(w_hi_ready, u + (n + 1))
                V.tensor_tensor(w_lo[:, n % RING], w_raw[:, n % RING], w_hi[:, n % RING].bitcast(F32), ALU.subtract
                                ).then_inc(w_lo_ready, 1)

            def ada_unit(q, k):
                vec.wait_ge(ada_landed[k % RING], q * 64 + 16 * (k // RING + 1))
                if k == 0:
                    if not (isinstance(q, int) and q == 0):
                        vec.wait_ge(chunk_summed, q)
                    V.tensor_scalar(ada_acc[:], ada_raw[:, 0], csil[:, 0:1], None, ALU.mult).then_inc(ada_used, 1)
                else:
                    vec.wait_ge(ada_used, q * AU + k)
                    V.scalar_tensor_tensor(out=ada_acc[:], in0=ada_raw[:, k % RING], scalar=csil[:, k:k + 1],
                                           in1=ada_acc[:], op0=ALU.mult, op1=ALU.add).then_inc(ada_used, 1)

            def store_chunk(q, q_first):
                vec.wait_ge(chunk_summed, q + 1)
                if is_gate(q_first):
                    V.tensor_scalar(grow[:, ds(gate_column(q, q_first), AW)], M[:].rearrange("p a n -> p (a n)"), 1.0, None,
                                    ALU.add).then_inc(mod_ready, 1)
                else:
                    V.tensor_copy(modcol[:, ds(q, 1), :].rearrange("p a b -> p (a b)"), M[:, 0, 0:8]).then_inc(mod_ready, 1)

            vec.sem_inc(rope_ready, 1)
            vec.wait_ge(in_landed, 16 * 9)
            vec.wait_ge(act_prep, 1)
            V.tensor_copy(pos_f[:], pos_i[:])
            link(V.tensor_scalar(ang[:, 192:256], a_im[:], dt[:], None, ALU.mult))
            V.tensor_scalar(decay[:], a_re[:], dt[:], None, ALU.mult).then_inc(dve_prep, 1)
            for t in range(TOK):
                V.tensor_scalar(ang[:, t * 64:t * 64 + 64], cst[:, 0:64], pos_f[:, t:t + 1], None, ALU.mult)
                ins = V.tensor_scalar(ang[:, 128 + t * 32:160 + t * 32], cst[:, 64:96], pos_f[:, t:t + 1], None, ALU.mult)
            link(ins)
            link(V.tensor_scalar(turns[:], ang[:], 1.0 / TWO_PI, None, ALU.mult))
            link(V.tensor_scalar(turns[:], turns[:], ROUND, None, ALU.add))
            link(V.tensor_scalar(turns[:], turns[:], -ROUND, None, ALU.add))
            for part in (C1, C2, C3):
                link(V.scalar_tensor_tensor(out=ang[:], in0=turns[:], scalar=-part, in1=ang[:], op0=ALU.mult, op1=ALU.add))
            LIM = 3.1415925
            link(V.tensor_scalar(turns[:], ang[:], LIM, -LIM, ALU.min, ALU.max))
            link(V.tensor_scalar(ang[:], turns[:], TWO_PI / 4, None, ALU.add))
            link(V.tensor_scalar(quarter[:], ang[:], LIM, -TWO_PI, ALU.is_gt, ALU.mult))
            link(V.tensor_tensor(quarter[:], quarter[:], ang[:], ALU.add))
            V.tensor_scalar(quarter[:], quarter[:], LIM, -LIM, ALU.min, ALU.max).then_inc(dve_prep, 1)
            vec.wait_ge(act_prep, 3)
            for k in range(4):
                ada_unit(0, k)
            vec.wait_ge(act_prep, 5)
            V.tensor_copy(sin_t[:], sinv[:, 0:192])
            V.tensor_copy(cos_t[:], cosv[:, 0:192])
            V.tensor_tensor(lam[0][:], mag[:], cosv[:, 192:256], ALU.mult)
            link(V.tensor_tensor(lam[1][:], mag[:], sinv[:, 192:256], ALU.mult))
            V.tensor_scalar(num[:], lam[0][:], -1.0, None, ALU.add)
            V.tensor_tensor(q0[:], a_re[:], a_re[:], ALU.mult)
            link(V.tensor_tensor(q1[:], a_im[:], a_im[:], ALU.mult))
            link(V.tensor_tensor(den[:], q0[:], q1[:], ALU.add))
            link(V.reciprocal(den[:], den[:]))
            V.tensor_tensor(q0[:], num[:], a_re[:], ALU.mult)
            link(V.tensor_tensor(q1[:], lam[1][:], a_im[:], ALU.mult))
            link(V.tensor_tensor(q0[:], q0[:], q1[:], ALU.add))
            link(V.tensor_tensor(coef[0][:], q0[:], den[:], ALU.mult))
            V.tensor_tensor(q0[:], lam[1][:], a_re[:], ALU.mult)
            link(V.tensor_tensor(q1[:], num[:], a_im[:], ALU.mult))
            link(V.tensor_tensor(q0[:], q0[:], q1[:], ALU.subtract))
            link(V.tensor_tensor(coef[1][:], q0[:], den[:], ALU.mult))
            vec.wait_ge(b_landed, 32)
            wide = [coef[ri][:].unsqueeze(2).to_broadcast([P, STATE, GSIZE]) for ri in range(2)]
            V.tensor_tensor(Btmp[0][:], Bnat[0][:], wide[0], ALU.mult)
            link(V.tensor_tensor(Btmp[1][:], Bnat[1][:], wide[1], ALU.mult))
            for par in range(2):
                ins = V.tensor_tensor(Bbar[0][:, :, par].rearrange("p k n -> p n k"), Btmp[0][:], Btmp[1][:], ALU.subtract)
            link(ins)
            V.tensor_tensor(Btmp[0][:], Bnat[1][:], wide[0], ALU.mult)
            link(V.tensor_tensor(Btmp[1][:], Bnat[0][:], wide[1], ALU.mult))
            for ri in range(2):
                for par in range(2):
                    V.tensor_copy(lam_twice[ri][:, par], lam[ri][:])
            for par in range(2):
                ins = V.tensor_tensor(Bbar[1][:, :, par].rearrange("p k n -> p n k"), Btmp[0][:], Btmp[1][:], ALU.add)
            ins.then_inc(dve_prep, 1)
            vec.wait_ge(cm_landed, 32)
            for ri in range(2):
                for par in range(2):
                    ins = V.tensor_scalar(Cmask[ri][:, :, par, :], Cnat[ri][:], cst[:, 96 + par:97 + par],
                                          1.0 if ri == 0 else -1.0, ALU.mult, ALU.mult)
            ins.then_inc(dve_prep, 1)
            for k in range(4, 8):
                ada_unit(0, k)
            vec.wait_ge(constants, 5)
            vec.wait_ge(pe_prep, 3)
            for par in range(2):
                rows = slice(64 * par, 64 * par + 64)
                for row, col, ri, sign in ((0, 0, 0, 1.0), (0, 1, 1, -1.0), (1, 0, 1, 1.0), (1, 1, 0, 1.0)):
                    ins = V.tensor_scalar(lam4[rows, row, col, :], M[rows, 0, ri * P + par:ri * P + P:2], sign, None, ALU.mult)
            ins.then_inc(dve_prep, 1)
            for n in range(8):
                vec.wait_ge(pe_prep, 3 + n + 1)
                ri, p4 = divmod(n, 4)
                bank = PS[n % 2][:, n // 2 % 2].rearrange("p (k g o) -> p k g o", k=4, o=2)
                for par in range(2):
                    rows = slice(64 * par, 64 * par + 64)
                    ins = V.tensor_copy(Bdiag[ri][rows, :, par, 4 * p4:4 * p4 + 4].rearrange("p g k -> p k g"),
                                        bank[rows, :, :, par])
                ins.then_inc(dve_prep, 1)
            for k in range(8, AU):
                ada_unit(0, k)
            store_chunk(0, 0)
            with vec.Fori(1, 4) as q:
                for k in range(AU):
                    ada_unit(q, k)
                store_chunk(q, 0)

            def make_scale(r):
                q = r.layer * CHUNKS + (0 if r.kind in ("u", "rope") else 6)
                shift = modcol[:, q:q + 2].rearrange("p a b -> p (a b)")
                scale = modcol[:, q + 2:q + 4].rearrange("p a b -> p (a b)")
                vec.wait_ge(mod_ready, q + 4)
                if r.before == "x":
                    V.tensor_scalar(scol[:], scale, 1.0, None, ALU.add)
                    V.tensor_copy(bcol[:], shift).then_inc(scale_ready, 1)
                else:
                    gain, bias = parT[:, r.norm * KT:r.norm * KT + KT], parT[:, 64 + r.norm * KT:64 + r.norm * KT + KT]
                    V.scalar_tensor_tensor(out=scol[:], in0=scale, scalar=1.0, in1=gain, op0=ALU.add, op1=ALU.mult)
                    link(V.scalar_tensor_tensor(out=bcol[:], in0=scale, scalar=1.0, in1=bias, op0=ALU.add, op1=ALU.mult))
                    V.tensor_tensor(bcol[:], bcol[:], shift, ALU.add).then_inc(scale_ready, 1)

            def moments(norm):
                for t in range(TOK):
                    ins = V.bn_aggr(mv[:, t], stats[:, t])
                link(ins)
                V.tensor_scalar(rstd[:, :, 0], mv[:, :, 1], LN_EPS, None, ALU.add).then_inc(var_ready, 1)
                vec.wait_ge(std_ready, norm + 1)
                link(V.reciprocal(rstd[:, :, 1], rstd[:, :, 1]))

            def normalise(g):
                for t in range(TOK):
                    ins = V.tensor_scalar(xz[:, t, g * NB:(g + 1) * NB], xz[:, t, g * NB:(g + 1) * NB], mv[:, t, 0:1],
                                          rstd[:, t, 1:2], ALU.subtract, ALU.mult)
                return ins

            def make_h(r):
                if r.before == "ln":
                    moments(r.norm)
                make_scale(r)
                for g in range(5):
                    if g < 4 and r.before == "ln":
                        normalise(g).then_inc(xn_ready, 1)
                    if g >= 1:
                        vec.wait_ge(h_hi, r.h0 + g)
                        V.tensor_tensor(hT_lo[:, 4 * g - 4:4 * g].rearrange("p a t -> p (a t)"),
                                        stg[(g - 1) % 2][:].rearrange("p a t -> p (a t)"),
                                        hT_hi[:, 4 * g - 4:4 * g].rearrange("p a t -> p (a t)").bitcast(F32), ALU.subtract
                                        ).then_inc(h_ready, 1)

            def affine(norm, chunk, scale, last=None):
                vec.wait_ge(rows_landed[chunk % 2], 32 * (2 * norm + chunk // 2 + 1))
                part = xz[:, :, chunk * NB:(chunk + 1) * NB]
                gain, bias = (lnrow[:, chunk % 2, w].unsqueeze(1).to_broadcast([P, TOK, NB]) for w in range(2))
                link(V.scalar_tensor_tensor(out=part, in0=part, scalar=scale, in1=gain, op0=ALU.mult, op1=ALU.mult))
                V.scalar_tensor_tensor(out=part, in0=bias, scalar=scale, in1=part, op0=ALU.mult, op1=ALU.add
                                       ).then_inc(row_used if last is None else last, 1)

            def s5():
                n = 0

                def post(ch):
                    vec.wait_ge(y_full, ch + 1)
                    if ch >= 1:
                        vec.wait_ge(g_ready, ch)
                    link(V.tensor_tensor(y_in[:], uc[:, ch % 2], dcol[:].unsqueeze(2).to_broadcast([P, KT, TC]), ALU.mult))
                    V.tensor_tensor(y_in[:].rearrange("p k t -> p (k t)"), y_in[:].rearrange("p k t -> p (k t)"),
                                    T[:].rearrange("p a n -> p (a n)"), ALU.add).then_inc(y_ready, 1)

                def gelu_lo(ch):
                    vec.wait_ge(g_hi, ch + 1)
                    V.tensor_tensor(hT_lo[:, :, ch * TC:(ch + 1) * TC], y_act[:],
                                    hT_hi[:, :, ch * TC:(ch + 1) * TC].bitcast(F32), ALU.subtract).then_inc(s5_done, 1)

                for ch in range(SEQ // TC):
                    b = ch % 2
                    vec.wait_ge(bu_read, 4 * ch + 4)
                    for t in range(TC):
                        for half in range(2):
                            g = slice(32 * half, 32 * half + 32)
                            if n:
                                vec.wait_ge(rec, n - 1 + half)
                            s = carry[:, :, g] if t == 0 else st[b][:, t - 1, :, g]
                            V.tensor_tensor(prod[:, :, :, g], s.unsqueeze(1).to_broadcast([P, 2, 2, 32]), lam4[:, :, :, g],
                                            ALU.mult).then_inc(rec, 1)
                        for half in range(2):
                            g = slice(32 * half, 32 * half + 32)
                            vec.wait_ge(rec, n + 1 + half)
                            V.tensor_tensor(tmp[:, :, g], prod[:, :, 0, g], prod[:, :, 1, g], ALU.add).then_inc(rec, 1)
                        for half in range(2):
                            g = slice(32 * half, 32 * half + 32)
                            vec.wait_ge(rec, n + 3 + half)
                            V.tensor_tensor(st[b][:, t, :, g], tmp[:, :, g], st[b][:, t, :, g], ALU.add).then_inc(rec, 1)
                        n += 6
                        if ch >= 1 and t == 24:
                            post(ch - 1)
                        if ch >= 1 and t == 36:
                            gelu_lo(ch - 1)
                    vec.wait_ge(rec, n)
                    V.tensor_copy(carry[:], st[b][:, TC - 1]).then_inc(states_ready, 1)
                    vec.wait_ge(states_ready, ch + 1)
                post(SEQ // TC - 1)
                gelu_lo(SEQ // TC - 1)

            def rope(r, i, s, heads, half, table):
                vec.wait_ge(w_used, product(r, i, s))
                vec.wait_ge(T_full, r.turn + i * r.turns + (s - 1 if s else -1) if r.kind != "ki" else r.turn)
                vec.wait_ge(rope_ready, r.roped + i * r.blocks + s)
                c0 = IDX_HEADS if r.kind == "ki" else 0
                wide = heads * 2 * half
                for t in range(TOK):
                    at0 = t * half + (0 if table == "h" else 2 * (HD // 2))
                    shape = [P, heads, 2, half]
                    cosb, sinb = (w[:, at0:at0 + half].unsqueeze(1).unsqueeze(1).to_broadcast(shape) for w in (cos_t, sin_t))
                    src = PS[s][:, t, c0:c0 + wide].rearrange("p (h x d) -> p h x d", x=2, d=half)
                    dst = stg[s][:, t, 0:wide].rearrange("p (h x d) -> p h x d", x=2, d=half)
                    other = rt[:, 0:wide].rearrange("p (h x d) -> p h x d", x=2, d=half)
                    V.tensor_tensor(dst, src, cosb, ALU.mult)
                    link(V.tensor_tensor(other, src, sinb, ALU.mult))
                    if t == TOK - 1 and r.kind != "ki":
                        vec.sem_inc(ps_free[s], 1)
                    V.tensor_tensor(dst[:, :, 0], dst[:, :, 0], other[:, :, 1], ALU.subtract)
                    ins = V.tensor_tensor(dst[:, :, 1], dst[:, :, 1], other[:, :, 0], ALU.add)
                    if t < TOK - 1:
                        link(ins)
                return ins

            def links(r):
                return {"u": 0, "v": 0, "ff": 0, "z": 4 if r.part == 2 else 2, "glu": 3, "rope": 6, "idx": 6, "ki": 4}[r.kind]

            def attention():
                vec.wait_ge(constants, 6)
                vec.wait_ge(T_full, attn_out.turn)
                link(V.tensor_scalar(off[:], causal[:], -MASKED, MASKED, ALU.mult, ALU.add))
                n = 0
                for t in range(TOK):
                    N = (t + 1) * P
                    for h in range(IDX_HEADS):
                        vec.wait_ge(idx_relu, n + 1)
                        if h == 0:
                            V.tensor_scalar(score[:, 0, 0:N], relu[:, n % 2, 0:N], wic[:, t, 0:1], None, ALU.mult
                                            ).then_inc(idx_read, 1)
                        else:
                            vec.wait_ge(idx_read, n)
                            V.scalar_tensor_tensor(out=score[:, 0, 0:N], in0=relu[:, n % 2, 0:N], scalar=wic[:, t, h:h + 1],
                                                   in1=score[:, 0, 0:N], op0=ALU.mult, op1=ALU.add).then_inc(idx_read, 1)
                        n += 1
                    vec.wait_ge(idx_read, n)
                    link(V.tensor_tensor(score[:, 1, 0:N], score[:, 0, 0:N], causal[:, t, 0:N], ALU.mult))
                    link(V.tensor_tensor(score[:, 0, 0:N], score[:, 1, 0:N], off[:, t, 0:N], ALU.add))
                    for k in range(TOPK // 8):
                        a, b = k % 2, 1 - k % 2
                        link(V.max(best[:], score[:, a, 0:N]))
                        link(V.match_replace(score[:, b, 0:N], best[:], score[:, a, 0:N], TAKEN))
                    a = TOPK // 8 % 2
                    link(V.tensor_scalar(score[:, 1 - a, 0:N], score[:, a, 0:N], (MASKED + TAKEN) / 2, None, ALU.is_le))
                    link(V.tensor_tensor(score[:, a, 0:N], score[:, 1 - a, 0:N], causal[:, t, 0:N], ALU.mult))
                    link(V.tensor_scalar(selb[:, t, 0:N], score[:, a, 0:N], -1.0, UNSEEN, ALU.add, ALU.mult))
                A = TOK * HEADS

                def o_lo(g):
                    t, h = divmod(4 * g, HEADS)
                    vec.wait_ge(o_hi, g + 1)
                    V.tensor_tensor(hT_lo[:, h:h + 4, t * P:(t + 1) * P], M[:, g % 2].rearrange("p (h t) -> p h t", t=P),
                                    hT_hi[:, h:h + 4, t * P:(t + 1) * P].bitcast(F32), ALU.subtract).then_inc(o_ready, 1)

                for a in range(A + 1):
                    if a < A:
                        t = a // HEADS
                        N = (t + 1) * P
                        vec.wait_ge(lg_full, a + 1)
                        if a >= 2:
                            vec.wait_ge(exp_done, a - 1)
                        link(V.scalar_tensor_tensor(out=logit[:, a % 2, 0:N], in0=PS[a % 2][:, 0, 0:N], scalar=HD ** -0.5,
                                                    in1=selb[:, t, 0:N], op0=ALU.mult, op1=ALU.add))
                        link(V.reduce_max(soft[:, a % 4, 0:1], logit[:, a % 2, 0:N], AXX))
                        V.tensor_scalar(soft[:, a % 4, 1:2], soft[:, a % 4, 0:1], -1.0, None, ALU.mult).then_inc(lg_ready, 1)
                    if a >= 1:
                        b = a - 1
                        N = (b // HEADS + 1) * P
                        vec.wait_ge(exp_done, b + 1)
                        link(V.reciprocal(soft[:, b % 4, 3:4], soft[:, b % 4, 2:3]))
                        V.tensor_scalar(prob[:, b % 2, 0:N], prob[:, b % 2, 0:N], soft[:, b % 4, 3:4], None, ALU.mult
                                        ).then_inc(p_ready, 1)
                    if a % 4 == 3 and a >= 7:
                        o_lo(a // 4 - 1)
                o_lo(A // 4 - 1)

            for r in runs:
                if r.before in ("x", "ln"):
                    make_h(r)
                    if r.before == "ln":
                        for chunk in range(4):
                            affine(r.norm, chunk, ALPHA)
                    else:
                        vec.wait_ge(T_full, r.hturn + 4)
                        link(V.tensor_scalar(xz[:].rearrange("p a d -> p (a d)"), xz[:].rearrange("p a d -> p (a d)"), ALPHA,
                                             None, ALU.mult))
                elif r.before == "s5":
                    s5()
                elif r.before == "attention":
                    attention()
                if r is runs[0] or r is glu:
                    for n in range(AHEAD):
                        lo_unit(r.unit, n)
                base = chain[0]
                for i, q, layer, q_first in iterations(vec, r):
                    u = r.unit + i * r.per
                    stop = isinstance(i, int) and i == r.n - 1 and (r is runs[0] or r is runs[-1])
                    chain[0] = base + i * links(r)

                    def finish(s, i=i, r=r):
                        full = r.use[s] + i + 1
                        if r.kind == "z":
                            vec.wait_ge(w_used, product(r, i, s))
                            c = cols(i, s)
                            gate = 0 if r is attn_out else D
                            g = grow[:, ds(gate + i * (2 * NB) + s * NB, NB)].unsqueeze(1).to_broadcast([P, TOK, NB])
                            V.tensor_tensor(stg[s][:], PS[s][:], g, ALU.mult).then_inc(ps_free[s], 1)
                            vec.wait_ge(ps_free[s], full)
                            link(V.tensor_tensor(xz[:, :, c], xz[:, :, c], stg[s][:], ALU.add))
                            if r.part == 2:
                                for t in range(TOK):
                                    ins = V.bn_stats(stats[:, t, ds(i * 2 + s, 1)].rearrange("p a b -> p (a b)"), xz[:, t, c])
                                link(ins)
                        if r.kind == "glu" and s == 1:
                            vec.wait_ge(ps_free[0], r.use[0] + i + 1)
                            vec.wait_ge(w_used, product(r, i, 1))
                            V.tensor_tensor(stg[1][:], stg[0][:], PS[1][:], ALU.mult).then_inc(ps_free[1], 1)
                            vec.wait_ge(ps_free[1], full)
                            c = ds(i * NB, NB)
                            g = grow[:, c].unsqueeze(1).to_broadcast([P, TOK, NB])
                            link(V.tensor_tensor(stg[1][:], stg[1][:], g, ALU.mult))
                            link(V.tensor_tensor(xz[:, :, c], xz[:, :, c], stg[1][:], ALU.add))
                            for t in range(TOK):
                                ins = V.bn_stats(stats[:, t, ds(i, 1)].rearrange("p a b -> p (a b)"), xz[:, t, c])
                            link(ins)
                        if r.kind == "ff" and s == 1:
                            vec.wait_ge(ps_free[0], r.use[0] + i + 1)
                            vec.wait_ge(w_used, product(r, i, 1))
                            V.tensor_tensor(stg[1][:], stg[0][:], PS[1][:], ALU.mult).then_inc(ps_free[1], 1)
                        if r.kind in ("rope", "idx"):
                            heads, half, table = (4, 64, "h") if r.kind == "rope" else (8, 32, "i")
                            rope(r, i, s, heads, half, table).then_inc(rope_ready, 1)
                        if r.kind == "ki":
                            link(rope(r, i, 0, 1, 32, "i"))
                            V.tensor_copy(stg[0][:, :, 64:128], stg[0][:, :, 0:64]).then_inc(rope_ready, 1)
                            V.tensor_scalar(wic[:], PS[0][:, :, 0:IDX_HEADS], IDX_HEADS ** -0.5, None, ALU.mult
                                            ).then_inc(ps_free[0], 1)

                    def turned(s, i=i, r=r):
                        if r.kind == "ff" and s == 1:
                            vec.wait_ge(T_hi, r.aT0 + i + 1)
                            V.tensor_tensor(aT_lo[:, ds(i * 4, 4)].rearrange("p a t -> p (a t)"), T[:].rearrange("p a t -> p (a t)"),
                                            aT_hi[:, ds(i * 4, 4)].rearrange("p a t -> p (a t)").bitcast(F32), ALU.subtract
                                            ).then_inc(T_free, 1)

                    for n in range(r.per):
                        if not (stop and n + AHEAD >= r.per):
                            lo_unit(u, n + AHEAD)
                        if q is not None:
                            for kk in ada_at(n, r.per):
                                ada_unit(q, kk)
                        if r.blocks == 2 and n == r.units:
                            finish(0)
                    finish(r.blocks - 1)
                    if q is not None:
                        store_chunk(q, q_first)
                    turned(r.blocks - 1)
                chain[0] = base + links(r) * r.n
            moments(NORMS)
            for chunk in range(4):
                link(normalise(chunk))
            for chunk in range(4):
                affine(NORMS, chunk, 1.0, last=out_ready)

        @block.tensor
        def _(pe):
            MM = nc.tensor.matmul

            def turn_T(full, wait, src):
                for sem_, value in wait:
                    pe.wait_ge(sem_, value)
                if not (isinstance(full, int) and full == 1):
                    pe.wait_ge(T_free, full - 1)
                for t in range(TOK):
                    for j in range(4):
                        ins = nc.tensor.transpose(T[:, j // 2, (j % 2) * SEQ + t * P:(j % 2) * SEQ + (t + 1) * P],
                                                  src(t, j), ident[:])
                ins.then_inc(T_full, 1)

            def sum_chunk(q, q_first):
                pe.wait_ge(ada_used, (q + 1) * AU)
                pe.wait_ge(brow_landed, (q + 1) * 16)
                if not (isinstance(q, int) and q == 0):
                    pe.wait_ge(mod_ready, q)
                if is_gate(q_first):
                    for h in range(2):
                        MM(M[:, h], ones[:], ada_acc[:, h * NB:(h + 1) * NB], start=True, stop=False)
                        ins = MM(M[:, h], ones[0:1, :], brow[:, h * NB:(h + 1) * NB], start=False, stop=True)
                else:
                    for j in range(AW // P):
                        MM(M[:, 0, j:j + 1], ada_acc[:, j * P:(j + 1) * P], ones[:, 0:1], start=True, stop=False)
                        ins = MM(M[:, 0, j:j + 1], brow[:, j * P:(j + 1) * P], ones[0:1, 0:1], start=False, stop=True)
                ins.then_inc(chunk_summed, 1)

            pe.wait_ge(constants, 2)
            pe.wait_ge(in_landed, 16 * 9)
            nc.tensor.transpose(M[:, 0, 0:2 * KT], cdn[:], ident[0:2 * KT, 0:2 * KT])
            nc.tensor.transpose(M[:, 0, P:2 * P], parn[:], ident[:]).then_inc(pe_prep, 1)
            pe.wait_ge(act_prep, 4)
            pe.wait_ge(dve_prep, 3)

            nc.tensor.transpose(M[:, 0, 0:P], lam_twice[0][:].rearrange("p a n -> p (a n)"), ident[:]).then_inc(pe_prep, 1)
            nc.tensor.transpose(M[:, 0, P:2 * P], lam_twice[1][:].rearrange("p a n -> p (a n)"), ident[:]).then_inc(pe_prep, 1)
            for n in range(8):
                if n >= 4:
                    pe.wait_ge(dve_prep, 6 + n - 4)
                ri, p4 = divmod(n, 4)
                for k in range(4):
                    ins = nc.tensor.transpose(PS[n % 2][:, n // 2 % 2, k * P:(k + 1) * P],
                                              Bbar[ri][:, 4 * p4 + k].rearrange("p a n -> p (a n)"), ident[:])
                ins.then_inc(pe_prep, 1)
            for n in range(16):
                if n < 4:
                    pe.wait_ge(dve_prep, 13)
                else:
                    pe.wait_ge(act_prep, 6 + n - 4)
                ri, j4 = divmod(n % 8, 4)
                for k in range(4):
                    j = 4 * j4 + k
                    src = Bdiag[ri][:, 4 * j:4 * j + 4].rearrange("p g a k -> p (g a k)") if n < 8 else \
                        Cmask[ri][:, j].rearrange("p a n -> p (a n)")
                    ins = nc.tensor.transpose(PS[n % 2][:, n // 2 % 2, k * P:(k + 1) * P], src, ident[:])
                ins.then_inc(pe_prep, 1)
            pe.wait_ge(dve_prep, 5)
            sum_chunk(0, 0)
            with pe.Fori(1, 4) as q:
                sum_chunk(q, 0)

            def s5():
                for ch in range(SEQ // TC + 1):
                    if ch < SEQ // TC:
                        b = ch % 2
                        pe.wait_ge(uc_ready, ch + 1)
                        for j4 in range(4):
                            if ch or j4:
                                pe.wait_ge(bu_read, 4 * ch + j4)
                            else:
                                for s in range(2):
                                    pe.wait_ge(ps_free[s], s5_in.n)
                            for f in range(4):
                                for g in range(4):
                                    rows = slice(32 * g, 32 * g + 32)
                                    for ri in range(2):
                                        at_ = (2 * f + ri) * TC
                                        ins = MM(PS[g // 2][:, g % 2, at_:at_ + TC], Btab[ri][rows, 4 * j4 + f, :],
                                                 uc[rows, b, 4 * j4 + f, :], start=True, stop=True)
                            ins.then_inc(bu_full, 1)
                    if ch >= 1:
                        b = (ch - 1) % 2
                        pe.wait_ge(states_ready, ch)
                        if ch >= 2:
                            pe.wait_ge(y_ready, ch - 1)
                        for f in range(KT):
                            for g in range(4):
                                rows = slice(32 * g, 32 * g + 32)
                                for ri in range(2):
                                    ins = MM(T[rows, f // 8, f % 8 * TC:f % 8 * TC + TC], Ctab[ri][:, f, rows],
                                             st[b][:, :, ri, 4 * f + g], start=ri == 0, stop=ri == 1)
                        ins.then_inc(y_full, 1)

            def attention():
                n = 0
                pe.wait_ge(T_free, attn_out.turn)
                pe.wait_ge(ps_free[0], attn_out.use[0])
                pe.wait_ge(ps_free[1], attn_out.use[1])
                for t in range(TOK):
                    N = (t + 1) * P
                    for h in range(IDX_HEADS):
                        if n >= 4:
                            pe.wait_ge(idx_relu, n - 3)
                        rows = slice(64 * (h % 2), 64 * (h % 2) + 64)
                        MM(PS[h % 2][:, h // 2 % 2, 0:N], qiT[rows, h // 2, t * P:(t + 1) * P], kiT[rows, 0:N],
                           start=True, stop=True).then_inc(idx_full, 1)
                        n += 1
                A = TOK * HEADS
                pe.wait_ge(idx_relu, n)
                pe.wait_ge(mod_ready, 2 * CHUNKS)
                for a in range(A + 2):
                    if a < A:
                        t, h = divmod(a, HEADS)
                        N = (t + 1) * P
                        if a >= 2:
                            pe.wait_ge(lg_ready, a - 1)
                        MM(PS[a % 2][:, 0, 0:N], qkT[:, h, t * P:(t + 1) * P], qkT[:, HEADS + h, 0:N],
                           start=True, stop=True).then_inc(lg_full, 1)
                    if 1 <= a <= A:
                        b = a - 1
                        pe.wait_ge(p_ready, b + 1)
                        if b >= 2:
                            pe.wait_ge(pT_ready, b - 1)
                        for k in range(b // HEADS + 1):
                            ins = nc.tensor.transpose(T[:, b % 2, k * P:(k + 1) * P], prob[:, b % 2, k * P:(k + 1) * P], ident[:])
                        ins.then_inc(pT_full, 1)
                    if a >= 2:
                        b = a - 2
                        t, h = divmod(b, HEADS)
                        pe.wait_ge(pT_ready, b + 1)
                        if b % 4 == 0 and b >= 8:
                            pe.wait_ge(o_ready, b // 4 - 1)
                        for k in range(t + 1):
                            ins = MM(M[:, b // 4 % 2, b % 4 * P:(b % 4 + 1) * P], v[:, k, h * P:(h + 1) * P],
                                     probT[:, b % 2, k * P:(k + 1) * P], start=k == 0, stop=k == t)
                        if b % 4 == 3:
                            ins.then_inc(o_full, 1)

            pe.wait_ge(act_prep, 21)
            for r in runs:
                if r.before in ("x", "ln"):
                    for g in range(4):
                        wait = [(x_landed, 16)] if r.before == "x" else [(xn_ready, 4 * r.norm + g + 1)]
                        turn_T(r.hturn + g + 1, wait, lambda t, j, g=g: xz[:, t, g * NB + j * P:g * NB + (j + 1) * P])
                elif r.before == "s5":
                    s5()
                elif r.before == "attention":
                    attention()
                for i, q, layer, q_first in iterations(pe, r):
                    u = r.unit + i * r.per
                    for s in range(r.blocks):
                        if not (isinstance(i, int) and r.use[s] + i == 0):
                            pe.wait_ge(ps_free[s], r.use[s] + i)
                        for k in range(r.units):
                            n = s * r.units + k
                            pe.wait_ge(w_lo_ready, u + (n + 1))
                            if r.kind == "z" and r.before is None:
                                pe.wait_ge(T_free, ff_turn + k // 2 + 1)
                                hi, lo = aT_hi, aT_lo
                            else:
                                if r.kind == "glu":
                                    pe.wait_ge(s5_done, SEQ // TC)
                                elif r.before == "attention":
                                    pe.wait_ge(o_ready, TOK * HEADS // 4)
                                elif r.before in ("x", "ln"):
                                    pe.wait_ge(h_ready, r.h0 + k // 2 + 1)
                                hi, lo = hT_hi, hT_lo
                            last = k == r.units - 1
                            if k == 0 and r.kind == "glu":
                                pe.wait_ge(glub_landed, i * 32 + 32)
                                for t in range(TOK):
                                    MM(PS[s][:, t], ones[0:1, :], glub[:, s], start=True, stop=False)
                            for t in range(TOK):
                                for kk in range(UK):
                                    kt = k * UK + kk
                                    tok = slice(t * P, (t + 1) * P)
                                    for m, (a_, b_) in enumerate(((hi, w_hi), (hi, w_lo), (lo, w_hi))):
                                        ins = MM(PS[s][:, t, 0:r.width], a_[:, kt, tok], b_[:, n % RING, kk, 0:r.width],
                                                 start=kt == 0 and m == 0 and r.kind != "glu", stop=last and kk == UK - 1 and m == 2)
                            ins.then_inc(w_used, 1)
                            if q is not None and n == r.per - 2:
                                sum_chunk(q, q_first)
                            if s == 1 and k == 2 and r.kind in ("u", "rope", "idx"):
                                ready = (ps_free[0], r.use[0] + i + 1) if r.kind == "u" else (rope_ready, r.roped + i * 2 + 1)
                                turn_T(r.turn + i * r.turns + 1, [ready], lambda t, j: stg[0][:, t, j * P:(j + 1) * P])
                    if r.kind in ("u", "rope", "idx"):
                        ready = (ps_free[1], r.use[1] + i + 1) if r.kind == "u" else (rope_ready, r.roped + i * 2 + 2)
                        turn_T(r.turn + i * r.turns + 2, [ready], lambda t, j: stg[1][:, t, j * P:(j + 1) * P])
                    if r.kind == "ff":
                        turn_T(r.turn + i + 1, [(ps_free[1], r.use[1] + i + 1)], lambda t, j: stg[1][:, t, j * P:(j + 1) * P])
                    if r.kind == "ki":
                        pe.wait_ge(rope_ready, r.roped + 1)
                        pe.wait_ge(T_free, r.turn)
                        for t in range(TOK):
                            ins = nc.tensor.transpose(T[:, 0, t * P:(t + 1) * P], stg[0][:, t, 0:P], ident[:])
                        ins.then_inc(T_full, 1)
                if r.kind == "ff":
                    ff_turn = r.turn


_INS = ["x", "c", "positions", "ada_w", "ada_b", "ln_g", "ln_b", "s5_in_w", "s5_a_re", "s5_a_im", "s5_log_dt", "s5_b_re",
        "s5_b_im", "s5_c_re", "s5_c_im", "s5_d", "s5_glu_w", "s5_glu_b", "dsa_in_w", "dsa_out_w", "ffn_w_in", "ffn_w_out"]


def kernel(**inputs):
    import concourse.bacc as bacc
    from concourse.bass_utils import run_bass_kernel_spmd

    nc = bacc.Bacc("TRN2", target_bir_lowering=False, num_devices=1)
    arrays, args = {}, []
    for name in _INS:
        a = np.ascontiguousarray(inputs[name])
        arrays[f"in_{name}"] = a
        args.append(nc.dram_tensor(f"in_{name}", a.shape, mybir.dt.from_np(a.dtype), kind="ExternalInput").ap())
    arrays["in_consts"] = shape_constants()
    args.append(nc.dram_tensor("in_consts", (P, 98), F32, kind="ExternalInput").ap())
    args.append(nc.dram_tensor("out", (1, SEQ, D), F32, kind="ExternalOutput").ap())
    build(nc, *args)
    r = run_bass_kernel_spmd(nc, [arrays], core_ids=[0])
    return r.results[0]["out"]
```

```python
from contextlib import ExitStack

import numpy as np

import concourse.bass as bass
from concourse import mybir

F32 = mybir.dt.float32
F32R = mybir.dt.float32r
I32 = mybir.dt.int32
ALU = mybir.AluOpType
ACT = mybir.ActivationFunctionType
AXX = mybir.AxisListType.X
ds = bass.ds

P = 128
SEQ = 256
TOK = SEQ // P
D = 2048
KT = D // P
DEPTH = 2
HEADS = 16
HD = D // HEADS
IDX_HEADS = 16
IDX_DIM = 64
TOPK = min(256, SEQ // 4)
D_FF = 5632
GROUPS = 128
GSIZE = 16
STATE = 64
ALPHA = (2.0 * DEPTH) ** 0.25
LN_EPS = 1e-5
ROPE_THETA = 10000.0

NB = 512
UK = 2
RING = 4
CW = 1024
STAGE = 2 * D // CW
COLS = 2 * STAGE
AW = 512
AU = D // P
ARING = 8
G = D // AW
STREAM = [(0, 0, 2 * D, 0, None), (G, 0, 5 * D, 1, None), (2 * G, 1, 2 * D, 0, None),
          (3 * G, 1, 0, None, 4 * KT), (5 * G, 1, 3 * D, None, 6 * KT), (7 * G, 1, 5 * D, 1, None)]
STREAMED = 8 * G
TC = 64
PAIRS = GROUPS // 2
TWO_PI = 6.283185307179586
C1 = 6.28125
C2 = float(np.float32(int((TWO_PI - C1) * 2 ** 21) / 2 ** 21))
C3 = float(np.float32(TWO_PI - C1 - C2))
ROUND = 12582912.0
MASKED = -3.0e38
TAKEN = -3.3e38
UNSEEN = 1.0e30


def shape_constants():
    out = np.zeros((P, 98), np.float32)
    for at, dim in ((0, HD), (HD // 2, IDX_DIM)):
        power = np.arange(0, dim, 2, dtype=np.float32) / np.float32(dim)
        out[:, at:at + dim // 2] = np.float32(1.0) / np.power(np.float32(ROPE_THETA), power).astype(np.float32)
    odd = (np.arange(P) // GSIZE) % 2
    out[:, 96] = 1 - odd
    out[:, 97] = odd
    return out


def build(nc, x, c, positions, ada_w, ada_b, ln_g, ln_b, s5_in_w, s5_a_re, s5_a_im, s5_log_dt, s5_b_re, s5_b_im,
          s5_c_re, s5_c_im, s5_d, s5_glu_w, s5_glu_b, dsa_in_w, dsa_out_w, ffn_w_in, ffn_w_out, consts, out):
    ctx = ExitStack()
    with ctx:
        K = 1024
        MAP = {}
        top = [0]

        def region(name, size):
            MAP[name] = top[0]
            top[0] += size

        for name, size in (("xz", 16 * K), ("hT_hi", 16 * K), ("hT_lo", 16 * K), ("aT_hi", 16 * K), ("aT_lo", 16 * K),
                           ("w_raw", 16 * K), ("w_hi", 16 * K), ("w_lo", 16 * K), ("growA", 8 * K), ("growB", 8 * K),
                           ("ada_raw", 16 * K), ("ada_acc", 4 * K), ("brow", 4 * K), ("lnrow", 8 * K), ("stgA", 4 * K),
                           ("stgB", 4 * K), ("uT", 16 * K), ("ident", 512), ("ones", 512), ("parT", 512),
                           ("sin", 768), ("cos", 768), ("modcol", 768), ("phase", 3 * K), ("small", 768)):
            region(name, size)
        base = (nc.sbuf_base + 31) // 32 * 32
        ctx.enter_context(nc.sbuf_tensor("slab", [P, top[0] // 4], F32))

        def at(name, where, shape, dtype=F32, plus=0):
            return nc.alloc_sbuf_tensor_at(name, shape, dtype, offset=base + MAP[where] + plus)

        xz = at("xz", "xz", [P, TOK, D])
        hT_hi = at("hT_hi", "hT_hi", [P, KT, SEQ], F32R)
        hT_lo = at("hT_lo", "hT_lo", [P, KT, SEQ], F32R)
        aT_hi = at("aT_hi", "aT_hi", [P, KT, SEQ], F32R)
        aT_lo = at("aT_lo", "aT_lo", [P, KT, SEQ], F32R)
        w_raw = at("w_raw", "w_raw", [P, RING, UK, NB])
        w_hi = at("w_hi", "w_hi", [P, RING, UK, NB], F32R)
        w_lo = at("w_lo", "w_lo", [P, RING, UK, NB], F32R)
        grow = at("grow", "growA", [P, 2 * D])
        ada_raw = at("ada_raw", "ada_raw", [P, ARING, AW])
        ada_acc = at("ada_acc", "ada_acc", [P, AW])
        brow = at("brow", "brow", [1, AW])
        col_raw = [at("col_raw0", "ada_raw", [P, RING, CW]), at("col_raw1", "w_raw", [P, RING, CW])]
        lnrow = at("lnrow", "lnrow", [P, 2, 2, NB])
        glub = at("glub", "lnrow", [1, 2, NB])
        stg = [at("stgA", "stgA", [P, TOK, NB]), at("stgB", "stgB", [P, TOK, NB])]
        ident = at("ident", "ident", [P, P])
        ones = at("ones", "ones", [P, P])
        parT = at("parT", "parT", [P, P])
        sin_t = at("sin_t", "sin", [P, 192])
        cos_t = at("cos_t", "cos", [P, 192])
        modcol = at("modcol", "modcol", [P, 4 * DEPTH * KT])
        csil = at("csil", "small", [P, KT])
        dcol = at("dcol", "small", [P, KT], plus=64)
        scol = at("scol", "small", [P, KT], plus=128)
        bcol = at("bcol", "small", [P, KT], plus=192)
        stats = at("stats", "small", [P, TOK, 4, 6], plus=256)
        mv = at("mv", "small", [P, TOK, 2], plus=448)
        rstd = at("rstd", "small", [P, TOK, 2], plus=480)
        wic = at("wic", "small", [P, TOK, IDX_HEADS], plus=512)
        soft = at("soft", "small", [P, 4, 4], plus=640)

        uT = at("uT", "uT", [P, KT, SEQ])
        st = [at("st0", "w_hi", [P, TC, 2, PAIRS]), at("st1", "growB", [P, TC, 2, PAIRS])]
        uc = at("uc", "lnrow", [P, 2, KT, TC])
        y_in = at("y_in", "stgA", [P, KT, TC])
        y_act = at("y_act", "stgB", [P, KT, TC])
        Btab = [at("B_re_tab", "aT_hi", [P, KT, P]), at("B_im_tab", "aT_hi", [P, KT, P], plus=8 * K)]
        Ctab = [at("C_re_tab", "aT_lo", [P, KT, P]), at("C_im_tab", "aT_lo", [P, KT, P], plus=8 * K)]
        prod = at("prod", "phase", [P, 2, 2, PAIRS])
        tmp = at("tmp", "phase", [P, 2, PAIRS], plus=1024)
        carry = at("carry", "phase", [P, 2, PAIRS], plus=1536)
        lam4 = at("lam4", "phase", [P, 2, 2, PAIRS], plus=2048)
        Bnat = [at("Bnat_re", "w_hi", [P, STATE, GSIZE]), at("Bnat_im", "w_hi", [P, STATE, GSIZE], plus=4 * K)]
        Cnat = [at("Cnat_re", "w_hi", [P, KT, STATE], plus=8 * K), at("Cnat_im", "w_hi", [P, KT, STATE], plus=12 * K)]
        Bbar = [at("Bbar_re", "w_lo", [P, GSIZE, 2, STATE]), at("Bbar_im", "w_lo", [P, GSIZE, 2, STATE], plus=8 * K)]
        Btmp = [at("Btmp0", "aT_hi", [P, STATE, GSIZE]), at("Btmp1", "aT_hi", [P, STATE, GSIZE], plus=4 * K)]
        Bdiag = [at("Bdiag_re", "hT_hi", [P, PAIRS, 2, GSIZE]), at("Bdiag_im", "hT_hi", [P, PAIRS, 2, GSIZE], plus=8 * K)]
        Cmask = [at("Cmask_re", "hT_lo", [P, KT, 2, STATE]), at("Cmask_im", "hT_lo", [P, KT, 2, STATE], plus=8 * K)]
        scratch = [0]

        def pre(name, shape, dtype=F32):
            t = at(name, "uT", shape, dtype, plus=scratch[0])
            n = 4
            for s in shape[1:]:
                n *= s
            scratch[0] += (n + 31) // 32 * 32
            return t

        cst = pre("cst", [P, 98])
        parn = pre("parn", [P, P])
        cdn = pre("cdn", [2 * KT, P])
        biasn = pre("biasn", [P, P])
        pos_i = pre("pos_i", [P, TOK], I32)
        pos_f = pre("pos_f", [P, TOK])
        a_re = pre("a_re", [P, STATE])
        a_im = pre("a_im", [P, STATE])
        ldt = pre("ldt", [P, 1])
        dt = pre("dt", [P, 1])
        decay = pre("decay", [P, STATE])
        mag = pre("mag", [P, STATE])
        ang = pre("ang", [P, 256])
        turns = pre("turns", [P, 256])
        quarter = pre("quarter", [P, 256])
        sinv = pre("sinv", [P, 256])
        cosv = pre("cosv", [P, 256])
        lam = [pre("lam_re", [P, STATE]), pre("lam_im", [P, STATE])]
        lam_twice = [pre("lam_re_twice", [P, 2, STATE]), pre("lam_im_twice", [P, 2, STATE])]
        num = pre("num", [P, STATE])
        den = pre("den", [P, STATE])
        q0 = pre("q0", [P, STATE])
        q1 = pre("q1", [P, STATE])
        coef = [pre("coef_re", [P, STATE]), pre("coef_im", [P, STATE])]
        assert scratch[0] <= 16 * K

        qkT = at("qkT", "aT_hi", [P, 2 * HEADS, SEQ])
        v = at("v", "uT", [P, TOK, D])
        qiT = at("qiT", "lnrow", [P, IDX_HEADS // 2, SEQ])
        kiT = at("kiT", "phase", [P, SEQ], plus=2048)
        selb = at("selb", "phase", [P, TOK, SEQ])
        rt = at("rt", "phase", [P, NB])
        causal = at("causal", "hT_hi", [P, TOK, SEQ])
        score = at("score", "hT_hi", [P, 2, SEQ], plus=2 * K)
        relu = at("relu", "hT_hi", [P, 2, SEQ], plus=4 * K)
        off = at("off", "hT_hi", [P, TOK, SEQ], plus=6 * K)
        best = at("best", "hT_hi", [P, 8], plus=8 * K)
        logit = at("logit", "stgA", [P, 2, SEQ])
        prob = at("prob", "stgA", [P, 2, SEQ], plus=2 * K)
        probT = at("probT", "stgB", [P, 2, SEQ])

        PS = [ctx.enter_context(nc.psum_tensor("psA", [P, TOK, NB], F32)),
              ctx.enter_context(nc.psum_tensor("psB", [P, TOK, NB], F32))]
        T = ctx.enter_context(nc.psum_tensor("psT", [P, 2, NB], F32))
        M = ctx.enter_context(nc.psum_tensor("psM", [P, 2, NB], F32))

        def sem(name):
            return ctx.enter_context(nc.semaphore(name))

        w_landed = [sem(f"w_landed{n}") for n in range(RING)]
        w_hi_ready, w_lo_ready, w_used = sem("w_hi_ready"), sem("w_lo_ready"), sem("w_used")
        ada_landed = [sem(f"ada_landed{n}") for n in range(ARING)]
        ada_used, brow_landed, chunk_summed, chunk_stored = (sem("ada_used"), sem("brow_landed"), sem("chunk_summed"),
                                                          sem("chunk_stored"))
        col_landed = [sem(f"col_landed{n}") for n in range(RING)]
        col_used, bias_landed, bias_ready = sem("col_used"), sem("bias_landed"), sem("bias_ready")
        ps_free = [sem("psA_free"), sem("psB_free")]
        T_full, T_hi, T_free = sem("T_full"), sem("T_hi"), sem("T_free")
        rope_ready, rows_landed, row_used = sem("rope_ready"), [sem("rows_landed0"), sem("rows_landed1")], sem("row_used")
        glub_landed = sem("glub_landed")
        xn_ready, scale_ready, h_hi, h_ready = sem("xn_ready"), sem("scale_ready"), sem("h_hi"), sem("h_ready")
        var_ready, std_ready = sem("var_ready"), sem("std_ready")
        dve = sem("dve")
        const_ready, constants = sem("const_ready"), sem("constants")
        x_landed, in_landed, b_landed, cm_landed = sem("x_landed"), sem("in_landed"), sem("b_landed"), sem("cm_landed")
        pe_prep, act_prep, dve_prep = sem("pe_prep"), sem("act_prep"), sem("dve_prep")
        uT_ready, uc_ready, bu_full, bu_read = sem("uT_ready"), sem("uc_ready"), sem("bu_full"), sem("bu_read")
        rec, states_ready, y_full, y_ready, g_ready, g_hi, s5_done = (
            sem("rec"), sem("states_ready"), sem("y_full"), sem("y_ready"), sem("g_ready"), sem("g_hi"), sem("s5_done"))
        idx_full, idx_relu, idx_read, sel_ready = sem("idx_full"), sem("idx_relu"), sem("idx_read"), sem("sel_ready")
        lg_full, lg_ready, exp_done, p_ready, pT_full, pT_ready, o_full, o_hi, o_ready = (
            sem("lg_full"), sem("lg_ready"), sem("exp_done"), sem("p_ready"), sem("pT_full"), sem("pT_ready"),
            sem("o_full"), sem("o_hi"), sem("o_ready"))
        out_ready, out_landed = sem("out_ready"), sem("out_landed")

        class Run:
            def __init__(self, kind, n, w, col, row=0, units=KT // UK, layer=0, part=0, ada=(), before=None):
                self.kind, self.n, self.w, self.row, self.units = kind, n, w, row, units
                self.col = col
                self.step = 2 * NB if col[1] - col[0] == NB else NB
                self.layer, self.part, self.before = layer, part, before
                self.ada = list(ada)
                self.blocks = 1 if kind == "ki" else 2
                self.per = self.blocks * units
                self.width = IDX_HEADS + IDX_DIM if kind == "ki" else NB

        s5_in = Run("u", 2, s5_in_w[0], (0, NB), ada=[(0, 2, 0)], before="x")
        glu = Run("glu", 4, s5_glu_w[0], (D, 0), ada=[(0, 2, 2), (2, 4, 4)], before="s5")
        runs = [s5_in, glu]
        parts = [4, 4, 3]
        for layer in range(DEPTH):
            if layer == 1:
                runs += [Run("rope", 4, dsa_in_w[0], (0, NB), layer=1, ada=[(0, 4, 21)], before="ln"),
                         Run("v", 2, dsa_in_w[0], (2 * D, 2 * D + NB), layer=1, ada=[(0, 2, 25)]),
                         Run("idx", 1, dsa_in_w[0], (3 * D, 3 * D + NB), layer=1, ada=[(0, 1, 27)]),
                         Run("ki", 1, dsa_in_w[0], (3 * D + IDX_HEADS * IDX_DIM, 0), layer=1),
                         Run("z", 2, dsa_out_w[0], (0, NB), layer=1, part=2, before="attention")]
            done = 0
            for part, n in enumerate(parts):
                ada = [[[(0, 2, 6), (2, 4, 8)], [(0, 4, 12)], [(0, 2, 18), (2, 3, 20)]], [[(0, 4, 28)], [], []]][layer][part]
                z_ada = [[[(0, 2, 10)], [(0, 2, 16)], []], [[], [], []]][layer][part]
                runs += [Run("ff", n, ffn_w_in[layer], (done * NB, D_FF + done * NB), layer=layer, part=part, ada=ada,
                             before="ln" if part == 0 else None),
                         Run("z", 2, ffn_w_out[layer], (0, NB), row=done * NB, units=2 * n, layer=layer, part=part,
                             ada=z_ada)]
                done += n
        attn_out_chunks = 7 * G
        assert SEQ // TC == STAGE
        attn_out = next(r for r in runs if r.before == "attention")
        unit = turn = hs = aT_parts = norms = 0
        roped = 1
        use = [0, 0]
        for r in runs:
            r.h0 = hs
            r.norm = norms
            if r.before in ("x", "ln"):
                r.hturn = turn
                turn += 4
                hs += 4
                norms += r.before == "ln"
            r.unit, r.turn, r.use, r.roped, r.aT0 = unit, turn, list(use), roped, aT_parts
            unit += r.per * r.n
            r.turns = {"u": 2, "rope": 2, "idx": 2, "ff": 1, "ki": 1}.get(r.kind, 0)
            turn += r.turns * r.n
            use[0] += r.n
            use[1] += r.n if r.blocks == 2 else 0
            roped += r.n * r.blocks if r.kind in ("rope", "idx", "ki") else 0
            aT_parts += r.n if r.kind == "ff" else 0
        runs[-1].final = True
        UNITS, TURNS, NORMS = unit, turn, norms
        AHEAD = RING - 1

        def iterations(eng, r):
            cuts = sorted({0, 1, r.n} | {a for a, b, q in r.ada} | {b for a, b, q in r.ada})
            for lo, hi in zip(cuts[:-1], cuts[1:]):
                q = next((q + lo - a for a, b, q in r.ada if a <= lo < b), None)
                if hi - lo == 1 or r is runs[0] or r is runs[-1]:
                    for i in range(lo, hi):
                        yield i, (None if q is None else q + i - lo), q
                else:
                    with eng.Fori(lo, hi) as i:
                        yield i, (None if q is None else i + (q - lo)), q

        def streamed(q_first):
            return next(e for e in reversed(STREAM) if e[0] <= q_first)

        def ada_at(n, per):
            return [k for k in range(AU) if 1 + k * (per - 5) // AU == n]

        def column_source(m):
            return m // (2 * STAGE), m // STAGE % 2 * 3 * D - m // STAGE * STAGE * CW

        def closing(r, i):
            if not (isinstance(i, int) and i == 0):
                return r, i - 1
            before = runs.index(r) - 1
            return None if r.before or before < 0 else (runs[before], runs[before].n - 1)

        def closes(r):
            return r is runs[-1] or bool(runs[runs.index(r) + 1].before)

        def product(r, i, s):
            return r.unit + i * r.per + (s + 1) * r.units

        def cols(i, s):
            return ds(i * (2 * NB) + s * NB, NB)

        block = ctx.enter_context(nc.Block())

        @block.sync
        def _(sp):
            sp.dma_start(cst[:], consts).then_inc(in_landed, 16)
            sp.dma_start(cdn[0:KT], c.rearrange("b (t p) -> (b t) p", p=P)).then_inc(in_landed, 16)
            sp.dma_start(cdn[KT:2 * KT], s5_d.rearrange("b (t p) -> (b t) p", p=P)).then_inc(in_landed, 16)
            sp.dma_start(parn[0:64], ln_g.rearrange("i j (t p) -> (i j t) p", p=P)).then_inc(in_landed, 16)
            sp.dma_start(parn[64:128], ln_b.rearrange("i j (t p) -> (i j t) p", p=P)).then_inc(in_landed, 16)
            sp.dma_start(a_re[:], s5_a_re[0]).then_inc(in_landed, 16)
            sp.dma_start(a_im[:], s5_a_im[0]).then_inc(in_landed, 16)
            sp.dma_start(ldt[:], s5_log_dt[0].rearrange("(g o) -> g o", o=1)).then_inc(in_landed, 16)
            for row, c0 in ((0, 0), (32, 3 * D)):
                for layer in range(DEPTH):
                    sp.dma_start(biasn[64 * layer + row:64 * layer + row + 32],
                                 ada_b[layer, c0:c0 + 2 * D].rearrange("(a p) -> a p", p=P)).then_inc(bias_landed, 16)
            sp.dma_start(pos_i[:], positions.rearrange("b (a p) -> p (b a)", p=P), allow_slow_non_contiguous=True).then_inc(in_landed, 16)

            def column(first, i, step):
                at_ = first + i * step
                return at_ if isinstance(at_, int) else sp.snap(at_)

            def ada_unit(first, k, layer, col):
                if not (isinstance(first, int) and first + k < ARING):
                    sp.wait_ge(ada_used, first + (k - ARING + 1))
                sp.dma_start(ada_raw[:, k % ARING], ada_w[layer, k * P:(k + 1) * P, ds(col, AW)]
                             ).then_inc(ada_landed[k % ARING], 16)

            def col_unit(ring, m, k, layer, col):
                if not (isinstance(m, int) and m == 0 and k < RING):
                    sp.wait_ge(col_used, m * AU + (k - RING + 1))
                sp.dma_start(col_raw[ring][:, k % RING], ada_w[layer, k * P:(k + 1) * P, ds(col, CW)]
                             ).then_inc(col_landed[k % RING], 16)

            def col_chunks(ring, first, n):
                layer, c0 = column_source(first)
                with sp.Fori(first, first + n) as m:
                    col, used = column(c0, m, CW), column(0, m, 1)
                    for k in range(AU):
                        col_unit(ring, used, k, layer, col)

            def w_unit(r, n, s, k, col):
                row = r.row + k * UK * P
                sp.dma_start(w_raw[:, n % RING, :, 0:r.width],
                             r.w[row:row + UK * P, ds(col, r.width)].rearrange("(k p) n -> p k n", p=P)
                             ).then_inc(w_landed[n % RING], 16)

            for k in range(AU):
                col_unit(0, 0, k, 0, 0)
                if k == 3:
                    sp.dma_start(Bnat[0][:], s5_b_re[0]).then_inc(b_landed, 16)
                    sp.dma_start(Bnat[1][:], s5_b_im[0]).then_inc(b_landed, 16)
                if k == 5:
                    for ri, src in ((0, s5_c_re), (1, s5_c_im)):
                        sp.dma_start(Cnat[ri][:], src[0].rearrange("(t g) q n -> (g q) t n", g=8)).then_inc(cm_landed, 16)
            col_chunks(0, 1, 1)
            sp.dma_start(xz[:], x.rearrange("b (a p) d -> p (b a) d", p=P)).then_inc(x_landed, 16)
            for n in range(RING):
                w_unit(runs[0], n, 0, n, 0)
            col_chunks(0, 2, 2)
            for r in runs:
                if r is runs[0]:
                    sp.wait_ge(col_used, STAGE * AU)
                if r is glu:
                    sp.wait_ge(w_lo_ready, glu.unit)
                    col_chunks(1, STAGE, STAGE)
                for i, q, q_first in iterations(sp, r):
                    col = [column(r.col[s], i, r.step) for s in range(r.blocks)]
                    u = column(r.unit, i, r.per)
                    if q is not None:
                        chunk0, layer, c0, _, _ = streamed(q_first)
                        c0 -= chunk0 * AW
                        ada_col, ada_first = column(c0, q, AW), column(0, q, AU)
                    for n in range(r.per):
                        s, k = divmod(n, r.units)
                        first = isinstance(i, int) and i == 0 and n < RING
                        early = r is glu and n == r.units - 1
                        if first and r is glu:
                            sp.wait_ge(col_used, COLS * AU + (n - RING + 1))
                        elif not (first and r is runs[0]) and not (r is glu and n == r.units):
                            sp.wait_ge(w_lo_ready, u + (n - RING + 1 + early))
                        if not (first and r is runs[0]):
                            w_unit(r, n, s, k, col[s])
                        if q is not None:
                            if r is glu and n == 1:
                                sp.wait_ge(s5_done, SEQ // TC)
                            for k in ada_at(n, r.per):
                                ada_unit(ada_first, k, layer, ada_col)
            for chunk in range(4):
                sp.wait_ge(out_ready, chunk + 1)
                sp.dma_start(out.rearrange("b (a p) d -> p (b a) d", p=P)[:, :, chunk * NB:(chunk + 1) * NB],
                             xz[:, :, chunk * NB:(chunk + 1) * NB]).then_inc(out_landed, 16)
            sp.wait_ge(out_landed, 64)

        @block.gpsimd
        def _(pool):
            nc.gpsimd.memset(ident[:], 0.0).then_inc(const_ready, 1)
            nc.gpsimd.memset(ones[:], 1.0).then_inc(constants, 1)
            pool.wait_ge(const_ready, 1)
            nc.gpsimd.affine_select(out=ident[:], in_=ident[:], compare_op=ALU.not_equal, fill=1.0, base=0,
                                    pattern=[[-1, P]], channel_multiplier=1).then_inc(constants, 1)
            for ri in range(2):
                nc.gpsimd.memset(Bdiag[ri][:], 0.0).then_inc(constants, 1)
            nc.gpsimd.memset(carry[:], 0.0).then_inc(constants, 1)

            def load_brow(q, q_first):
                if not (isinstance(q, int) and q == 0):
                    pool.wait_ge(chunk_summed, q)
                chunk0, layer, c0, _, _ = streamed(q_first)
                pool.dma_start(brow[:], ada_b[layer:layer + 1, ds(q * AW + (c0 - chunk0 * AW), AW)]).then_inc(brow_landed, 16)

            def load_rows(norm, chunk):
                if norm == NORMS and chunk >= 2:
                    pool.wait_ge(out_ready, chunk - 1)
                elif 4 * norm + chunk >= 2:
                    pool.wait_ge(row_used, 4 * norm + chunk - 1)
                for which, src in ((0, ln_g), (1, ln_b)):
                    pool.dma_start(lnrow[:, chunk % 2, which],
                                   src[norm // 2, norm % 2:norm % 2 + 1, chunk * NB:(chunk + 1) * NB].to_broadcast([P, NB])
                                   ).then_inc(rows_landed[chunk % 2], 16)

            for r in runs:
                if r.before == "ln":
                    if r.norm == 0:
                        pool.wait_ge(w_used, glu.unit + glu.n * glu.per)
                    if r.norm == 2:
                        pool.wait_ge(idx_full, TOK * IDX_HEADS)
                    for chunk in range(4):
                        load_rows(r.norm, chunk)
                if r is glu:
                    pool.wait_ge(s5_done, SEQ // TC)
                if r is attn_out:
                    pool.wait_ge(w_used, r.unit)
                    nc.gpsimd.memset(causal[:], 1.0).then_inc(const_ready, 1)
                    pool.wait_ge(const_ready, 2)
                    nc.gpsimd.affine_select(out=causal[:], in_=causal[:], compare_op=ALU.is_ge, fill=0.0, base=0,
                                            pattern=[[P, TOK], [-1, SEQ]], channel_multiplier=1).then_inc(constants, 1)
                if not r.ada and r.kind != "glu":
                    continue
                for i, q, q_first in iterations(pool, r):
                    if r.kind == "glu":
                        pool.wait_ge(w_used, r.unit + i * r.per)
                        for which, c0 in ((0, D), (1, 0)):
                            pool.dma_start(glub[:, which], s5_glu_b[0:1, ds(i * NB + c0, NB)]).then_inc(glub_landed, 16)
                    if q is not None:
                        load_brow(q, q_first)
            for chunk in range(4):
                load_rows(NORMS, chunk)

        @block.scalar
        def _(act):
            def hi_unit(u, n):
                act.wait_ge(w_landed[n % RING], u * (16 // RING) + (n // RING + 1) * 16)
                if not (isinstance(u, int) and u + n < RING):
                    act.wait_ge(w_used, u + (n - RING + 1))
                nc.scalar.activation(w_hi[:, n % RING], w_raw[:, n % RING], ACT.Copy).then_inc(w_hi_ready, 1)

            act.wait_ge(in_landed, 16 * 9)
            nc.scalar.activation(dt[:], ldt[:], ACT.Exp).then_inc(act_prep, 1)
            act.wait_ge(dve_prep, 1)
            nc.scalar.activation(mag[:], decay[:], ACT.Exp).then_inc(act_prep, 1)
            act.wait_ge(pe_prep, 1)
            nc.scalar.activation(csil[:], M[:, 0, 0:KT], ACT.Silu).then_inc(act_prep, 1)
            nc.scalar.activation(dcol[:], M[:, 0, KT:2 * KT], ACT.Copy)
            nc.scalar.activation(modcol[:], M[:, 0, 2 * P:3 * P], ACT.Copy).then_inc(bias_ready, 1)
            nc.scalar.activation(parT[:], M[:, 0, P:2 * P], ACT.Copy).then_inc(act_prep, 1)
            act.wait_ge(dve_prep, 2)
            nc.scalar.activation(sinv[:], turns[:], ACT.Sin)
            nc.scalar.activation(cosv[:], quarter[:], ACT.Sin).then_inc(act_prep, 1)
            for n in range(16):
                act.wait_ge(pe_prep, 12 + n)
                tab = (Btab if n < 8 else Ctab)[n % 8 // 4]
                j = n % 4
                nc.scalar.activation(tab[:, 4 * j:4 * j + 4, :], PS[n % 2][:, n // 2 % 2].rearrange("p (j m) -> p j m", m=P),
                                     ACT.Copy).then_inc(act_prep, 1)

            def make_h(r):
                act.wait_ge(scale_ready, r.h0 // 4 + 1)
                for g in range(4):
                    act.wait_ge(T_full, r.hturn + g + 1)
                    if g >= 2:
                        act.wait_ge(h_ready, r.h0 + g - 1)
                    h32 = stg[g % 2][:].rearrange("p a (b t) -> p (a b) t", t=SEQ)
                    for j in range(4):
                        k = 4 * g + j
                        ins = nc.scalar.activation(h32[:, j], T[:].rearrange("p a (b t) -> p (a b) t", t=SEQ)[:, j],
                                                   ACT.Identity, scale=scol[:, k:k + 1], bias=bcol[:, k:k + 1])
                    ins.then_inc(T_free, 1)
                    act.wait_ge(T_free, r.hturn + g + 1)
                    nc.scalar.activation(hT_hi[:, 4 * g:4 * g + 4], h32, ACT.Copy).then_inc(h_hi, 1)

            def std(norm):
                act.wait_ge(var_ready, norm + 1)
                nc.scalar.activation(rstd[:, :, 1], rstd[:, :, 0], ACT.Sqrt).then_inc(std_ready, 1)

            def read_T(r, i, k, dst, hi=False):
                act.wait_ge(T_full, r.turn + i * r.turns + (k + 1))
                n = dst.shape[1] if len(dst.shape) > 2 else 1
                src = T[:].rearrange("p a (b t) -> p (a b) t", t=SEQ)
                src = src[:, 0:n] if len(dst.shape) > 2 else src[:, 0]
                ins = nc.scalar.activation(dst, src, ACT.Copy)
                ins.then_inc(T_hi if hi else T_free, 1)

            def s5():
                for ch in range(SEQ // TC):
                    b = ch % 2
                    if ch == 0:
                        act.wait_ge(T_free, s5_in.turn + 4)
                        act.wait_ge(w_used, glu.unit)
                        act.wait_ge(chunk_stored, 2)
                    if ch >= 2:
                        act.wait_ge(y_ready, ch - 1)
                    nc.scalar.activation(uc[:, b], uT[:, :, ch * TC:(ch + 1) * TC], ACT.Copy).then_inc(uc_ready, 1)
                    if ch >= 2:
                        act.wait_ge(y_full, ch - 1)
                    for j4 in range(4):
                        act.wait_ge(bu_full, 4 * ch + j4 + 1)
                        for g in range(4):
                            dst = st[b][:, :, :, 16 * j4 + g:16 * j4 + g + 13:4].rearrange("p t r f -> p f r t")
                            src = PS[g // 2][:, g % 2].rearrange("p (f r t) -> p f r t", f=4, r=2)
                            for f in range(4):
                                ins = nc.scalar.activation(dst[:, f], src[:, f], ACT.Copy)
                        ins.then_inc(bu_read, 1)
                    if ch >= 1:
                        gelu(ch - 1)
                gelu(SEQ // TC - 1)

            def gelu(ch):
                act.wait_ge(y_ready, ch + 1)
                if ch >= 1:
                    act.wait_ge(s5_done, ch)
                nc.scalar.activation(y_act[:], y_in[:], ACT.Gelu_apprx_tanh).then_inc(g_ready, 1)
                act.wait_ge(g_ready, ch + 1)
                nc.scalar.activation(hT_hi[:, :, ch * TC:(ch + 1) * TC], y_act[:], ACT.Copy).then_inc(g_hi, 1)

            def attention():
                n = 0
                for t in range(TOK):
                    for h in range(IDX_HEADS):
                        act.wait_ge(idx_full, n + 1)
                        if n >= 2:
                            act.wait_ge(idx_read, n - 1)
                        else:
                            act.wait_ge(w_used, attn_out.unit)
                        nc.scalar.activation(relu[:, n % 2, 0:(t + 1) * P], PS[h % 2][:, h // 2 % 2, 0:(t + 1) * P],
                                             ACT.Relu, scale=IDX_DIM ** -0.5).then_inc(idx_relu, 1)
                        n += 1
                for a in range(TOK * HEADS + 2):
                    if a < TOK * HEADS:
                        N = (a // HEADS + 1) * P
                        act.wait_ge(lg_ready, a + 1)
                        if a >= 2:
                            act.wait_ge(pT_full, a - 1)
                        nc.scalar.activation(prob[:, a % 2, 0:N], logit[:, a % 2, 0:N], ACT.Exp, bias=soft[:, a % 4, 1:2],
                                             accum_out=soft[:, a % 4, 2:3]).then_inc(exp_done, 1)
                    if 1 <= a <= TOK * HEADS:
                        b = a - 1
                        N = (b // HEADS + 1) * P
                        act.wait_ge(pT_full, b + 1)
                        nc.scalar.activation(probT[:, b % 2, 0:N], T[:, b % 2, 0:N], ACT.Copy).then_inc(pT_ready, 1)
                    if a >= 5 and a % 4 == 1:
                        g = a // 4 - 1
                        t, h = divmod(4 * g, HEADS)
                        act.wait_ge(o_full, g + 1)
                        nc.scalar.activation(hT_hi[:, h:h + 4, t * P:(t + 1) * P],
                                             M[:, g % 2].rearrange("p (h t) -> p h t", t=P), ACT.Copy).then_inc(o_hi, 1)

            def finish(r, i, s):
                if r.kind in ("u", "v") or (r.kind in ("glu", "ff") and s == 0):
                    act.wait_ge(w_used, product(r, i, s))
                if r.kind == "u":
                    nc.scalar.activation(stg[s][:], PS[s][:], ACT.Copy).then_inc(ps_free[s], 1)
                if r.kind in ("glu", "ff") and s == 0:
                    act.wait_ge(ps_free[1], r.use[1] + i)
                    nc.scalar.activation(stg[0][:], PS[0][:], ACT.Sigmoid if r.kind == "glu" else ACT.Silu
                                         ).then_inc(ps_free[0], 1)
                if r.kind == "v":
                    nc.scalar.activation(v[:, :, cols(i, s)], PS[s][:], ACT.Copy).then_inc(ps_free[s], 1)

            def turned(r, i, s):
                if r.kind == "u":
                    read_T(r, i, s, uT[:, ds(i * 8 + s * 4, 4)])
                if r.kind == "rope":
                    read_T(r, i, s, qkT[:, ds(i * 8 + s * 4, 4)])
                if r.kind == "idx":
                    if s == 0:
                        act.wait_ge(row_used, 4 * (NORMS - 1))
                    read_T(r, i, s, qiT[:, 4 * s:4 * s + 4])
                if r.kind == "ff" and s == 1:
                    read_T(r, i, 0, aT_hi[:, ds(i * 4, 4)], hi=True)
                if r.kind == "ki" and s == 0:
                    read_T(r, i, 0, kiT[:])

            for r in runs:
                if r.before == "ln":
                    std(r.norm)
                if r.before in ("x", "ln"):
                    make_h(r)
                elif r.before == "s5":
                    s5()
                    act.wait_ge(y_full, SEQ // TC)
                    act.wait_ge(g_hi, SEQ // TC)
                elif r.before == "attention":
                    attention()
                if r is runs[0]:
                    act.wait_ge(dve_prep, 4)
                if r is runs[0] or r is glu:
                    for n in range(AHEAD):
                        hi_unit(r.unit, n)
                for i, q, q_first in iterations(act, r):
                    u = r.unit + i * r.per
                    stop = isinstance(i, int) and i == r.n - 1 and (r is runs[0] or r is runs[-1])
                    last = closing(r, i)
                    for n in range(r.per):
                        if n == 0 and last:
                            finish(*last, last[0].blocks - 1)
                        if r.blocks == 2 and n == r.units:
                            finish(r, i, 0)
                        if not (stop and n + AHEAD >= r.per):
                            hi_unit(u, n + AHEAD)
                        if n == 3 and last:
                            turned(*last, last[0].blocks - 1)
                        if r.blocks == 2 and n == r.units + 3:
                            turned(r, i, 0)
                if closes(r):
                    finish(r, r.n - 1, r.blocks - 1)
                    turned(r, r.n - 1, r.blocks - 1)
            std(NORMS)

        @block.vector
        def _(vec):
            V = nc.vector
            chain = [0]

            def link(ins):
                chain[0] += 1
                ins.then_inc(dve, 1)
                vec.wait_ge(dve, chain[0])

            def lo_unit(u, n):
                vec.wait_ge(w_hi_ready, u + (n + 1))
                V.tensor_tensor(w_lo[:, n % RING], w_raw[:, n % RING], w_hi[:, n % RING].bitcast(F32), ALU.subtract
                                ).then_inc(w_lo_ready, 1)

            def ada_unit(q, k):
                vec.wait_ge(ada_landed[k % ARING], q * (16 * AU // ARING) + 16 * (k // ARING + 1))
                if k == 0:
                    if not (isinstance(q, int) and q == 0):
                        vec.wait_ge(chunk_summed, q)
                    V.tensor_scalar(ada_acc[:], ada_raw[:, 0], csil[:, 0:1], None, ALU.mult).then_inc(ada_used, 1)
                else:
                    vec.wait_ge(ada_used, q * AU + k)
                    V.scalar_tensor_tensor(out=ada_acc[:], in0=ada_raw[:, k % ARING], scalar=csil[:, k:k + 1],
                                           in1=ada_acc[:], op0=ALU.mult, op1=ALU.add).then_inc(ada_used, 1)

            def store_chunk(q, q_first):
                chunk0, _, _, gate, column = streamed(q_first)
                vec.wait_ge(chunk_summed, q + 1)
                if gate is not None:
                    V.tensor_scalar(grow[:, ds((q - chunk0) * AW + gate * D, AW)], M[:, 1], 1.0, None, ALU.add
                                    ).then_inc(chunk_stored, 1)
                else:
                    V.tensor_copy(modcol[:, ds((q - chunk0) * (AW // P) + column, AW // P)], M[:, 1, 0:AW // P]
                                  ).then_inc(chunk_stored, 1)

            def store_columns(first, n, units):
                vec.wait_ge(col_used, units)
                c = slice(first * (CW // P), (first + n) * (CW // P))
                link(V.tensor_copy(modcol[:, c], M[:, 0, c]))

            vec.sem_inc(rope_ready, 1)
            vec.wait_ge(in_landed, 16 * 9)
            vec.wait_ge(act_prep, 1)
            V.tensor_copy(pos_f[:], pos_i[:])
            link(V.tensor_scalar(ang[:, 192:256], a_im[:], dt[:], None, ALU.mult))
            V.tensor_scalar(decay[:], a_re[:], dt[:], None, ALU.mult).then_inc(dve_prep, 1)
            for t in range(TOK):
                V.tensor_scalar(ang[:, t * 64:t * 64 + 64], cst[:, 0:64], pos_f[:, t:t + 1], None, ALU.mult)
                ins = V.tensor_scalar(ang[:, 128 + t * 32:160 + t * 32], cst[:, 64:96], pos_f[:, t:t + 1], None, ALU.mult)
            link(ins)
            link(V.tensor_scalar(turns[:], ang[:], 1.0 / TWO_PI, None, ALU.mult))
            link(V.tensor_scalar(turns[:], turns[:], ROUND, None, ALU.add))
            link(V.tensor_scalar(turns[:], turns[:], -ROUND, None, ALU.add))
            for part in (C1, C2, C3):
                link(V.scalar_tensor_tensor(out=ang[:], in0=turns[:], scalar=-part, in1=ang[:], op0=ALU.mult, op1=ALU.add))
            LIM = 3.1415925
            link(V.tensor_scalar(turns[:], ang[:], LIM, -LIM, ALU.min, ALU.max))
            link(V.tensor_scalar(ang[:], turns[:], TWO_PI / 4, None, ALU.add))
            link(V.tensor_scalar(quarter[:], ang[:], LIM, -TWO_PI, ALU.is_gt, ALU.mult))
            link(V.tensor_tensor(quarter[:], quarter[:], ang[:], ALU.add))
            V.tensor_scalar(quarter[:], quarter[:], LIM, -LIM, ALU.min, ALU.max).then_inc(dve_prep, 1)
            vec.wait_ge(act_prep, 5)
            V.tensor_copy(sin_t[:], sinv[:, 0:192])
            V.tensor_copy(cos_t[:], cosv[:, 0:192])
            V.tensor_tensor(lam[0][:], mag[:], cosv[:, 192:256], ALU.mult)
            link(V.tensor_tensor(lam[1][:], mag[:], sinv[:, 192:256], ALU.mult))
            V.tensor_scalar(num[:], lam[0][:], -1.0, None, ALU.add)
            V.tensor_tensor(q0[:], a_re[:], a_re[:], ALU.mult)
            link(V.tensor_tensor(q1[:], a_im[:], a_im[:], ALU.mult))
            link(V.tensor_tensor(den[:], q0[:], q1[:], ALU.add))
            link(V.reciprocal(den[:], den[:]))
            V.tensor_tensor(q0[:], num[:], a_re[:], ALU.mult)
            link(V.tensor_tensor(q1[:], lam[1][:], a_im[:], ALU.mult))
            link(V.tensor_tensor(q0[:], q0[:], q1[:], ALU.add))
            link(V.tensor_tensor(coef[0][:], q0[:], den[:], ALU.mult))
            V.tensor_tensor(q0[:], lam[1][:], a_re[:], ALU.mult)
            link(V.tensor_tensor(q1[:], num[:], a_im[:], ALU.mult))
            link(V.tensor_tensor(q0[:], q0[:], q1[:], ALU.subtract))
            link(V.tensor_tensor(coef[1][:], q0[:], den[:], ALU.mult))
            vec.wait_ge(b_landed, 32)
            wide = [coef[ri][:].unsqueeze(2).to_broadcast([P, STATE, GSIZE]) for ri in range(2)]
            V.tensor_tensor(Btmp[0][:], Bnat[0][:], wide[0], ALU.mult)
            link(V.tensor_tensor(Btmp[1][:], Bnat[1][:], wide[1], ALU.mult))
            for par in range(2):
                ins = V.tensor_tensor(Bbar[0][:, :, par].rearrange("p k n -> p n k"), Btmp[0][:], Btmp[1][:], ALU.subtract)
            link(ins)
            V.tensor_tensor(Btmp[0][:], Bnat[1][:], wide[0], ALU.mult)
            link(V.tensor_tensor(Btmp[1][:], Bnat[0][:], wide[1], ALU.mult))
            for ri in range(2):
                for par in range(2):
                    V.tensor_copy(lam_twice[ri][:, par], lam[ri][:])
            for par in range(2):
                ins = V.tensor_tensor(Bbar[1][:, :, par].rearrange("p k n -> p n k"), Btmp[0][:], Btmp[1][:], ALU.add)
            ins.then_inc(dve_prep, 1)
            vec.wait_ge(cm_landed, 32)
            for ri in range(2):
                for par in range(2):
                    ins = V.tensor_scalar(Cmask[ri][:, :, par, :], Cnat[ri][:], cst[:, 96 + par:97 + par],
                                          1.0 if ri == 0 else -1.0, ALU.mult, ALU.mult)
            ins.then_inc(dve_prep, 1)
            vec.wait_ge(constants, 5)
            vec.wait_ge(pe_prep, 3)
            for par in range(2):
                rows = slice(64 * par, 64 * par + 64)
                for row, col, ri, sign in ((0, 0, 0, 1.0), (0, 1, 1, -1.0), (1, 0, 1, 1.0), (1, 1, 0, 1.0)):
                    ins = V.tensor_scalar(lam4[rows, row, col, :], M[rows, 1, ri * P + par:ri * P + P:2], sign, None, ALU.mult)
            ins.then_inc(dve_prep, 1)
            for n in range(8):
                vec.wait_ge(pe_prep, 3 + n + 1)
                ri, p4 = divmod(n, 4)
                bank = PS[n % 2][:, n // 2 % 2].rearrange("p (k g o) -> p k g o", k=4, o=2)
                for par in range(2):
                    rows = slice(64 * par, 64 * par + 64)
                    ins = V.tensor_copy(Bdiag[ri][rows, :, par, 4 * p4:4 * p4 + 4].rearrange("p g k -> p k g"),
                                        bank[rows, :, :, par])
                ins.then_inc(dve_prep, 1)
            store_columns(0, STAGE, STAGE * AU)

            def make_scale(r):
                at_ = (2 * r.layer + (r.kind == "ff")) * 2 * KT
                shift, scale = modcol[:, at_:at_ + KT], modcol[:, at_ + KT:at_ + 2 * KT]
                if r.before == "x":
                    V.tensor_scalar(scol[:], scale, 1.0, None, ALU.add)
                    V.tensor_copy(bcol[:], shift).then_inc(scale_ready, 1)
                else:
                    gain, bias = parT[:, r.norm * KT:r.norm * KT + KT], parT[:, 64 + r.norm * KT:64 + r.norm * KT + KT]
                    V.scalar_tensor_tensor(out=scol[:], in0=scale, scalar=1.0, in1=gain, op0=ALU.add, op1=ALU.mult)
                    link(V.scalar_tensor_tensor(out=bcol[:], in0=scale, scalar=1.0, in1=bias, op0=ALU.add, op1=ALU.mult))
                    V.tensor_tensor(bcol[:], bcol[:], shift, ALU.add).then_inc(scale_ready, 1)

            def moments(norm):
                for t in range(TOK):
                    ins = V.bn_aggr(mv[:, t], stats[:, t])
                link(ins)
                V.tensor_scalar(rstd[:, :, 0], mv[:, :, 1], LN_EPS, None, ALU.add).then_inc(var_ready, 1)
                vec.wait_ge(std_ready, norm + 1)
                link(V.reciprocal(rstd[:, :, 1], rstd[:, :, 1]))

            def normalise(g):
                for t in range(TOK):
                    ins = V.tensor_scalar(xz[:, t, g * NB:(g + 1) * NB], xz[:, t, g * NB:(g + 1) * NB], mv[:, t, 0:1],
                                          rstd[:, t, 1:2], ALU.subtract, ALU.mult)
                return ins

            def make_h(r):
                if r.before == "ln":
                    moments(r.norm)
                make_scale(r)
                for g in range(5):
                    if g < 4 and r.before == "ln":
                        normalise(g).then_inc(xn_ready, 1)
                    if g >= 1:
                        vec.wait_ge(h_hi, r.h0 + g)
                        V.tensor_tensor(hT_lo[:, 4 * g - 4:4 * g].rearrange("p a t -> p (a t)"),
                                        stg[(g - 1) % 2][:].rearrange("p a t -> p (a t)"),
                                        hT_hi[:, 4 * g - 4:4 * g].rearrange("p a t -> p (a t)").bitcast(F32), ALU.subtract
                                        ).then_inc(h_ready, 1)

            def affine(norm, chunk, scale, last=None):
                vec.wait_ge(rows_landed[chunk % 2], 32 * (2 * norm + chunk // 2 + 1))
                part = xz[:, :, chunk * NB:(chunk + 1) * NB]
                gain, bias = (lnrow[:, chunk % 2, w].unsqueeze(1).to_broadcast([P, TOK, NB]) for w in range(2))
                link(V.scalar_tensor_tensor(out=part, in0=part, scalar=scale, in1=gain, op0=ALU.mult, op1=ALU.mult))
                V.scalar_tensor_tensor(out=part, in0=bias, scalar=scale, in1=part, op0=ALU.mult, op1=ALU.add
                                       ).then_inc(row_used if last is None else last, 1)

            def s5():
                n = 0

                def post(ch):
                    vec.wait_ge(y_full, ch + 1)
                    if ch >= 1:
                        vec.wait_ge(g_ready, ch)
                    link(V.tensor_tensor(y_in[:], uc[:, ch % 2], dcol[:].unsqueeze(2).to_broadcast([P, KT, TC]), ALU.mult))
                    V.tensor_tensor(y_in[:].rearrange("p k t -> p (k t)"), y_in[:].rearrange("p k t -> p (k t)"),
                                    T[:].rearrange("p a n -> p (a n)"), ALU.add).then_inc(y_ready, 1)

                def gelu_lo(ch):
                    vec.wait_ge(g_hi, ch + 1)
                    V.tensor_tensor(hT_lo[:, :, ch * TC:(ch + 1) * TC], y_act[:],
                                    hT_hi[:, :, ch * TC:(ch + 1) * TC].bitcast(F32), ALU.subtract).then_inc(s5_done, 1)

                for ch in range(SEQ // TC):
                    b = ch % 2
                    vec.wait_ge(bu_read, 4 * ch + 4)
                    for t in range(TC):
                        for half in range(2):
                            g = slice(32 * half, 32 * half + 32)
                            if n:
                                vec.wait_ge(rec, n - 1 + half)
                            s = carry[:, :, g] if t == 0 else st[b][:, t - 1, :, g]
                            V.tensor_tensor(prod[:, :, :, g], s.unsqueeze(1).to_broadcast([P, 2, 2, 32]), lam4[:, :, :, g],
                                            ALU.mult).then_inc(rec, 1)
                        for half in range(2):
                            g = slice(32 * half, 32 * half + 32)
                            vec.wait_ge(rec, n + 1 + half)
                            V.tensor_tensor(tmp[:, :, g], prod[:, :, 0, g], prod[:, :, 1, g], ALU.add).then_inc(rec, 1)
                        for half in range(2):
                            g = slice(32 * half, 32 * half + 32)
                            vec.wait_ge(rec, n + 3 + half)
                            V.tensor_tensor(st[b][:, t, :, g], tmp[:, :, g], st[b][:, t, :, g], ALU.add).then_inc(rec, 1)
                        n += 6
                        if ch >= 1 and t == 24:
                            post(ch - 1)
                        if ch >= 1 and t == 36:
                            gelu_lo(ch - 1)
                    vec.wait_ge(rec, n)
                    V.tensor_copy(carry[:], st[b][:, TC - 1]).then_inc(states_ready, 1)
                    vec.wait_ge(states_ready, ch + 1)
                post(SEQ // TC - 1)
                gelu_lo(SEQ // TC - 1)
                store_columns(STAGE, COLS - STAGE, COLS * AU)

            def rope(r, i, s, heads, half, table):
                vec.wait_ge(w_used, product(r, i, s))
                vec.wait_ge(T_full, r.turn + i * r.turns + (s - 1 if s else -1) if r.kind != "ki" else r.turn)
                vec.wait_ge(rope_ready, r.roped + i * r.blocks + s)
                c0 = IDX_HEADS if r.kind == "ki" else 0
                wide = heads * 2 * half
                for t in range(TOK):
                    at0 = t * half + (0 if table == "h" else 2 * (HD // 2))
                    shape = [P, heads, 2, half]
                    cosb, sinb = (w[:, at0:at0 + half].unsqueeze(1).unsqueeze(1).to_broadcast(shape) for w in (cos_t, sin_t))
                    src = PS[s][:, t, c0:c0 + wide].rearrange("p (h x d) -> p h x d", x=2, d=half)
                    dst = stg[s][:, t, 0:wide].rearrange("p (h x d) -> p h x d", x=2, d=half)
                    other = rt[:, 0:wide].rearrange("p (h x d) -> p h x d", x=2, d=half)
                    V.tensor_tensor(dst, src, cosb, ALU.mult)
                    link(V.tensor_tensor(other, src, sinb, ALU.mult))
                    if t == TOK - 1 and r.kind != "ki":
                        vec.sem_inc(ps_free[s], 1)
                    V.tensor_tensor(dst[:, :, 0], dst[:, :, 0], other[:, :, 1], ALU.subtract)
                    ins = V.tensor_tensor(dst[:, :, 1], dst[:, :, 1], other[:, :, 0], ALU.add)
                    if t < TOK - 1:
                        link(ins)
                return ins

            def links(r):
                return {"u": (0, 0), "v": (0, 0), "ff": (0, 0), "z": (2, 2) if r.part == 2 else (1, 1), "glu": (0, 3),
                        "rope": (3, 3), "idx": (3, 3), "ki": (0, 4)}[r.kind]

            def attention():
                vec.wait_ge(constants, 6)
                vec.wait_ge(T_full, attn_out.turn)
                link(V.tensor_scalar(off[:], causal[:], -MASKED, MASKED, ALU.mult, ALU.add))
                n = 0
                for t in range(TOK):
                    N = (t + 1) * P
                    for h in range(IDX_HEADS):
                        vec.wait_ge(idx_relu, n + 1)
                        if h == 0:
                            V.tensor_scalar(score[:, 0, 0:N], relu[:, n % 2, 0:N], wic[:, t, 0:1], None, ALU.mult
                                            ).then_inc(idx_read, 1)
                        else:
                            vec.wait_ge(idx_read, n)
                            V.scalar_tensor_tensor(out=score[:, 0, 0:N], in0=relu[:, n % 2, 0:N], scalar=wic[:, t, h:h + 1],
                                                   in1=score[:, 0, 0:N], op0=ALU.mult, op1=ALU.add).then_inc(idx_read, 1)
                        n += 1
                    vec.wait_ge(idx_read, n)
                    link(V.tensor_tensor(score[:, 1, 0:N], score[:, 0, 0:N], causal[:, t, 0:N], ALU.mult))
                    link(V.tensor_tensor(score[:, 0, 0:N], score[:, 1, 0:N], off[:, t, 0:N], ALU.add))
                    for k in range(TOPK // 8):
                        a, b = k % 2, 1 - k % 2
                        link(V.max(best[:], score[:, a, 0:N]))
                        link(V.match_replace(score[:, b, 0:N], best[:], score[:, a, 0:N], TAKEN))
                    a = TOPK // 8 % 2
                    link(V.tensor_scalar(score[:, 1 - a, 0:N], score[:, a, 0:N], (MASKED + TAKEN) / 2, None, ALU.is_le))
                    link(V.tensor_tensor(score[:, a, 0:N], score[:, 1 - a, 0:N], causal[:, t, 0:N], ALU.mult))
                    link(V.tensor_scalar(selb[:, t, 0:N], score[:, a, 0:N], -1.0, UNSEEN, ALU.add, ALU.mult))
                A = TOK * HEADS

                def o_lo(g):
                    t, h = divmod(4 * g, HEADS)
                    vec.wait_ge(o_hi, g + 1)
                    V.tensor_tensor(hT_lo[:, h:h + 4, t * P:(t + 1) * P], M[:, g % 2].rearrange("p (h t) -> p h t", t=P),
                                    hT_hi[:, h:h + 4, t * P:(t + 1) * P].bitcast(F32), ALU.subtract).then_inc(o_ready, 1)

                for a in range(A + 1):
                    if a < A:
                        t = a // HEADS
                        N = (t + 1) * P
                        vec.wait_ge(lg_full, a + 1)
                        if a >= 2:
                            vec.wait_ge(exp_done, a - 1)
                        link(V.scalar_tensor_tensor(out=logit[:, a % 2, 0:N], in0=PS[a % 2][:, 0, 0:N], scalar=HD ** -0.5,
                                                    in1=selb[:, t, 0:N], op0=ALU.mult, op1=ALU.add))
                        link(V.reduce_max(soft[:, a % 4, 0:1], logit[:, a % 2, 0:N], AXX))
                        V.tensor_scalar(soft[:, a % 4, 1:2], soft[:, a % 4, 0:1], -1.0, None, ALU.mult).then_inc(lg_ready, 1)
                    if a >= 1:
                        b = a - 1
                        N = (b // HEADS + 1) * P
                        vec.wait_ge(exp_done, b + 1)
                        link(V.reciprocal(soft[:, b % 4, 3:4], soft[:, b % 4, 2:3]))
                        V.tensor_scalar(prob[:, b % 2, 0:N], prob[:, b % 2, 0:N], soft[:, b % 4, 3:4], None, ALU.mult
                                        ).then_inc(p_ready, 1)
                    if a % 4 == 3 and a >= 7:
                        o_lo(a // 4 - 1)
                o_lo(A // 4 - 1)

            def chain_at(r, i, s):
                chain[0] = r.chain + i * sum(links(r)) + s * links(r)[0]

            def finish(r, i, s):
                full = r.use[s] + i + 1
                if r.kind == "z":
                    vec.wait_ge(w_used, product(r, i, s))
                    c = cols(i, s)
                    gate = 0 if r is attn_out else D
                    g = grow[:, ds(gate + i * (2 * NB) + s * NB, NB)].unsqueeze(1).to_broadcast([P, TOK, NB])
                    V.tensor_tensor(stg[s][:], PS[s][:], g, ALU.mult).then_inc(ps_free[s], 1)
                    vec.wait_ge(ps_free[s], full)
                    link(V.tensor_tensor(xz[:, :, c], xz[:, :, c], stg[s][:], ALU.add))
                    if r.part == 2:
                        for t in range(TOK):
                            ins = V.bn_stats(stats[:, t, ds(i * 2 + s, 1)].rearrange("p a b -> p (a b)"), xz[:, t, c])
                        link(ins)
                if r.kind == "glu" and s == 1:
                    vec.wait_ge(ps_free[0], r.use[0] + i + 1)
                    vec.wait_ge(w_used, product(r, i, 1))
                    V.tensor_tensor(stg[1][:], stg[0][:], PS[1][:], ALU.mult).then_inc(ps_free[1], 1)
                    vec.wait_ge(ps_free[1], full)
                    c = ds(i * NB, NB)
                    g = grow[:, c].unsqueeze(1).to_broadcast([P, TOK, NB])
                    link(V.tensor_tensor(stg[1][:], stg[1][:], g, ALU.mult))
                    link(V.tensor_tensor(xz[:, :, c], xz[:, :, c], stg[1][:], ALU.add))
                    for t in range(TOK):
                        ins = V.bn_stats(stats[:, t, ds(i, 1)].rearrange("p a b -> p (a b)"), xz[:, t, c])
                    link(ins)
                if r.kind == "ff" and s == 1:
                    vec.wait_ge(ps_free[0], r.use[0] + i + 1)
                    vec.wait_ge(w_used, product(r, i, 1))
                    V.tensor_tensor(stg[1][:], stg[0][:], PS[1][:], ALU.mult).then_inc(ps_free[1], 1)
                if r.kind in ("rope", "idx"):
                    heads, half, table = (4, 64, "h") if r.kind == "rope" else (8, 32, "i")
                    rope(r, i, s, heads, half, table).then_inc(rope_ready, 1)
                if r.kind == "ki":
                    link(rope(r, i, 0, 1, 32, "i"))
                    V.tensor_copy(stg[0][:, :, 64:128], stg[0][:, :, 0:64]).then_inc(rope_ready, 1)
                    V.tensor_scalar(wic[:], PS[0][:, :, 0:IDX_HEADS], IDX_HEADS ** -0.5, None, ALU.mult
                                    ).then_inc(ps_free[0], 1)

            def turned(r, i, s):
                if r.kind == "ff" and s == 1:
                    vec.wait_ge(T_hi, r.aT0 + i + 1)
                    V.tensor_tensor(aT_lo[:, ds(i * 4, 4)].rearrange("p a t -> p (a t)"), T[:].rearrange("p a t -> p (a t)"),
                                    aT_hi[:, ds(i * 4, 4)].rearrange("p a t -> p (a t)").bitcast(F32), ALU.subtract
                                    ).then_inc(T_free, 1)

            for r in runs:
                if r.before in ("x", "ln"):
                    make_h(r)
                    if r.before == "ln":
                        for chunk in range(4):
                            affine(r.norm, chunk, ALPHA)
                    else:
                        vec.wait_ge(T_full, r.hturn + 4)
                        link(V.tensor_scalar(xz[:].rearrange("p a d -> p (a d)"), xz[:].rearrange("p a d -> p (a d)"), ALPHA,
                                             None, ALU.mult))
                elif r.before == "s5":
                    s5()
                elif r.before == "attention":
                    attention()
                if r is runs[0] or r is glu:
                    for n in range(AHEAD):
                        lo_unit(r.unit, n)
                before = runs[runs.index(r) - 1]
                r.chain = chain[0] if r.before else before.chain + before.n * sum(links(before))
                for i, q, q_first in iterations(vec, r):
                    u = r.unit + i * r.per
                    stop = isinstance(i, int) and i == r.n - 1 and (r is runs[0] or r is runs[-1])
                    last = closing(r, i)
                    for n in range(r.per):
                        if n == 0 and last:
                            chain_at(*last, 1)
                            finish(*last, last[0].blocks - 1)
                        if r.blocks == 2 and n == r.units:
                            chain_at(r, i, 0)
                            finish(r, i, 0)
                        if not (stop and n + AHEAD >= r.per):
                            lo_unit(u, n + AHEAD)
                        if q is not None:
                            for kk in ada_at(n, r.per):
                                ada_unit(q, kk)
                            if n == r.per - 1:
                                store_chunk(q, q_first)
                        if n == 3 and last:
                            turned(*last, last[0].blocks - 1)
                if closes(r):
                    chain_at(r, r.n - 1, 1)
                    finish(r, r.n - 1, r.blocks - 1)
                    turned(r, r.n - 1, r.blocks - 1)
            moments(NORMS)
            for chunk in range(4):
                link(normalise(chunk))
            for chunk in range(4):
                affine(NORMS, chunk, 1.0, last=out_ready)

        @block.tensor
        def _(pe):
            MM = nc.tensor.matmul

            def turn_T(full, wait, src):
                for sem_, value in wait:
                    pe.wait_ge(sem_, value)
                if not (isinstance(full, int) and full == 1):
                    pe.wait_ge(T_free, full - 1)
                for t in range(TOK):
                    for j in range(4):
                        ins = nc.tensor.transpose(T[:, j // 2, (j % 2) * SEQ + t * P:(j % 2) * SEQ + (t + 1) * P],
                                                  src(t, j), ident[:])
                ins.then_inc(T_full, 1)

            def sum_chunk(q, q_first):
                pe.wait_ge(ada_used, (q + 1) * AU)
                pe.wait_ge(brow_landed, (q + 1) * 16)
                if not (isinstance(q, int) and q == 0):
                    pe.wait_ge(chunk_stored, q)
                if streamed(q_first)[3] is not None:
                    MM(M[:, 1], ones[:], ada_acc[:], start=True, stop=False)
                    ins = MM(M[:, 1], ones[0:1, :], brow[:], start=False, stop=True)
                else:
                    for j in range(AW // P):
                        MM(M[:, 1, j:j + 1], ada_acc[:, j * P:(j + 1) * P], ones[:, 0:1], start=True, stop=False)
                        ins = MM(M[:, 1, j:j + 1], brow[:, j * P:(j + 1) * P], ones[0:1, 0:1], start=False, stop=True)
                ins.then_inc(chunk_summed, 1)

            def open_columns(first, n):
                c = slice(first * (CW // P), (first + n) * (CW // P))
                MM(M[:, 0, c], ident[:], modcol[:, c], start=True, stop=False)

            def col_chunk(ring, m, last=False):
                for k in range(AU):
                    pe.wait_ge(col_landed[k % RING], m * (16 * AU // RING) + 16 * (k // RING + 1))
                    for j in range(CW // P):
                        ins = MM(M[:, 0, ds(m * (CW // P) + j, 1)], col_raw[ring][:, k % RING, j * P:(j + 1) * P],
                                 csil[:, k:k + 1], start=False,
                                 stop=last and k == AU - 1 and j == CW // P - 1)
                    ins.then_inc(col_used, 1)

            pe.wait_ge(constants, 2)
            pe.wait_ge(in_landed, 16 * 9)
            nc.tensor.transpose(M[:, 0, 0:2 * KT], cdn[:], ident[0:2 * KT, 0:2 * KT])
            pe.wait_ge(bias_landed, 64)
            nc.tensor.transpose(M[:, 0, 2 * P:3 * P], biasn[:], ident[:])
            nc.tensor.transpose(M[:, 0, P:2 * P], parn[:], ident[:]).then_inc(pe_prep, 1)
            pe.wait_ge(act_prep, 4)
            pe.wait_ge(bias_ready, 1)
            open_columns(0, STAGE)
            col_chunk(0, 0)
            pe.wait_ge(dve_prep, 3)

            nc.tensor.transpose(M[:, 1, 0:P], lam_twice[0][:].rearrange("p a n -> p (a n)"), ident[:]).then_inc(pe_prep, 1)
            nc.tensor.transpose(M[:, 1, P:2 * P], lam_twice[1][:].rearrange("p a n -> p (a n)"), ident[:]).then_inc(pe_prep, 1)
            for n in range(8):
                if n >= 4:
                    pe.wait_ge(dve_prep, 6 + n - 4)
                ri, p4 = divmod(n, 4)
                for k in range(4):
                    ins = nc.tensor.transpose(PS[n % 2][:, n // 2 % 2, k * P:(k + 1) * P],
                                              Bbar[ri][:, 4 * p4 + k].rearrange("p a n -> p (a n)"), ident[:])
                ins.then_inc(pe_prep, 1)
            col_chunk(0, 1)
            for n in range(16):
                if n < 4:
                    pe.wait_ge(dve_prep, 13)
                else:
                    pe.wait_ge(act_prep, 6 + n - 4)
                ri, j4 = divmod(n % 8, 4)
                for k in range(4):
                    j = 4 * j4 + k
                    src = Bdiag[ri][:, 4 * j:4 * j + 4].rearrange("p g a k -> p (g a k)") if n < 8 else \
                        Cmask[ri][:, j].rearrange("p a n -> p (a n)")
                    ins = nc.tensor.transpose(PS[n % 2][:, n // 2 % 2, k * P:(k + 1) * P], src, ident[:])
                ins.then_inc(pe_prep, 1)
            pe.wait_ge(dve_prep, 5)
            for m in range(2, STAGE):
                col_chunk(0, m, last=m == STAGE - 1)

            def s5():
                for ch in range(SEQ // TC + 1):
                    if ch < SEQ // TC:
                        b = ch % 2
                        pe.wait_ge(uc_ready, ch + 1)
                        for j4 in range(4):
                            if ch or j4:
                                pe.wait_ge(bu_read, 4 * ch + j4)
                            else:
                                for s in range(2):
                                    pe.wait_ge(ps_free[s], s5_in.n)
                            for f in range(4):
                                for g in range(4):
                                    rows = slice(32 * g, 32 * g + 32)
                                    for ri in range(2):
                                        at_ = (2 * f + ri) * TC
                                        ins = MM(PS[g // 2][:, g % 2, at_:at_ + TC], Btab[ri][rows, 4 * j4 + f, :],
                                                 uc[rows, b, 4 * j4 + f, :], start=True, stop=True)
                            ins.then_inc(bu_full, 1)
                    if ch >= 1:
                        if ch == 1:
                            open_columns(STAGE, STAGE)
                        col_chunk(1, STAGE + ch - 1, last=ch == SEQ // TC)
                        b = (ch - 1) % 2
                        pe.wait_ge(states_ready, ch)
                        if ch >= 2:
                            pe.wait_ge(y_ready, ch - 1)
                        for f in range(KT):
                            for g in range(4):
                                rows = slice(32 * g, 32 * g + 32)
                                for ri in range(2):
                                    ins = MM(T[rows, f // 8, f % 8 * TC:f % 8 * TC + TC], Ctab[ri][:, f, rows],
                                             st[b][:, :, ri, 4 * f + g], start=ri == 0, stop=ri == 1)
                        ins.then_inc(y_full, 1)

            def attention():
                n = 0
                pe.wait_ge(T_free, attn_out.turn)
                pe.wait_ge(ps_free[0], attn_out.use[0])
                pe.wait_ge(ps_free[1], attn_out.use[1])
                for t in range(TOK):
                    N = (t + 1) * P
                    for h in range(IDX_HEADS):
                        if n >= 4:
                            pe.wait_ge(idx_relu, n - 3)
                        rows = slice(64 * (h % 2), 64 * (h % 2) + 64)
                        MM(PS[h % 2][:, h // 2 % 2, 0:N], qiT[rows, h // 2, t * P:(t + 1) * P], kiT[rows, 0:N],
                           start=True, stop=True).then_inc(idx_full, 1)
                        n += 1
                A = TOK * HEADS
                pe.wait_ge(idx_relu, n)
                pe.wait_ge(chunk_stored, attn_out_chunks)
                for a in range(A + 2):
                    if a < A:
                        t, h = divmod(a, HEADS)
                        N = (t + 1) * P
                        if a >= 2:
                            pe.wait_ge(lg_ready, a - 1)
                        MM(PS[a % 2][:, 0, 0:N], qkT[:, h, t * P:(t + 1) * P], qkT[:, HEADS + h, 0:N],
                           start=True, stop=True).then_inc(lg_full, 1)
                    if 1 <= a <= A:
                        b = a - 1
                        pe.wait_ge(p_ready, b + 1)
                        if b >= 2:
                            pe.wait_ge(pT_ready, b - 1)
                        for k in range(b // HEADS + 1):
                            ins = nc.tensor.transpose(T[:, b % 2, k * P:(k + 1) * P], prob[:, b % 2, k * P:(k + 1) * P], ident[:])
                        ins.then_inc(pT_full, 1)
                    if a >= 2:
                        b = a - 2
                        t, h = divmod(b, HEADS)
                        pe.wait_ge(pT_ready, b + 1)
                        if b % 4 == 0 and b >= 8:
                            pe.wait_ge(o_ready, b // 4 - 1)
                        for k in range(t + 1):
                            ins = MM(M[:, b // 4 % 2, b % 4 * P:(b % 4 + 1) * P], v[:, k, h * P:(h + 1) * P],
                                     probT[:, b % 2, k * P:(k + 1) * P], start=k == 0, stop=k == t)
                        if b % 4 == 3:
                            ins.then_inc(o_full, 1)

            def turn(r, i, s):
                if r.kind in ("u", "rope", "idx"):
                    ready = (ps_free[s], r.use[s] + i + 1) if r.kind == "u" else (rope_ready, r.roped + i * 2 + (s + 1))
                    turn_T(r.turn + i * r.turns + (s + 1), [ready], lambda t, j: stg[s][:, t, j * P:(j + 1) * P])
                if r.kind == "ff" and s == 1:
                    turn_T(r.turn + i + 1, [(ps_free[1], r.use[1] + i + 1)], lambda t, j: stg[1][:, t, j * P:(j + 1) * P])
                if r.kind == "ki":
                    pe.wait_ge(rope_ready, r.roped + 1)
                    pe.wait_ge(T_free, r.turn)
                    for t in range(TOK):
                        ins = nc.tensor.transpose(T[:, 0, t * P:(t + 1) * P], stg[0][:, t, 0:P], ident[:])
                    ins.then_inc(T_full, 1)

            pe.wait_ge(act_prep, 21)
            for r in runs:
                if r.before in ("x", "ln"):
                    for g in range(4):
                        wait = [(x_landed, 16)] if r.before == "x" else [(xn_ready, 4 * r.norm + g + 1)]
                        turn_T(r.hturn + g + 1, wait, lambda t, j, g=g: xz[:, t, g * NB + j * P:g * NB + (j + 1) * P])
                elif r.before == "s5":
                    s5()
                elif r.before == "attention":
                    attention()
                for i, q, q_first in iterations(pe, r):
                    u = r.unit + i * r.per
                    last = closing(r, i)
                    for n in range(r.per):
                        s, k = divmod(n, r.units)
                        if n == 3 and last:
                            turn(*last, last[0].blocks - 1)
                        if s == 1 and k == 3:
                            turn(r, i, 0)
                        if k == 0 and not (isinstance(i, int) and r.use[s] + i == 0):
                            pe.wait_ge(ps_free[s], r.use[s] + i)
                        pe.wait_ge(w_lo_ready, u + (n + 1))
                        if r.kind == "z" and r.before is None:
                            pe.wait_ge(T_free, ff_turn + k // 2 + 1)
                            hi, lo = aT_hi, aT_lo
                        else:
                            if r.kind == "glu":
                                pe.wait_ge(s5_done, SEQ // TC)
                            elif r.before == "attention":
                                pe.wait_ge(o_ready, TOK * HEADS // 4)
                            elif r.before in ("x", "ln"):
                                pe.wait_ge(h_ready, r.h0 + k // 2 + 1)
                            hi, lo = hT_hi, hT_lo
                        if k == 0 and r.kind == "glu":
                            pe.wait_ge(glub_landed, i * 32 + 32)
                            for t in range(TOK):
                                MM(PS[s][:, t], ones[0:1, :], glub[:, s], start=True, stop=False)
                        for t in range(TOK):
                            for kk in range(UK):
                                kt = k * UK + kk
                                tok = slice(t * P, (t + 1) * P)
                                for m, (a_, b_) in enumerate(((hi, w_hi), (hi, w_lo), (lo, w_hi))):
                                    ins = MM(PS[s][:, t, 0:r.width], a_[:, kt, tok], b_[:, n % RING, kk, 0:r.width],
                                             start=kt == 0 and m == 0 and r.kind != "glu",
                                             stop=k == r.units - 1 and kk == UK - 1 and m == 2)
                        ins.then_inc(w_used, 1)
                        if q is not None and n == r.per - 3:
                            sum_chunk(q, q_first)
                if closes(r):
                    turn(r, r.n - 1, r.blocks - 1)
                if r.kind == "ff":
                    ff_turn = r.turn


_INS = ["x", "c", "positions", "ada_w", "ada_b", "ln_g", "ln_b", "s5_in_w", "s5_a_re", "s5_a_im", "s5_log_dt", "s5_b_re",
        "s5_b_im", "s5_c_re", "s5_c_im", "s5_d", "s5_glu_w", "s5_glu_b", "dsa_in_w", "dsa_out_w", "ffn_w_in", "ffn_w_out"]


def kernel(**inputs):
    import concourse.bacc as bacc
    from concourse.bass_utils import run_bass_kernel_spmd

    nc = bacc.Bacc("TRN2", target_bir_lowering=False, num_devices=1)
    arrays, args = {}, []
    for name in _INS:
        a = np.ascontiguousarray(inputs[name])
        arrays[f"in_{name}"] = a
        args.append(nc.dram_tensor(f"in_{name}", a.shape, mybir.dt.from_np(a.dtype), kind="ExternalInput").ap())
    arrays["in_consts"] = shape_constants()
    args.append(nc.dram_tensor("in_consts", (P, 98), F32, kind="ExternalInput").ap())
    args.append(nc.dram_tensor("out", (1, SEQ, D), F32, kind="ExternalOutput").ap())
    build(nc, *args)
    r = run_bass_kernel_spmd(nc, [arrays], core_ids=[0])
    return r.results[0]["out"]
```

```python
from contextlib import ExitStack

import numpy as np

import concourse.bass as bass
from concourse import mybir

F32 = mybir.dt.float32
F32R = mybir.dt.float32r
I32 = mybir.dt.int32
ALU = mybir.AluOpType
ACT = mybir.ActivationFunctionType
AXX = mybir.AxisListType.X
ds = bass.ds

P = 128
SEQ = 256
TOK = SEQ // P
D = 2048
KT = D // P
DEPTH = 2
HEADS = 16
HD = D // HEADS
IDX_HEADS = 16
IDX_DIM = 64
TOPK = min(256, SEQ // 4)
D_FF = 5632
GROUPS = 128
GSIZE = 16
STATE = 64
ALPHA = (2.0 * DEPTH) ** 0.25
LN_EPS = 1e-5
ROPE_THETA = 10000.0

NB = 512
UK = 2
RING = 4
CW = 1024
STAGE = 2 * D // CW
AW = 512
AU = D // P
LAPS = AU // RING
SHARED = 2
COL_PE = SHARED * LAPS
COL_DVE = STAGE * AU - COL_PE
ARING = 8
G = D // AW
STREAM = [(0, 0, 2 * D, 0, None), (G, 0, 5 * D, 1, None), (2 * G, 1, 2 * D, 0, None),
          (3 * G, 1, 0, None, 4 * KT), (5 * G, 1, 3 * D, None, 6 * KT), (7 * G, 1, 5 * D, 1, None)]
TC = 64
PAIRS = GROUPS // 2
TWO_PI = 6.283185307179586
C1 = 6.28125
C2 = float(np.float32(int((TWO_PI - C1) * 2 ** 21) / 2 ** 21))
C3 = float(np.float32(TWO_PI - C1 - C2))
ROUND = 12582912.0
MASKED = -3.0e38
TAKEN = -3.3e38
UNSEEN = 1.0e30


def shape_constants():
    out = np.zeros((P, 98), np.float32)
    for at, dim in ((0, HD), (HD // 2, IDX_DIM)):
        power = np.arange(0, dim, 2, dtype=np.float32) / np.float32(dim)
        out[:, at:at + dim // 2] = np.float32(1.0) / np.power(np.float32(ROPE_THETA), power).astype(np.float32)
    odd = (np.arange(P) // GSIZE) % 2
    out[:, 96] = 1 - odd
    out[:, 97] = odd
    return out


def build(nc, x, c, positions, ada_w, ada_b, ln_g, ln_b, s5_in_w, s5_a_re, s5_a_im, s5_log_dt, s5_b_re, s5_b_im,
          s5_c_re, s5_c_im, s5_d, s5_glu_w, s5_glu_b, dsa_in_w, dsa_out_w, ffn_w_in, ffn_w_out, consts, out):
    ctx = ExitStack()
    with ctx:
        K = 1024
        MAP = {}
        top = [0]

        def region(name, size):
            MAP[name] = top[0]
            top[0] += size

        for name, size in (("xz", 16 * K), ("hT_hi", 16 * K), ("hT_lo", 16 * K), ("aT_hi", 16 * K), ("aT_lo", 16 * K),
                           ("w_raw", 16 * K), ("w_hi", 16 * K), ("w_lo", 16 * K), ("growA", 8 * K), ("growB", 8 * K),
                           ("ada_raw", 16 * K), ("ada_acc", 4 * K), ("brow", 4 * K), ("lnrow", 8 * K), ("stgA", 4 * K),
                           ("stgB", 4 * K), ("uT", 16 * K), ("ident", 512), ("ones", 512), ("parT", 512),
                           ("sin", 768), ("cos", 768), ("modcol", 768), ("phase", 3 * K), ("small", 768)):
            region(name, size)
        base = (nc.sbuf_base + 31) // 32 * 32
        ctx.enter_context(nc.sbuf_tensor("slab", [P, top[0] // 4], F32))

        def at(name, where, shape, dtype=F32, plus=0):
            return nc.alloc_sbuf_tensor_at(name, shape, dtype, offset=base + MAP[where] + plus)

        xz = at("xz", "xz", [P, TOK, D])
        hT_hi = at("hT_hi", "hT_hi", [P, KT, SEQ], F32R)
        hT_lo = at("hT_lo", "hT_lo", [P, KT, SEQ], F32R)
        aT_hi = at("aT_hi", "aT_hi", [P, KT, SEQ], F32R)
        aT_lo = at("aT_lo", "aT_lo", [P, KT, SEQ], F32R)
        w_raw = at("w_raw", "w_raw", [P, RING, UK, NB])
        w_hi = at("w_hi", "w_hi", [P, RING, UK, NB], F32R)
        w_lo = at("w_lo", "w_lo", [P, RING, UK, NB], F32R)
        grow = at("grow", "growA", [P, 2 * D])
        ada_raw = at("ada_raw", "ada_raw", [P, ARING, AW])
        ada_acc = at("ada_acc", "ada_acc", [P, AW])
        brow = at("brow", "brow", [P, AW])
        col_acc = [at("col_acc0", "ada_acc", [P, CW]), at("col_acc1", "brow", [P, CW])]
        col_row = at("col_row", "w_lo", [P, CW], plus=12 * K)
        col_raw = [at("col_raw0", "ada_raw", [P, RING, CW]), at("col_raw1", "w_raw", [P, RING, CW])]
        lnrow = at("lnrow", "lnrow", [P, 2, 2, NB])
        glub = at("glub", "lnrow", [P, 2, NB])
        stg = [at("stgA", "stgA", [P, TOK, NB]), at("stgB", "stgB", [P, TOK, NB])]
        ident = at("ident", "ident", [P, P])
        ones = at("ones", "ones", [P, P])
        parT = at("parT", "parT", [P, P])
        sin_t = at("sin_t", "sin", [P, 192])
        cos_t = at("cos_t", "cos", [P, 192])
        modcol = at("modcol", "modcol", [P, 4 * DEPTH * KT])
        csil = at("csil", "small", [P, KT])
        dcol = at("dcol", "small", [P, KT], plus=64)
        scol = at("scol", "small", [P, KT], plus=128)
        bcol = at("bcol", "small", [P, KT], plus=192)
        stats = at("stats", "small", [P, TOK, 4, 6], plus=256)
        mv = at("mv", "small", [P, TOK, 2], plus=448)
        rstd = at("rstd", "small", [P, TOK, 2], plus=480)
        wic = at("wic", "small", [P, TOK, IDX_HEADS], plus=512)
        soft = at("soft", "small", [P, 4, 4], plus=640)

        uT = at("uT", "uT", [P, KT, SEQ])
        st = [at("st0", "w_hi", [P, TC, 2, PAIRS]), at("st1", "growB", [P, TC, 2, PAIRS])]
        uc = at("uc", "lnrow", [P, 2, 4, 4, TC])
        y_in = at("y_in", "stgA", [P, KT, TC])
        y_act = at("y_act", "stgB", [P, KT, TC])
        Btab = [at("B_re_tab", "aT_hi", [P, KT, P]), at("B_im_tab", "aT_hi", [P, KT, P], plus=8 * K)]
        Ctab = [at("C_re_tab", "aT_lo", [P, KT, P]), at("C_im_tab", "aT_lo", [P, KT, P], plus=8 * K)]
        prod = at("prod", "phase", [P, 2, 2, PAIRS])
        tmp = at("tmp", "phase", [P, 2, PAIRS], plus=1024)
        carry = at("carry", "phase", [P, 2, PAIRS], plus=1536)
        lam4 = at("lam4", "phase", [P, 2, 2, PAIRS], plus=2048)
        Bnat = [at("Bnat_re", "w_hi", [P, STATE, GSIZE]), at("Bnat_im", "w_hi", [P, STATE, GSIZE], plus=4 * K)]
        Cnat = [at("Cnat_re", "w_hi", [P, KT, STATE], plus=8 * K), at("Cnat_im", "w_hi", [P, KT, STATE], plus=12 * K)]
        Bbar = [at("Bbar_re", "w_lo", [P, GSIZE, 2, STATE]), at("Bbar_im", "w_lo", [P, GSIZE, 2, STATE], plus=8 * K)]
        Btmp = [at("Btmp0", "aT_hi", [P, STATE, GSIZE]), at("Btmp1", "aT_hi", [P, STATE, GSIZE], plus=4 * K)]
        Bdiag = [at("Bdiag_re", "hT_hi", [P, PAIRS, 2, GSIZE]), at("Bdiag_im", "hT_hi", [P, PAIRS, 2, GSIZE], plus=8 * K)]
        Cmask = [at("Cmask_re", "hT_lo", [P, KT, 2, STATE]), at("Cmask_im", "hT_lo", [P, KT, 2, STATE], plus=8 * K)]
        scratch = [0]

        def pre(name, shape, dtype=F32):
            t = at(name, "uT", shape, dtype, plus=scratch[0])
            n = 4
            for s in shape[1:]:
                n *= s
            scratch[0] += (n + 31) // 32 * 32
            return t

        cst = pre("cst", [P, 98])
        parn = pre("parn", [P, P])
        cdn = pre("cdn", [2 * KT, P])
        biasn = pre("biasn", [P, P])
        pos_i = pre("pos_i", [P, TOK], I32)
        pos_f = pre("pos_f", [P, TOK])
        a_re = pre("a_re", [P, STATE])
        a_im = pre("a_im", [P, STATE])
        ldt = pre("ldt", [P, 1])
        dt = pre("dt", [P, 1])
        decay = pre("decay", [P, STATE])
        mag = pre("mag", [P, STATE])
        ang = pre("ang", [P, 256])
        turns = pre("turns", [P, 256])
        quarter = pre("quarter", [P, 256])
        sinv = pre("sinv", [P, 256])
        cosv = pre("cosv", [P, 256])
        lam = [pre("lam_re", [P, STATE]), pre("lam_im", [P, STATE])]
        lam_twice = [pre("lam_re_twice", [P, 2, STATE]), pre("lam_im_twice", [P, 2, STATE])]
        num = pre("num", [P, STATE])
        den = pre("den", [P, STATE])
        q0 = pre("q0", [P, STATE])
        q1 = pre("q1", [P, STATE])
        coef = [pre("coef_re", [P, STATE]), pre("coef_im", [P, STATE])]
        assert scratch[0] <= 16 * K

        qkT = at("qkT", "aT_hi", [P, 2 * HEADS, SEQ])
        v = at("v", "uT", [P, TOK, D])
        qiT = at("qiT", "lnrow", [P, IDX_HEADS // 2, SEQ])
        kiT = at("kiT", "phase", [P, SEQ], plus=2048)
        selb = at("selb", "phase", [P, TOK, SEQ])
        rt = at("rt", "phase", [P, NB])
        causal = at("causal", "hT_hi", [P, TOK, SEQ])
        score = at("score", "hT_hi", [P, 2, SEQ], plus=2 * K)
        relu = at("relu", "hT_hi", [P, 2, SEQ], plus=4 * K)
        off = at("off", "hT_hi", [P, TOK, SEQ], plus=6 * K)
        best = at("best", "hT_hi", [P, 8], plus=8 * K)
        logit = at("logit", "stgA", [P, 2, SEQ])
        prob = at("prob", "stgA", [P, 2, SEQ], plus=2 * K)
        probT = at("probT", "stgB", [P, 2, SEQ])

        PS = [ctx.enter_context(nc.psum_tensor("psA", [P, TOK, NB], F32)),
              ctx.enter_context(nc.psum_tensor("psB", [P, TOK, NB], F32))]
        T = ctx.enter_context(nc.psum_tensor("psT", [P, 2, NB], F32))
        M = ctx.enter_context(nc.psum_tensor("psM", [P, 2, NB], F32))

        def sem(name):
            return ctx.enter_context(nc.semaphore(name))

        w_landed = [sem(f"w_landed{n}") for n in range(RING)]
        w_hi_ready, w_lo_ready, w_used = sem("w_hi_ready"), sem("w_lo_ready"), sem("w_used")
        ada_landed = [sem(f"ada_landed{n}") for n in range(ARING)]
        ada_used, brow_landed, chunk_summed, chunk_stored = (sem("ada_used"), sem("brow_landed"), sem("chunk_summed"),
                                                          sem("chunk_stored"))
        col_landed = [sem(f"col_landed{n}") for n in range(RING)]
        col_summed, col_added = sem("col_summed"), sem("col_added")
        rows_read, rows_turned = sem("rows_read"), sem("rows_turned")
        col_used, bias_landed, bias_ready = sem("col_used"), sem("bias_landed"), sem("bias_ready")
        ps_free = [sem("psA_free"), sem("psB_free")]
        T_full, T_hi, T_free = sem("T_full"), sem("T_hi"), sem("T_free")
        rope_ready, rows_landed, row_used = sem("rope_ready"), [sem("rows_landed0"), sem("rows_landed1")], sem("row_used")
        glub_landed, sigmoid_done = sem("glub_landed"), sem("sigmoid_done")
        xn_ready, scale_ready, h_hi, h_ready = sem("xn_ready"), sem("scale_ready"), sem("h_hi"), sem("h_ready")
        var_ready, std_ready = sem("var_ready"), sem("std_ready")
        gained = sem("gained")
        dve = sem("dve")
        const_ready, constants = sem("const_ready"), sem("constants")
        x_landed, in_landed, b_landed, cm_landed = sem("x_landed"), sem("in_landed"), sem("b_landed"), sem("cm_landed")
        pe_prep, act_prep, dve_prep = sem("pe_prep"), sem("act_prep"), sem("dve_prep")
        uT_ready, uc_ready, bu_full, bu_read = sem("uT_ready"), sem("uc_ready"), sem("bu_full"), sem("bu_read")
        rec, states_ready, y_full, y_ready, g_ready, g_hi, s5_done = (
            sem("rec"), sem("states_ready"), sem("y_full"), sem("y_ready"), sem("g_ready"), sem("g_hi"), sem("s5_done"))
        idx_full, idx_relu, idx_read, sel_ready = sem("idx_full"), sem("idx_relu"), sem("idx_read"), sem("sel_ready")
        lg_full, lg_ready, exp_done, p_ready, pT_full, pT_ready, o_full, o_hi, o_ready = (
            sem("lg_full"), sem("lg_ready"), sem("exp_done"), sem("p_ready"), sem("pT_full"), sem("pT_ready"),
            sem("o_full"), sem("o_hi"), sem("o_ready"))
        out_ready, out_landed = sem("out_ready"), sem("out_landed")

        class Run:
            def __init__(self, kind, n, w, col, row=0, units=KT // UK, layer=0, part=0, ada=(), before=None):
                self.kind, self.n, self.w, self.row, self.units = kind, n, w, row, units
                self.col = col
                self.step = 2 * NB if col[1] - col[0] == NB else NB
                self.layer, self.part, self.before = layer, part, before
                self.ada = list(ada)
                self.blocks = 1 if kind == "ki" else 2
                self.per = self.blocks * units
                self.width = IDX_HEADS + IDX_DIM if kind == "ki" else NB

        s5_in = Run("u", 2, s5_in_w[0], (0, NB), ada=[(0, 2, 0)], before="x")
        glu = Run("glu", 4, s5_glu_w[0], (D, 0), ada=[(0, 2, 2), (2, 4, 4)], before="s5")
        runs = [s5_in, glu]
        parts = [4, 4, 3]
        for layer in range(DEPTH):
            if layer == 1:
                runs += [Run("rope", 4, dsa_in_w[0], (0, NB), layer=1, ada=[(0, 4, 21)], before="ln"),
                         Run("v", 2, dsa_in_w[0], (2 * D, 2 * D + NB), layer=1, ada=[(0, 2, 25)]),
                         Run("idx", 1, dsa_in_w[0], (3 * D, 3 * D + NB), layer=1, ada=[(0, 1, 27)]),
                         Run("ki", 1, dsa_in_w[0], (3 * D + IDX_HEADS * IDX_DIM, 0), layer=1),
                         Run("z", 2, dsa_out_w[0], (0, NB), layer=1, part=2, before="attention")]
            done = 0
            for part, n in enumerate(parts):
                ada = [[[(0, 2, 6), (2, 4, 8)], [(0, 4, 12)], [(0, 2, 18), (2, 3, 20)]], [[(0, 4, 28)], [], []]][layer][part]
                z_ada = [[[(0, 2, 10)], [(0, 2, 16)], []], [[], [], []]][layer][part]
                runs += [Run("ff", n, ffn_w_in[layer], (done * NB, D_FF + done * NB), layer=layer, part=part, ada=ada,
                             before="ln" if part == 0 else None),
                         Run("z", 2, ffn_w_out[layer], (0, NB), row=done * NB, units=2 * n, layer=layer, part=part,
                             ada=z_ada)]
                done += n
        attn_out_chunks = 7 * G
        assert SEQ // TC == STAGE
        attn_out = next(r for r in runs if r.before == "attention")
        unit = turn = hs = aT_parts = norms = 0
        roped = 1
        use = [0, 0]
        for r in runs:
            r.h0 = hs
            r.norm = norms
            if r.before in ("x", "ln"):
                r.hturn = turn
                turn += 4
                hs += 4
                norms += r.before == "ln"
            r.unit, r.turn, r.use, r.roped, r.aT0 = unit, turn, list(use), roped, aT_parts
            unit += r.per * r.n
            r.turns = {"u": 2, "rope": 2, "idx": 2, "ff": 1, "ki": 1}.get(r.kind, 0)
            turn += r.turns * r.n
            use[0] += r.n
            use[1] += r.n if r.blocks == 2 else 0
            roped += r.n * r.blocks if r.kind in ("rope", "idx", "ki") else 0
            aT_parts += r.n if r.kind == "ff" else 0
        runs[-1].final = True
        UNITS, TURNS, NORMS = unit, turn, norms
        AHEAD = RING - 1

        def iterations(eng, r):
            cuts = sorted({0, 1, r.n} | {a for a, b, q in r.ada} | {b for a, b, q in r.ada})
            for lo, hi in zip(cuts[:-1], cuts[1:]):
                q = next((q + lo - a for a, b, q in r.ada if a <= lo < b), None)
                if hi - lo == 1 or r is runs[0] or r is runs[-1]:
                    for i in range(lo, hi):
                        yield i, (None if q is None else q + i - lo), q
                else:
                    with eng.Fori(lo, hi) as i:
                        yield i, (None if q is None else i + (q - lo)), q

        def streamed(q_first):
            return next(e for e in reversed(STREAM) if e[0] <= q_first)

        def not_gates(q_first):
            return sum(streamed(q)[3] is None for q in range(q_first))

        def ada_at(n, per):
            return [k for k in range(AU) if 1 + k * (per - 5) // AU == n]

        def column_source(m):
            return m // (2 * STAGE), m // STAGE % 2 * 3 * D - m // STAGE * STAGE * CW

        def by_pe(m, k):
            return m < SHARED and k % RING == RING - 1

        def col_before(m, k):
            pe_units = sum(by_pe(n // AU, n % AU) for n in range(m * AU + k))
            return pe_units, m * AU + k - pe_units

        def closing(r, i):
            if not (isinstance(i, int) and i == 0):
                return r, i - 1
            before = runs.index(r) - 1
            return None if r.before or before < 0 else (runs[before], runs[before].n - 1)

        def closes(r):
            return r is runs[-1] or bool(runs[runs.index(r) + 1].before)

        def product(r, i, s):
            return r.unit + i * r.per + (s + 1) * r.units

        def cols(i, s):
            return ds(i * (2 * NB) + s * NB, NB)

        block = ctx.enter_context(nc.Block())

        @block.sync
        def _(sp):
            sp.dma_start(cst[:], consts).then_inc(in_landed, 16)
            sp.dma_start(cdn[0:KT], c.rearrange("b (t p) -> (b t) p", p=P)).then_inc(in_landed, 16)
            sp.dma_start(cdn[KT:2 * KT], s5_d.rearrange("b (t p) -> (b t) p", p=P)).then_inc(in_landed, 16)
            sp.dma_start(parn[0:64], ln_g.rearrange("i j (t p) -> (i j t) p", p=P)).then_inc(in_landed, 16)
            sp.dma_start(parn[64:128], ln_b.rearrange("i j (t p) -> (i j t) p", p=P)).then_inc(in_landed, 16)
            sp.dma_start(a_re[:], s5_a_re[0]).then_inc(in_landed, 16)
            sp.dma_start(a_im[:], s5_a_im[0]).then_inc(in_landed, 16)
            sp.dma_start(ldt[:], s5_log_dt[0].rearrange("(g o) -> g o", o=1)).then_inc(in_landed, 16)
            for row, c0 in ((0, 0), (32, 3 * D)):
                for layer in range(DEPTH):
                    sp.dma_start(biasn[64 * layer + row:64 * layer + row + 32],
                                 ada_b[layer, c0:c0 + 2 * D].rearrange("(a p) -> a p", p=P)).then_inc(bias_landed, 16)
            sp.dma_start(pos_i[:], positions.rearrange("b (a p) -> p (b a)", p=P), allow_slow_non_contiguous=True).then_inc(in_landed, 16)

            def column(first, i, step):
                at_ = first + i * step
                return at_ if isinstance(at_, int) else sp.snap(at_)

            def ada_unit(first, k, layer, col):
                if not (isinstance(first, int) and first + k < ARING):
                    sp.wait_ge(ada_used, first + (k - ARING + 1))
                sp.dma_start(ada_raw[:, k % ARING], ada_w[layer, k * P:(k + 1) * P, ds(col, AW)]
                             ).then_inc(ada_landed[k % ARING], 16)

            def col_unit(ring, k, layer, col):
                sp.dma_start(col_raw[ring][:, k % RING], ada_w[layer, k * P:(k + 1) * P, ds(col, CW)]
                             ).then_inc(col_landed[k % RING], 16)

            def first_col_unit(m, k):
                if m * AU + k >= RING:
                    last = divmod(m * AU + k - RING, AU)
                    if by_pe(*last):
                        sp.wait_ge(col_used, col_before(*last)[0] + 1)
                    else:
                        sp.wait_ge(col_summed, col_before(*last)[1] + 1)
                col_unit(0, k, 0, m * CW)

            def w_unit(r, n, s, k, col):
                row = r.row + k * UK * P
                sp.dma_start(w_raw[:, n % RING, :, 0:r.width],
                             r.w[row:row + UK * P, ds(col, r.width)].rearrange("(k p) n -> p k n", p=P)
                             ).then_inc(w_landed[n % RING], 16)

            for k in range(AU):
                first_col_unit(0, k)
                if k == 3:
                    sp.dma_start(Bnat[0][:], s5_b_re[0]).then_inc(b_landed, 16)
                    sp.dma_start(Bnat[1][:], s5_b_im[0]).then_inc(b_landed, 16)
                if k == 5:
                    for ri, src in ((0, s5_c_re), (1, s5_c_im)):
                        sp.dma_start(Cnat[ri][:], src[0].rearrange("(t g) q n -> (g q) t n", g=8)).then_inc(cm_landed, 16)
            for k in range(AU):
                first_col_unit(1, k)
            sp.dma_start(xz[:], x.rearrange("b (a p) d -> p (b a) d", p=P)).then_inc(x_landed, 16)
            for n in range(RING):
                w_unit(runs[0], n, 0, n, 0)
            for m in range(2, STAGE):
                for k in range(AU):
                    first_col_unit(m, k)
            for r in runs:
                if r is runs[0]:
                    sp.wait_ge(col_used, COL_PE)
                    sp.wait_ge(col_summed, COL_DVE)
                if r is glu:
                    sp.wait_ge(w_lo_ready, glu.unit)
                    layer, c0 = column_source(STAGE)
                    with sp.Fori(STAGE, 2 * STAGE) as m:
                        col, used = column(c0, m, CW), column(COL_PE - STAGE * AU, m, AU)
                        for k in range(AU):
                            sp.wait_ge(col_used, used + (k - RING + 1))
                            col_unit(1, k, layer, col)
                for i, q, q_first in iterations(sp, r):
                    col = [column(r.col[s], i, r.step) for s in range(r.blocks)]
                    u = column(r.unit, i, r.per)
                    if q is not None:
                        chunk0, layer, c0, _, _ = streamed(q_first)
                        c0 -= chunk0 * AW
                        ada_col, ada_first = column(c0, q, AW), column(0, q, AU)
                    for n in range(r.per):
                        s, k = divmod(n, r.units)
                        first = isinstance(i, int) and i == 0 and n < RING
                        early = r is glu and n == r.units - 1
                        if first and r is glu:
                            sp.wait_ge(col_used, COL_PE + STAGE * AU + (n - RING + 1))
                        elif not (first and r is runs[0]) and not (r is glu and n == r.units):
                            sp.wait_ge(w_lo_ready, u + (n - RING + 1 + early))
                        if not (first and r is runs[0]):
                            w_unit(r, n, s, k, col[s])
                        if q is not None:
                            if r is glu and n == 1:
                                sp.wait_ge(s5_done, SEQ // TC)
                            for k in ada_at(n, r.per):
                                ada_unit(ada_first, k, layer, ada_col)
            for chunk in range(4):
                sp.wait_ge(out_ready, chunk + 1)
                sp.dma_start(out.rearrange("b (a p) d -> p (b a) d", p=P)[:, :, chunk * NB:(chunk + 1) * NB],
                             xz[:, :, chunk * NB:(chunk + 1) * NB]).then_inc(out_landed, 16)
            sp.wait_ge(out_landed, 64)

        @block.gpsimd
        def _(pool):
            nc.gpsimd.memset(ident[:], 0.0).then_inc(const_ready, 1)
            nc.gpsimd.memset(ones[:], 1.0).then_inc(constants, 1)
            pool.wait_ge(const_ready, 1)
            nc.gpsimd.affine_select(out=ident[:], in_=ident[:], compare_op=ALU.not_equal, fill=1.0, base=0,
                                    pattern=[[-1, P]], channel_multiplier=1).then_inc(constants, 1)
            for ri in range(2):
                nc.gpsimd.memset(Bdiag[ri][:], 0.0).then_inc(constants, 1)
            nc.gpsimd.memset(carry[:], 0.0).then_inc(constants, 1)
            nc.gpsimd.memset(uc[:], 0.0).then_inc(constants, 1)

            def load_brow(q, q_first):
                chunk0, layer, c0, gate, _ = streamed(q_first)
                if gate is None:
                    return
                if not (isinstance(q, int) and q == 0):
                    pool.wait_ge(chunk_stored, q)
                pool.dma_start(brow[:], ada_b[layer:layer + 1, ds(q * AW + (c0 - chunk0 * AW), AW)].to_broadcast([P, AW])
                               ).then_inc(brow_landed, 16)

            def load_rows(norm, chunk):
                if norm == NORMS and chunk >= 2:
                    pool.wait_ge(out_ready, chunk - 1)
                elif 4 * norm + chunk >= 2:
                    pool.wait_ge(row_used, 4 * norm + chunk - 1)
                for which, src in ((0, ln_g), (1, ln_b)):
                    pool.dma_start(lnrow[:, chunk % 2, which],
                                   src[norm // 2, norm % 2:norm % 2 + 1, chunk * NB:(chunk + 1) * NB].to_broadcast([P, NB])
                                   ).then_inc(rows_landed[chunk % 2], 16)

            for r in runs:
                if r.before == "ln":
                    if r.norm == 0:
                        pool.wait_ge(ps_free[1], glu.use[1] + glu.n)
                    if r.norm == 2:
                        pool.wait_ge(idx_full, TOK * IDX_HEADS)
                    for chunk in range(4):
                        load_rows(r.norm, chunk)
                if r is glu:
                    pool.wait_ge(s5_done, SEQ // TC)
                if r is attn_out:
                    pool.wait_ge(w_used, r.unit)
                    nc.gpsimd.memset(causal[:], 1.0).then_inc(const_ready, 1)
                    pool.wait_ge(const_ready, 2)
                    nc.gpsimd.affine_select(out=causal[:], in_=causal[:], compare_op=ALU.is_ge, fill=0.0, base=0,
                                            pattern=[[P, TOK], [-1, SEQ]], channel_multiplier=1).then_inc(constants, 1)
                if not r.ada and r.kind != "glu":
                    continue
                if r is s5_in:
                    pool.wait_ge(col_added, STAGE)
                for i, q, q_first in iterations(pool, r):
                    if r.kind == "glu":
                        pool.wait_ge(ps_free[1], r.use[1] + i)
                        for which, c0 in ((0, D), (1, 0)):
                            pool.dma_start(glub[:, which], s5_glu_b[0:1, ds(i * NB + c0, NB)].to_broadcast([P, NB])).then_inc(glub_landed, 16)
                    if q is not None:
                        load_brow(q, q_first)
            for chunk in range(4):
                load_rows(NORMS, chunk)

        @block.scalar
        def _(act):
            def hi_unit(u, n):
                act.wait_ge(w_landed[n % RING], u * (16 // RING) + (n // RING + 1) * 16)
                if not (isinstance(u, int) and u + n < RING):
                    act.wait_ge(w_used, u + (n - RING + 1))
                nc.scalar.activation(w_hi[:, n % RING], w_raw[:, n % RING], ACT.Copy).then_inc(w_hi_ready, 1)

            act.wait_ge(in_landed, 16 * 9)
            nc.scalar.activation(dt[:], ldt[:], ACT.Exp).then_inc(act_prep, 1)
            act.wait_ge(dve_prep, 1)
            nc.scalar.activation(mag[:], decay[:], ACT.Exp).then_inc(act_prep, 1)
            act.wait_ge(pe_prep, 1)
            nc.scalar.activation(csil[:], M[:, 0, 0:KT], ACT.Silu).then_inc(act_prep, 1)
            nc.scalar.activation(dcol[:], M[:, 0, KT:2 * KT], ACT.Copy)
            nc.scalar.activation(modcol[:], M[:, 0, 2 * P:3 * P], ACT.Copy).then_inc(bias_ready, 1)
            nc.scalar.activation(parT[:], M[:, 0, P:2 * P], ACT.Copy).then_inc(act_prep, 1)
            act.wait_ge(dve_prep, 2)
            nc.scalar.activation(sinv[:], turns[:], ACT.Sin)
            nc.scalar.activation(cosv[:], quarter[:], ACT.Sin).then_inc(act_prep, 1)
            for n in range(16):
                act.wait_ge(pe_prep, 12 + n)
                tab = (Btab if n < 8 else Ctab)[n % 8 // 4]
                j = n % 4
                nc.scalar.activation(tab[:, 4 * j:4 * j + 4, :], PS[n % 2][:, n // 2 % 2].rearrange("p (j m) -> p j m", m=P),
                                     ACT.Copy).then_inc(act_prep, 1)

            def make_h(r):
                act.wait_ge(scale_ready, r.h0 // 4 + 1)
                for g in range(4):
                    act.wait_ge(T_full, r.hturn + g + 1)
                    if g >= 2:
                        act.wait_ge(h_ready, r.h0 + g - 1)
                    h32 = stg[g % 2][:].rearrange("p a (b t) -> p (a b) t", t=SEQ)
                    for j in range(4):
                        k = 4 * g + j
                        ins = nc.scalar.activation(h32[:, j], T[:].rearrange("p a (b t) -> p (a b) t", t=SEQ)[:, j],
                                                   ACT.Identity, scale=scol[:, k:k + 1], bias=bcol[:, k:k + 1])
                    ins.then_inc(T_free, 1)
                    act.wait_ge(T_free, r.hturn + g + 1)
                    nc.scalar.activation(hT_hi[:, 4 * g:4 * g + 4], h32, ACT.Copy).then_inc(h_hi, 1)

            def std(norm):
                act.wait_ge(var_ready, norm + 1)
                nc.scalar.activation(rstd[:, :, 1], rstd[:, :, 0], ACT.Sqrt).then_inc(std_ready, 1)

            def read_T(r, i, k, dst, hi=False):
                act.wait_ge(T_full, r.turn + i * r.turns + (k + 1))
                n = dst.shape[1] if len(dst.shape) > 2 else 1
                src = T[:].rearrange("p a (b t) -> p (a b) t", t=SEQ)
                src = src[:, 0:n] if len(dst.shape) > 2 else src[:, 0]
                ins = nc.scalar.activation(dst, src, ACT.Copy)
                ins.then_inc(T_hi if hi else T_free, 1)

            def s5():
                quarters = 4 * (SEQ // TC)

                def fill(n):
                    if n >= 2:
                        act.wait_ge(bu_full, 4 * (n - 1))
                    ch, j4 = divmod(n, 4)
                    for g in range(4):
                        rows = slice(32 * g, 32 * g + 32)
                        ins = nc.scalar.activation(uc[rows, n % 2, :, g], uT[rows, 4 * j4:4 * j4 + 4, ch * TC:(ch + 1) * TC],
                                                   ACT.Copy)
                    ins.then_inc(uc_ready, 1)

                act.wait_ge(T_free, s5_in.turn + 4)
                act.wait_ge(constants, 6)
                fill(0)
                fill(1)
                for ch in range(SEQ // TC):
                    b = ch % 2
                    if ch == 0:
                        act.wait_ge(w_used, glu.unit)
                        act.wait_ge(chunk_stored, 2)
                    if ch >= 2:
                        act.wait_ge(y_full, ch - 1)
                    for f in range(KT):
                        act.wait_ge(bu_full, KT * ch + f + 1)
                        nc.scalar.activation(st[b][:, :, :, 4 * f:4 * f + 4].rearrange("p t r g -> p r g t"),
                                             PS[f % 4 // 2][:, f % 2].rearrange("p (r g t) -> p r g t", r=2, g=4),
                                             ACT.Copy).then_inc(bu_read, 1)
                        if f % 4 == 3 and 4 * ch + f // 4 + 2 < quarters:
                            fill(4 * ch + f // 4 + 2)
                    if ch >= 1:
                        gelu(ch - 1)
                act.wait_ge(col_used, COL_PE + STAGE * AU)
                act.wait_ge(y_full, SEQ // TC - 1)
                for c in range(STAGE):
                    row = slice(32 * c, 32 * c + 1)
                    ins = nc.scalar.activation(col_row[row, :], M[row].rearrange("p a n -> p (a n)"), ACT.Copy)
                ins.then_inc(rows_read, 1)
                gelu(SEQ // TC - 1)

            def gelu(ch):
                act.wait_ge(y_ready, ch + 1)
                if ch >= 1:
                    act.wait_ge(s5_done, ch)
                nc.scalar.activation(y_act[:], y_in[:], ACT.Gelu_apprx_tanh).then_inc(g_ready, 1)
                act.wait_ge(g_ready, ch + 1)
                nc.scalar.activation(hT_hi[:, :, ch * TC:(ch + 1) * TC], y_act[:], ACT.Copy).then_inc(g_hi, 1)

            def attention():
                n = 0
                for t in range(TOK):
                    for h in range(IDX_HEADS):
                        act.wait_ge(idx_full, n + 1)
                        if n >= 2:
                            act.wait_ge(idx_read, n - 1)
                        else:
                            act.wait_ge(w_used, attn_out.unit)
                        nc.scalar.activation(relu[:, n % 2, 0:(t + 1) * P], PS[h % 2][:, h // 2 % 2, 0:(t + 1) * P],
                                             ACT.Relu, scale=IDX_DIM ** -0.5).then_inc(idx_relu, 1)
                        n += 1
                for a in range(TOK * HEADS + 2):
                    if a < TOK * HEADS:
                        N = (a // HEADS + 1) * P
                        act.wait_ge(lg_ready, a + 1)
                        if a >= 2:
                            act.wait_ge(pT_full, a - 1)
                        nc.scalar.activation(prob[:, a % 2, 0:N], logit[:, a % 2, 0:N], ACT.Exp, bias=soft[:, a % 4, 1:2],
                                             accum_out=soft[:, a % 4, 2:3]).then_inc(exp_done, 1)
                    if 1 <= a <= TOK * HEADS:
                        b = a - 1
                        N = (b // HEADS + 1) * P
                        act.wait_ge(pT_full, b + 1)
                        nc.scalar.activation(probT[:, b % 2, 0:N], T[:, b % 2, 0:N], ACT.Copy).then_inc(pT_ready, 1)
                    if a >= 5 and a % 4 == 1:
                        g = a // 4 - 1
                        t, h = divmod(4 * g, HEADS)
                        act.wait_ge(o_full, g + 1)
                        nc.scalar.activation(hT_hi[:, h:h + 4, t * P:(t + 1) * P],
                                             M[:, g % 2].rearrange("p (h t) -> p h t", t=P), ACT.Copy).then_inc(o_hi, 1)

            def finish(r, i, s):
                if r.kind in ("u", "v") or (r.kind == "ff" and s == 0):
                    act.wait_ge(w_used, product(r, i, s))
                if r.kind == "u":
                    nc.scalar.activation(stg[s][:], PS[s][:], ACT.Copy).then_inc(ps_free[s], 1)
                if r.kind == "ff" and s == 0:
                    act.wait_ge(ps_free[1], r.use[1] + i)
                    nc.scalar.activation(stg[0][:], PS[0][:], ACT.Silu).then_inc(ps_free[0], 1)
                if r.kind == "glu" and s == 0:
                    act.wait_ge(ps_free[0], r.use[0] + i + 1)
                    nc.scalar.activation(stg[0][:], stg[0][:], ACT.Sigmoid).then_inc(sigmoid_done, 1)
                if r.kind == "v":
                    nc.scalar.activation(v[:, :, cols(i, s)], PS[s][:], ACT.Copy).then_inc(ps_free[s], 1)

            def turned(r, i, s):
                if r.kind == "u":
                    read_T(r, i, s, uT[:, ds(i * 8 + s * 4, 4)])
                if r.kind == "rope":
                    read_T(r, i, s, qkT[:, ds(i * 8 + s * 4, 4)])
                if r.kind == "idx":
                    if s == 0:
                        act.wait_ge(row_used, 4 * (NORMS - 1))
                    read_T(r, i, s, qiT[:, 4 * s:4 * s + 4])
                if r.kind == "ff" and s == 1:
                    read_T(r, i, 0, aT_hi[:, ds(i * 4, 4)], hi=True)
                if r.kind == "ki" and s == 0:
                    read_T(r, i, 0, kiT[:])

            for r in runs:
                if r.before == "ln":
                    std(r.norm)
                if r.before == "s5":
                    s5()
                    act.wait_ge(y_full, SEQ // TC)
                    act.wait_ge(g_hi, SEQ // TC)
                elif r.before == "attention":
                    attention()
                if r is runs[0]:
                    act.wait_ge(dve_prep, 4)
                if r is runs[0] or r is glu:
                    for n in range(AHEAD):
                        hi_unit(r.unit, n)
                if r.before in ("x", "ln"):
                    make_h(r)
                for i, q, q_first in iterations(act, r):
                    u = r.unit + i * r.per
                    stop = isinstance(i, int) and i == r.n - 1 and (r is runs[0] or r is runs[-1])
                    last = closing(r, i)
                    for n in range(r.per):
                        if n == 0 and last:
                            finish(*last, last[0].blocks - 1)
                        if r.blocks == 2 and n == r.units:
                            finish(r, i, 0)
                        if not (stop and n + AHEAD >= r.per):
                            hi_unit(u, n + AHEAD)
                        if n == 3 and last:
                            turned(*last, last[0].blocks - 1)
                        if r.blocks == 2 and n == r.units + 3:
                            turned(r, i, 0)
                if closes(r):
                    finish(r, r.n - 1, r.blocks - 1)
                    turned(r, r.n - 1, r.blocks - 1)
            std(NORMS)

        @block.vector
        def _(vec):
            V = nc.vector
            chain = [0]

            def link(ins):
                chain[0] += 1
                ins.then_inc(dve, 1)
                vec.wait_ge(dve, chain[0])

            def lo_unit(u, n):
                vec.wait_ge(w_hi_ready, u + (n + 1))
                V.tensor_tensor(w_lo[:, n % RING], w_raw[:, n % RING], w_hi[:, n % RING].bitcast(F32), ALU.subtract
                                ).then_inc(w_lo_ready, 1)

            def ada_unit(q, k):
                vec.wait_ge(ada_landed[k % ARING], q * (16 * AU // ARING) + 16 * (k // ARING + 1))
                if k == 0:
                    if not (isinstance(q, int) and q == 0):
                        vec.wait_ge(chunk_summed, q)
                    V.tensor_scalar(ada_acc[:], ada_raw[:, 0], csil[:, 0:1], None, ALU.mult).then_inc(ada_used, 1)
                else:
                    vec.wait_ge(ada_used, q * AU + k)
                    V.scalar_tensor_tensor(out=ada_acc[:], in0=ada_raw[:, k % ARING], scalar=csil[:, k:k + 1],
                                           in1=ada_acc[:], op0=ALU.mult, op1=ALU.add).then_inc(ada_used, 1)

            def store_chunk(q, q_first):
                chunk0, _, _, gate, column = streamed(q_first)
                vec.wait_ge(chunk_summed, q + 1)
                if gate is not None:
                    vec.wait_ge(brow_landed, (q - not_gates(q_first) + 1) * 16)
                    V.scalar_tensor_tensor(out=grow[:, ds((q - chunk0) * AW + gate * D, AW)], in0=M[:, 1], scalar=1.0,
                                           in1=brow[:], op0=ALU.add, op1=ALU.add).then_inc(chunk_stored, 1)
                else:
                    c = ds((q - chunk0) * (AW // P) + column, AW // P)
                    V.tensor_tensor(modcol[:, c], modcol[:, c], M[:, 1, 0:AW // P], ALU.add).then_inc(chunk_stored, 1)

            def col_unit(m, k):
                n = col_before(m, k)[1]
                acc = col_acc[m % 2]
                vec.wait_ge(col_landed[k % RING], (m * LAPS + k // RING + 1) * 16)
                if k == 0:
                    if m >= 2:
                        vec.wait_ge(col_added, m - 1)
                    V.tensor_scalar(acc[:], col_raw[0][:, 0], csil[:, 0:1], None, ALU.mult).then_inc(col_summed, 1)
                else:
                    vec.wait_ge(col_summed, n)
                    V.scalar_tensor_tensor(out=acc[:], in0=col_raw[0][:, k % RING], scalar=csil[:, k:k + 1],
                                           in1=acc[:], op0=ALU.mult, op1=ALU.add).then_inc(col_summed, 1)

            def col_units(m, first, end):
                for k in range(first, end):
                    if not by_pe(m, k):
                        col_unit(m, k)

            def store_columns():
                vec.wait_ge(col_added, STAGE)
                c = slice(0, STAGE * (CW // P))
                link(V.tensor_copy(modcol[:, c], M[:, 0, c]))

            vec.sem_inc(rope_ready, 1)
            vec.wait_ge(in_landed, 16 * 9)
            vec.wait_ge(act_prep, 1)
            V.tensor_copy(pos_f[:], pos_i[:])
            link(V.tensor_scalar(ang[:, 192:256], a_im[:], dt[:], None, ALU.mult))
            V.tensor_scalar(decay[:], a_re[:], dt[:], None, ALU.mult).then_inc(dve_prep, 1)
            for t in range(TOK):
                V.tensor_scalar(ang[:, t * 64:t * 64 + 64], cst[:, 0:64], pos_f[:, t:t + 1], None, ALU.mult)
                ins = V.tensor_scalar(ang[:, 128 + t * 32:160 + t * 32], cst[:, 64:96], pos_f[:, t:t + 1], None, ALU.mult)
            link(ins)
            link(V.tensor_scalar(turns[:], ang[:], 1.0 / TWO_PI, None, ALU.mult))
            link(V.tensor_scalar(turns[:], turns[:], ROUND, None, ALU.add))
            link(V.tensor_scalar(turns[:], turns[:], -ROUND, None, ALU.add))
            for part in (C1, C2, C3):
                link(V.scalar_tensor_tensor(out=ang[:], in0=turns[:], scalar=-part, in1=ang[:], op0=ALU.mult, op1=ALU.add))
            LIM = 3.1415925
            link(V.tensor_scalar(turns[:], ang[:], LIM, -LIM, ALU.min, ALU.max))
            link(V.tensor_scalar(ang[:], turns[:], TWO_PI / 4, None, ALU.add))
            link(V.tensor_scalar(quarter[:], ang[:], LIM, -TWO_PI, ALU.is_gt, ALU.mult))
            link(V.tensor_tensor(quarter[:], quarter[:], ang[:], ALU.add))
            V.tensor_scalar(quarter[:], quarter[:], LIM, -LIM, ALU.min, ALU.max).then_inc(dve_prep, 1)
            vec.wait_ge(act_prep, 3)
            col_units(0, 0, 4)
            vec.wait_ge(act_prep, 5)
            V.tensor_copy(sin_t[:], sinv[:, 0:192])
            V.tensor_copy(cos_t[:], cosv[:, 0:192])
            V.tensor_tensor(lam[0][:], mag[:], cosv[:, 192:256], ALU.mult)
            link(V.tensor_tensor(lam[1][:], mag[:], sinv[:, 192:256], ALU.mult))
            V.tensor_scalar(num[:], lam[0][:], -1.0, None, ALU.add)
            V.tensor_tensor(q0[:], a_re[:], a_re[:], ALU.mult)
            link(V.tensor_tensor(q1[:], a_im[:], a_im[:], ALU.mult))
            link(V.tensor_tensor(den[:], q0[:], q1[:], ALU.add))
            link(V.reciprocal(den[:], den[:]))
            V.tensor_tensor(q0[:], num[:], a_re[:], ALU.mult)
            link(V.tensor_tensor(q1[:], lam[1][:], a_im[:], ALU.mult))
            link(V.tensor_tensor(q0[:], q0[:], q1[:], ALU.add))
            link(V.tensor_tensor(coef[0][:], q0[:], den[:], ALU.mult))
            V.tensor_tensor(q0[:], lam[1][:], a_re[:], ALU.mult)
            link(V.tensor_tensor(q1[:], num[:], a_im[:], ALU.mult))
            link(V.tensor_tensor(q0[:], q0[:], q1[:], ALU.subtract))
            link(V.tensor_tensor(coef[1][:], q0[:], den[:], ALU.mult))
            col_units(0, 4, 8)
            vec.wait_ge(b_landed, 32)
            wide = [coef[ri][:].unsqueeze(2).to_broadcast([P, STATE, GSIZE]) for ri in range(2)]
            V.tensor_tensor(Btmp[0][:], Bnat[0][:], wide[0], ALU.mult)
            link(V.tensor_tensor(Btmp[1][:], Bnat[1][:], wide[1], ALU.mult))
            for par in range(2):
                ins = V.tensor_tensor(Bbar[0][:, :, par].rearrange("p k n -> p n k"), Btmp[0][:], Btmp[1][:], ALU.subtract)
            link(ins)
            V.tensor_tensor(Btmp[0][:], Bnat[1][:], wide[0], ALU.mult)
            link(V.tensor_tensor(Btmp[1][:], Bnat[0][:], wide[1], ALU.mult))
            for ri in range(2):
                for par in range(2):
                    V.tensor_copy(lam_twice[ri][:, par], lam[ri][:])
            for par in range(2):
                ins = V.tensor_tensor(Bbar[1][:, :, par].rearrange("p k n -> p n k"), Btmp[0][:], Btmp[1][:], ALU.add)
            ins.then_inc(dve_prep, 1)
            col_units(0, 8, 12)
            vec.wait_ge(cm_landed, 32)
            for ri in range(2):
                for par in range(2):
                    ins = V.tensor_scalar(Cmask[ri][:, :, par, :], Cnat[ri][:], cst[:, 96 + par:97 + par],
                                          1.0 if ri == 0 else -1.0, ALU.mult, ALU.mult)
            ins.then_inc(dve_prep, 1)
            col_units(0, 12, AU)
            vec.wait_ge(constants, 6)
            vec.wait_ge(pe_prep, 3)
            for par in range(2):
                rows = slice(64 * par, 64 * par + 64)
                for row, col, ri, sign in ((0, 0, 0, 1.0), (0, 1, 1, -1.0), (1, 0, 1, 1.0), (1, 1, 0, 1.0)):
                    ins = V.tensor_scalar(lam4[rows, row, col, :], M[rows, 1, ri * P + par:ri * P + P:2], sign, None, ALU.mult)
            ins.then_inc(dve_prep, 1)
            for n in range(8):
                vec.wait_ge(pe_prep, 3 + n + 1)
                ri, p4 = divmod(n, 4)
                bank = PS[n % 2][:, n // 2 % 2].rearrange("p (k g o) -> p k g o", k=4, o=2)
                for par in range(2):
                    rows = slice(64 * par, 64 * par + 64)
                    ins = V.tensor_copy(Bdiag[ri][rows, :, par, 4 * p4:4 * p4 + 4].rearrange("p g k -> p k g"),
                                        bank[rows, :, :, par])
                ins.then_inc(dve_prep, 1)
                if n % 2:
                    col_units(1, 4 * (n // 2), 4 * (n // 2) + 4)
            for m in range(2, STAGE):
                col_units(m, 0, AU)
            store_columns()

            def make_scale(r):
                at_ = (2 * r.layer + (r.kind == "ff")) * 2 * KT
                shift, scale = modcol[:, at_:at_ + KT], modcol[:, at_ + KT:at_ + 2 * KT]
                if r.before == "x":
                    V.tensor_scalar(scol[:], scale, 1.0, None, ALU.add)
                    V.tensor_copy(bcol[:], shift).then_inc(scale_ready, 1)
                else:
                    gain, bias = parT[:, r.norm * KT:r.norm * KT + KT], parT[:, 64 + r.norm * KT:64 + r.norm * KT + KT]
                    V.scalar_tensor_tensor(out=scol[:], in0=scale, scalar=1.0, in1=gain, op0=ALU.add, op1=ALU.mult)
                    link(V.scalar_tensor_tensor(out=bcol[:], in0=scale, scalar=1.0, in1=bias, op0=ALU.add, op1=ALU.mult))
                    V.tensor_tensor(bcol[:], bcol[:], shift, ALU.add).then_inc(scale_ready, 1)

            def moments(norm):
                for t in range(TOK):
                    ins = V.bn_aggr(mv[:, t], stats[:, t])
                link(ins)
                V.tensor_scalar(rstd[:, :, 0], mv[:, :, 1], LN_EPS, None, ALU.add).then_inc(var_ready, 1)
                vec.wait_ge(std_ready, norm + 1)
                link(V.reciprocal(rstd[:, :, 1], rstd[:, :, 1]))

            def normalise(g):
                for t in range(TOK):
                    ins = V.tensor_scalar(xz[:, t, g * NB:(g + 1) * NB], xz[:, t, g * NB:(g + 1) * NB], mv[:, t, 0:1],
                                          rstd[:, t, 1:2], ALU.subtract, ALU.mult)
                return ins

            def make_h(r):
                if r.before == "ln":
                    moments(r.norm)
                make_scale(r)
                for g in range(5):
                    if g < 4 and r.before == "ln":
                        normalise(g).then_inc(xn_ready, 1)
                    if g >= 1:
                        vec.wait_ge(h_hi, r.h0 + g)
                        V.tensor_tensor(hT_lo[:, 4 * g - 4:4 * g].rearrange("p a t -> p (a t)"),
                                        stg[(g - 1) % 2][:].rearrange("p a t -> p (a t)"),
                                        hT_hi[:, 4 * g - 4:4 * g].rearrange("p a t -> p (a t)").bitcast(F32), ALU.subtract
                                        ).then_inc(h_ready, 1)

            def affine(norm, chunk, scale, last=None):
                vec.wait_ge(rows_landed[chunk % 2], 32 * (2 * norm + chunk // 2 + 1))
                part = xz[:, :, chunk * NB:(chunk + 1) * NB]
                gain, bias = (lnrow[:, chunk % 2, w].unsqueeze(1).to_broadcast([P, TOK, NB]) for w in range(2))
                V.scalar_tensor_tensor(out=part, in0=part, scalar=scale, in1=gain, op0=ALU.mult, op1=ALU.mult
                                       ).then_inc(gained, 1)
                vec.wait_ge(gained, 4 * norm + chunk + 1)
                V.scalar_tensor_tensor(out=part, in0=bias, scalar=scale, in1=part, op0=ALU.mult, op1=ALU.add
                                       ).then_inc(row_used if last is None else last, 1)

            def s5():
                n = 0

                def post(ch):
                    vec.wait_ge(y_full, ch + 1)
                    if ch >= 1:
                        vec.wait_ge(g_ready, ch)
                    link(V.tensor_tensor(y_in[:], uT[:, :, ch * TC:(ch + 1) * TC], dcol[:].unsqueeze(2).to_broadcast([P, KT, TC]), ALU.mult))
                    V.tensor_tensor(y_in[:].rearrange("p k t -> p (k t)"), y_in[:].rearrange("p k t -> p (k t)"),
                                    T[:].rearrange("p a n -> p (a n)"), ALU.add).then_inc(y_ready, 1)

                def gelu_lo(ch):
                    vec.wait_ge(g_hi, ch + 1)
                    V.tensor_tensor(hT_lo[:, :, ch * TC:(ch + 1) * TC], y_act[:],
                                    hT_hi[:, :, ch * TC:(ch + 1) * TC].bitcast(F32), ALU.subtract).then_inc(s5_done, 1)

                for ch in range(SEQ // TC):
                    b = ch % 2
                    vec.wait_ge(bu_read, KT * (ch + 1))
                    for t in range(TC):
                        for half in range(2):
                            g = slice(32 * half, 32 * half + 32)
                            if n:
                                vec.wait_ge(rec, n - 1 + half)
                            s = carry[:, :, g] if t == 0 else st[b][:, t - 1, :, g]
                            V.tensor_tensor(prod[:, :, :, g], s.unsqueeze(1).to_broadcast([P, 2, 2, 32]), lam4[:, :, :, g],
                                            ALU.mult).then_inc(rec, 1)
                        for half in range(2):
                            g = slice(32 * half, 32 * half + 32)
                            vec.wait_ge(rec, n + 1 + half)
                            V.tensor_tensor(tmp[:, :, g], prod[:, :, 0, g], prod[:, :, 1, g], ALU.add).then_inc(rec, 1)
                        for half in range(2):
                            g = slice(32 * half, 32 * half + 32)
                            vec.wait_ge(rec, n + 3 + half)
                            V.tensor_tensor(st[b][:, t, :, g], tmp[:, :, g], st[b][:, t, :, g], ALU.add).then_inc(rec, 1)
                        n += 6
                        if ch >= 1 and t == 24:
                            post(ch - 1)
                        if ch >= 1 and t == 36:
                            gelu_lo(ch - 1)
                    vec.wait_ge(rec, n)
                    V.tensor_copy(carry[:], st[b][:, TC - 1]).then_inc(states_ready, 1)
                    vec.wait_ge(states_ready, ch + 1)
                post(SEQ // TC - 1)
                vec.wait_ge(rows_turned, 1)
                for s in range(2):
                    c = slice((STAGE + 2 * s) * (CW // P), (STAGE + 2 * s + 2) * (CW // P))
                    part = modcol[:, c].rearrange("p (a b) -> p a b", a=2)
                    ins = V.tensor_tensor(part, part, PS[s][:, :, 0:CW // P], ALU.add)
                link(ins)
                gelu_lo(SEQ // TC - 1)

            def rope(r, i, s, heads, half, table):
                vec.wait_ge(w_used, product(r, i, s))
                vec.wait_ge(T_full, r.turn + i * r.turns + (s - 1 if s else -1) if r.kind != "ki" else r.turn)
                vec.wait_ge(rope_ready, r.roped + i * r.blocks + s)
                c0 = IDX_HEADS if r.kind == "ki" else 0
                wide = heads * 2 * half
                for t in range(TOK):
                    at0 = t * half + (0 if table == "h" else 2 * (HD // 2))
                    shape = [P, heads, 2, half]
                    cosb, sinb = (w[:, at0:at0 + half].unsqueeze(1).unsqueeze(1).to_broadcast(shape) for w in (cos_t, sin_t))
                    src = PS[s][:, t, c0:c0 + wide].rearrange("p (h x d) -> p h x d", x=2, d=half)
                    dst = stg[s][:, t, 0:wide].rearrange("p (h x d) -> p h x d", x=2, d=half)
                    other = rt[:, 0:wide].rearrange("p (h x d) -> p h x d", x=2, d=half)
                    V.tensor_tensor(dst, src, cosb, ALU.mult)
                    link(V.tensor_tensor(other, src, sinb, ALU.mult))
                    if t == TOK - 1 and r.kind != "ki":
                        vec.sem_inc(ps_free[s], 1)
                    V.tensor_tensor(dst[:, :, 0], dst[:, :, 0], other[:, :, 1], ALU.subtract)
                    ins = V.tensor_tensor(dst[:, :, 1], dst[:, :, 1], other[:, :, 0], ALU.add)
                    if t < TOK - 1:
                        link(ins)
                return ins

            def links(r):
                return {"u": (0, 0), "v": (0, 0), "ff": (0, 0), "z": (2, 2) if r.part == 2 else (1, 1), "glu": (1, 3),
                        "rope": (3, 3), "idx": (3, 3), "ki": (0, 4)}[r.kind]

            def attention():
                vec.wait_ge(constants, 7)
                vec.wait_ge(T_full, attn_out.turn)
                link(V.tensor_scalar(off[:], causal[:], -MASKED, MASKED, ALU.mult, ALU.add))
                n = 0
                for t in range(TOK):
                    N = (t + 1) * P
                    for h in range(IDX_HEADS):
                        vec.wait_ge(idx_relu, n + 1)
                        if h == 0:
                            V.tensor_scalar(score[:, 0, 0:N], relu[:, n % 2, 0:N], wic[:, t, 0:1], None, ALU.mult
                                            ).then_inc(idx_read, 1)
                        else:
                            vec.wait_ge(idx_read, n)
                            V.scalar_tensor_tensor(out=score[:, 0, 0:N], in0=relu[:, n % 2, 0:N], scalar=wic[:, t, h:h + 1],
                                                   in1=score[:, 0, 0:N], op0=ALU.mult, op1=ALU.add).then_inc(idx_read, 1)
                        n += 1
                    vec.wait_ge(idx_read, n)
                    link(V.tensor_tensor(score[:, 1, 0:N], score[:, 0, 0:N], causal[:, t, 0:N], ALU.mult))
                    link(V.tensor_tensor(score[:, 0, 0:N], score[:, 1, 0:N], off[:, t, 0:N], ALU.add))
                    for k in range(TOPK // 8):
                        a, b = k % 2, 1 - k % 2
                        link(V.max(best[:], score[:, a, 0:N]))
                        link(V.match_replace(score[:, b, 0:N], best[:], score[:, a, 0:N], TAKEN))
                    a = TOPK // 8 % 2
                    link(V.tensor_scalar(score[:, 1 - a, 0:N], score[:, a, 0:N], (MASKED + TAKEN) / 2, None, ALU.is_le))
                    link(V.tensor_tensor(score[:, a, 0:N], score[:, 1 - a, 0:N], causal[:, t, 0:N], ALU.mult))
                    link(V.tensor_scalar(selb[:, t, 0:N], score[:, a, 0:N], -1.0, UNSEEN, ALU.add, ALU.mult))
                A = TOK * HEADS

                def o_lo(g):
                    t, h = divmod(4 * g, HEADS)
                    vec.wait_ge(o_hi, g + 1)
                    V.tensor_tensor(hT_lo[:, h:h + 4, t * P:(t + 1) * P], M[:, g % 2].rearrange("p (h t) -> p h t", t=P),
                                    hT_hi[:, h:h + 4, t * P:(t + 1) * P].bitcast(F32), ALU.subtract).then_inc(o_ready, 1)

                for a in range(A + 1):
                    if a < A:
                        t = a // HEADS
                        N = (t + 1) * P
                        vec.wait_ge(lg_full, a + 1)
                        if a >= 2:
                            vec.wait_ge(exp_done, a - 1)
                        link(V.scalar_tensor_tensor(out=logit[:, a % 2, 0:N], in0=PS[a % 2][:, a // 2 % 2, 0:N], scalar=HD ** -0.5,
                                                    in1=selb[:, t, 0:N], op0=ALU.mult, op1=ALU.add))
                        link(V.reduce_max(soft[:, a % 4, 0:1], logit[:, a % 2, 0:N], AXX))
                        V.tensor_scalar(soft[:, a % 4, 1:2], soft[:, a % 4, 0:1], -1.0, None, ALU.mult).then_inc(lg_ready, 1)
                    if a >= 1:
                        b = a - 1
                        N = (b // HEADS + 1) * P
                        vec.wait_ge(exp_done, b + 1)
                        link(V.reciprocal(soft[:, b % 4, 3:4], soft[:, b % 4, 2:3]))
                        V.tensor_scalar(prob[:, b % 2, 0:N], prob[:, b % 2, 0:N], soft[:, b % 4, 3:4], None, ALU.mult
                                        ).then_inc(p_ready, 1)
                    if a % 4 == 3 and a >= 7:
                        o_lo(a // 4 - 1)
                o_lo(A // 4 - 1)

            def chain_at(r, i, s):
                chain[0] = r.chain + i * sum(links(r)) + s * links(r)[0]

            def finish(r, i, s):
                full = r.use[s] + i + 1
                if r.kind == "z":
                    vec.wait_ge(w_used, product(r, i, s))
                    c = cols(i, s)
                    gate = 0 if r is attn_out else D
                    g = grow[:, ds(gate + i * (2 * NB) + s * NB, NB)].unsqueeze(1).to_broadcast([P, TOK, NB])
                    V.tensor_tensor(stg[s][:], PS[s][:], g, ALU.mult).then_inc(ps_free[s], 1)
                    vec.wait_ge(ps_free[s], full)
                    link(V.tensor_tensor(xz[:, :, c], xz[:, :, c], stg[s][:], ALU.add))
                    if r.part == 2:
                        for t in range(TOK):
                            ins = V.bn_stats(stats[:, t, ds(i * 2 + s, 1)].rearrange("p a b -> p (a b)"), xz[:, t, c])
                        link(ins)
                if r.kind == "glu":
                    vec.wait_ge(w_used, product(r, i, s))
                    if s == 0:
                        vec.wait_ge(glub_landed, i * 32 + 32)
                    V.tensor_tensor(stg[s][:], PS[s][:], glub[:, s].unsqueeze(1).to_broadcast([P, TOK, NB]), ALU.add
                                    ).then_inc(ps_free[s], 1)
                if r.kind == "glu" and s == 1:
                    vec.wait_ge(ps_free[1], full)
                    link(V.tensor_tensor(stg[1][:], stg[0][:], stg[1][:], ALU.mult))
                    c = ds(i * NB, NB)
                    link(V.tensor_tensor(xz[:, :, c], xz[:, :, c], stg[1][:], ALU.add))
                    for t in range(TOK):
                        ins = V.bn_stats(stats[:, t, ds(i, 1)].rearrange("p a b -> p (a b)"), xz[:, t, c])
                    link(ins)
                if r.kind == "ff" and s == 1:
                    vec.wait_ge(ps_free[0], r.use[0] + i + 1)
                    vec.wait_ge(w_used, product(r, i, 1))
                    V.tensor_tensor(stg[1][:], stg[0][:], PS[1][:], ALU.mult).then_inc(ps_free[1], 1)
                if r.kind in ("rope", "idx"):
                    heads, half, table = (4, 64, "h") if r.kind == "rope" else (8, 32, "i")
                    rope(r, i, s, heads, half, table).then_inc(rope_ready, 1)
                if r.kind == "ki":
                    link(rope(r, i, 0, 1, 32, "i"))
                    V.tensor_copy(stg[0][:, :, 64:128], stg[0][:, :, 0:64]).then_inc(rope_ready, 1)
                    V.tensor_scalar(wic[:], PS[0][:, :, 0:IDX_HEADS], IDX_HEADS ** -0.5, None, ALU.mult
                                    ).then_inc(ps_free[0], 1)

            def turned(r, i, s):
                if r.kind == "ff" and s == 1:
                    vec.wait_ge(T_hi, r.aT0 + i + 1)
                    V.tensor_tensor(aT_lo[:, ds(i * 4, 4)].rearrange("p a t -> p (a t)"), T[:].rearrange("p a t -> p (a t)"),
                                    aT_hi[:, ds(i * 4, 4)].rearrange("p a t -> p (a t)").bitcast(F32), ALU.subtract
                                    ).then_inc(T_free, 1)

            for r in runs:
                if r.before == "s5":
                    s5()
                elif r.before == "attention":
                    attention()
                if r is runs[0] or r is glu:
                    for n in range(AHEAD):
                        lo_unit(r.unit, n)
                if r.before in ("x", "ln"):
                    make_h(r)
                if r.before == "x":
                    vec.wait_ge(T_full, r.hturn + 4)
                    link(V.tensor_scalar(xz[:].rearrange("p a d -> p (a d)"), xz[:].rearrange("p a d -> p (a d)"), ALPHA,
                                         None, ALU.mult))
                before = runs[runs.index(r) - 1]
                r.chain = chain[0] if r.before else before.chain + before.n * sum(links(before))
                for i, q, q_first in iterations(vec, r):
                    u = r.unit + i * r.per
                    stop = isinstance(i, int) and i == r.n - 1 and (r is runs[0] or r is runs[-1])
                    last = closing(r, i)
                    for n in range(r.per):
                        if n == 0 and last:
                            chain_at(*last, 1)
                            finish(*last, last[0].blocks - 1)
                        if r.blocks == 2 and n == r.units:
                            chain_at(r, i, 0)
                            finish(r, i, 0)
                        if not (stop and n + AHEAD >= r.per):
                            lo_unit(u, n + AHEAD)
                        if r.before == "ln" and isinstance(i, int) and i == 0 and n in (3, 6, 9, 12):
                            affine(r.norm, n // 3 - 1, ALPHA)
                        if q is not None:
                            for kk in ada_at(n, r.per):
                                ada_unit(q, kk)
                            if n == r.per - 1:
                                store_chunk(q, q_first)
                        if n == 3 and last:
                            turned(*last, last[0].blocks - 1)
                        if r.kind == "glu" and n == r.units + 2:
                            vec.wait_ge(sigmoid_done, i + 1)
                            chain_at(r, i, 0)
                            g = grow[:, ds(i * NB, NB)].unsqueeze(1).to_broadcast([P, TOK, NB])
                            link(V.tensor_tensor(stg[0][:], stg[0][:], g, ALU.mult))
                if closes(r):
                    chain_at(r, r.n - 1, 1)
                    finish(r, r.n - 1, r.blocks - 1)
                    turned(r, r.n - 1, r.blocks - 1)
            moments(NORMS)
            for chunk in range(4):
                link(normalise(chunk))
                affine(NORMS, chunk, 1.0, last=out_ready)

        @block.tensor
        def _(pe):
            MM = nc.tensor.matmul

            def turn_T(full, wait, src):
                for sem_, value in wait:
                    pe.wait_ge(sem_, value)
                if not (isinstance(full, int) and full == 1):
                    pe.wait_ge(T_free, full - 1)
                for t in range(TOK):
                    for j in range(4):
                        ins = nc.tensor.transpose(T[:, j // 2, (j % 2) * SEQ + t * P:(j % 2) * SEQ + (t + 1) * P],
                                                  src(t, j), ident[:])
                ins.then_inc(T_full, 1)

            def sum_chunk(q, q_first):
                pe.wait_ge(ada_used, (q + 1) * AU)
                if not (isinstance(q, int) and q == 0):
                    pe.wait_ge(chunk_stored, q)
                if streamed(q_first)[3] is not None:
                    ins = MM(M[:, 1], ones[:], ada_acc[:], start=True, stop=True)
                else:
                    for j in range(AW // P):
                        ins = MM(M[:, 1, j:j + 1], ada_acc[:, j * P:(j + 1) * P], ones[:, 0:1], start=True, stop=True)
                ins.then_inc(chunk_summed, 1)

            def col_product(m, j, unit, by, stop):
                return MM(M[:, 0, m * (CW // P) + j:m * (CW // P) + j + 1], unit[:, j * P:(j + 1) * P], by,
                          start=False, stop=stop)

            def col_units(m, first, end):
                for k in range(first + RING - 1, end, RING):
                    pe.wait_ge(col_landed[k % RING], m * (16 * AU // RING) + 16 * (k // RING + 1))
                    for j in range(CW // P):
                        ins = col_product(m, j, col_raw[0][:, k % RING], csil[:, k:k + 1], False)
                    ins.then_inc(col_used, 1)

            def col_sums(m):
                pe.wait_ge(col_summed, col_before(m + 1, 0)[1])
                for j in range(CW // P):
                    ins = col_product(m, j, col_acc[m % 2], ones[:, 0:1], m == STAGE - 1 and j == CW // P - 1)
                ins.then_inc(col_added, 1)

            def col_row_chunk(m):
                row = 32 * (m - STAGE)
                for k in range(AU):
                    pe.wait_ge(col_landed[k % RING], m * (16 * AU // RING) + 16 * (k // RING + 1))
                    for h in range(2):
                        ins = MM(M[row:row + 1, h], csil[:, k:k + 1], col_raw[1][:, k % RING, h * NB:(h + 1) * NB],
                                 start=k == 0, stop=k == AU - 1)
                    ins.then_inc(col_used, 1)

            pe.wait_ge(constants, 2)
            pe.wait_ge(in_landed, 16 * 9)
            nc.tensor.transpose(M[:, 0, 0:2 * KT], cdn[:], ident[0:2 * KT, 0:2 * KT])
            pe.wait_ge(bias_landed, 64)
            nc.tensor.transpose(M[:, 0, 2 * P:3 * P], biasn[:], ident[:])
            nc.tensor.transpose(M[:, 0, P:2 * P], parn[:], ident[:]).then_inc(pe_prep, 1)
            pe.wait_ge(act_prep, 4)
            pe.wait_ge(bias_ready, 1)
            MM(M[:, 0, 0:STAGE * (CW // P)], ident[:], modcol[:, 0:STAGE * (CW // P)], start=True, stop=False)
            col_units(0, 0, AU - RING)
            pe.wait_ge(dve_prep, 3)

            nc.tensor.transpose(M[:, 1, 0:P], lam_twice[0][:].rearrange("p a n -> p (a n)"), ident[:]).then_inc(pe_prep, 1)
            nc.tensor.transpose(M[:, 1, P:2 * P], lam_twice[1][:].rearrange("p a n -> p (a n)"), ident[:]).then_inc(pe_prep, 1)
            for n in range(8):
                if n >= 4:
                    pe.wait_ge(dve_prep, 6 + n - 4)
                ri, p4 = divmod(n, 4)
                for k in range(4):
                    ins = nc.tensor.transpose(PS[n % 2][:, n // 2 % 2, k * P:(k + 1) * P],
                                              Bbar[ri][:, 4 * p4 + k].rearrange("p a n -> p (a n)"), ident[:])
                ins.then_inc(pe_prep, 1)
            col_units(0, AU - RING, AU)
            col_sums(0)
            col_units(1, 0, AU)
            for n in range(16):
                if n < 4:
                    pe.wait_ge(dve_prep, 13)
                else:
                    pe.wait_ge(act_prep, 6 + n - 4)
                ri, j4 = divmod(n % 8, 4)
                for k in range(4):
                    j = 4 * j4 + k
                    src = Bdiag[ri][:, 4 * j:4 * j + 4].rearrange("p g a k -> p (g a k)") if n < 8 else \
                        Cmask[ri][:, j].rearrange("p a n -> p (a n)")
                    ins = nc.tensor.transpose(PS[n % 2][:, n // 2 % 2, k * P:(k + 1) * P], src, ident[:])
                ins.then_inc(pe_prep, 1)
            pe.wait_ge(dve_prep, 5)
            for m in range(1, STAGE):
                col_sums(m)

            def s5():
                for ch in range(SEQ // TC + 1):
                    if ch < SEQ // TC:
                        for f in range(KT):
                            if f % 4 == 0:
                                pe.wait_ge(uc_ready, 4 * ch + f // 4 + 1)
                            if ch or f >= 4:
                                pe.wait_ge(bu_read, KT * ch + f - 3)
                            elif f == 0:
                                for s in range(2):
                                    pe.wait_ge(ps_free[s], s5_in.n)
                            for ri in range(2):
                                ins = MM(PS[f % 4 // 2][:, f % 2, ri * 4 * TC:(ri + 1) * 4 * TC], Btab[ri][:, f, :],
                                         uc[:, f // 4 % 2, f % 4].rearrange("p g t -> p (g t)"), start=True, stop=True)
                            ins.then_inc(bu_full, 1)
                    if ch >= 1:
                        if ch == 1:
                            pe.wait_ge(chunk_stored, 2)
                        col_row_chunk(STAGE + ch - 1)
                        b = (ch - 1) % 2
                        pe.wait_ge(states_ready, ch)
                        if ch >= 2:
                            pe.wait_ge(y_ready, ch - 1)
                        for f in range(KT):
                            for g in range(4):
                                rows = slice(32 * g, 32 * g + 32)
                                for ri in range(2):
                                    ins = MM(T[rows, f // 8, f % 8 * TC:f % 8 * TC + TC], Ctab[ri][:, f, rows],
                                             st[b][:, :, ri, 4 * f + g], start=ri == 0, stop=ri == 1)
                        ins.then_inc(y_full, 1)
                pe.wait_ge(rows_read, 1)
                for c in range(STAGE):
                    for j in range(CW // P):
                        ins = MM(PS[c // 2][:, c % 2, j:j + 1], col_row[32 * c:32 * c + 1, j * P:(j + 1) * P],
                                 ones[32 * c:32 * c + 1, 0:1], start=True, stop=True)
                ins.then_inc(rows_turned, 1)

            def attention():
                n = 0
                pe.wait_ge(T_free, attn_out.turn)
                pe.wait_ge(ps_free[0], attn_out.use[0])
                pe.wait_ge(ps_free[1], attn_out.use[1])
                for t in range(TOK):
                    N = (t + 1) * P
                    for h in range(IDX_HEADS):
                        if n >= 4:
                            pe.wait_ge(idx_relu, n - 3)
                        rows = slice(64 * (h % 2), 64 * (h % 2) + 64)
                        MM(PS[h % 2][:, h // 2 % 2, 0:N], qiT[rows, h // 2, t * P:(t + 1) * P], kiT[rows, 0:N],
                           start=True, stop=True).then_inc(idx_full, 1)
                        n += 1
                A = TOK * HEADS
                pe.wait_ge(idx_relu, n)
                pe.wait_ge(chunk_stored, attn_out_chunks)

                def logits(a):
                    t, h = divmod(a, HEADS)
                    N = (t + 1) * P
                    if a >= 4:
                        pe.wait_ge(lg_ready, a - 3)
                    MM(PS[a % 2][:, a // 2 % 2, 0:N], qkT[:, h, t * P:(t + 1) * P], qkT[:, HEADS + h, 0:N],
                       start=True, stop=True).then_inc(lg_full, 1)

                logits(0)
                logits(1)
                for a in range(A + 2):
                    if a + 2 < A:
                        logits(a + 2)
                    if 1 <= a <= A:
                        b = a - 1
                        pe.wait_ge(p_ready, b + 1)
                        if b >= 2:
                            pe.wait_ge(pT_ready, b - 1)
                        for k in range(b // HEADS + 1):
                            ins = nc.tensor.transpose(T[:, b % 2, k * P:(k + 1) * P], prob[:, b % 2, k * P:(k + 1) * P], ident[:])
                        ins.then_inc(pT_full, 1)
                    if a >= 2:
                        b = a - 2
                        t, h = divmod(b, HEADS)
                        pe.wait_ge(pT_ready, b + 1)
                        if b % 4 == 0 and b >= 8:
                            pe.wait_ge(o_ready, b // 4 - 1)
                        for k in range(t + 1):
                            ins = MM(M[:, b // 4 % 2, b % 4 * P:(b % 4 + 1) * P], v[:, k, h * P:(h + 1) * P],
                                     probT[:, b % 2, k * P:(k + 1) * P], start=k == 0, stop=k == t)
                        if b % 4 == 3:
                            ins.then_inc(o_full, 1)

            def turn_x(r, g):
                wait = [(x_landed, 16)] if r.before == "x" else [(xn_ready, 4 * r.norm + g + 1)]
                turn_T(r.hturn + g + 1, wait, lambda t, j: xz[:, t, g * NB + j * P:g * NB + (j + 1) * P])

            def turn(r, i, s):
                if r.kind in ("u", "rope", "idx"):
                    ready = (ps_free[s], r.use[s] + i + 1) if r.kind == "u" else (rope_ready, r.roped + i * 2 + (s + 1))
                    turn_T(r.turn + i * r.turns + (s + 1), [ready], lambda t, j: stg[s][:, t, j * P:(j + 1) * P])
                if r.kind == "ff" and s == 1:
                    turn_T(r.turn + i + 1, [(ps_free[1], r.use[1] + i + 1)], lambda t, j: stg[1][:, t, j * P:(j + 1) * P])
                if r.kind == "ki":
                    pe.wait_ge(rope_ready, r.roped + 1)
                    pe.wait_ge(T_free, r.turn)
                    for t in range(TOK):
                        ins = nc.tensor.transpose(T[:, 0, t * P:(t + 1) * P], stg[0][:, t, 0:P], ident[:])
                    ins.then_inc(T_full, 1)

            pe.wait_ge(act_prep, 21)
            for r in runs:
                if r.before in ("x", "ln"):
                    turn_x(r, 0)
                    turn_x(r, 1)
                elif r.before == "s5":
                    s5()
                elif r.before == "attention":
                    attention()
                for i, q, q_first in iterations(pe, r):
                    u = r.unit + i * r.per
                    last = closing(r, i)
                    for n in range(r.per):
                        s, k = divmod(n, r.units)
                        if n == 3 and last:
                            turn(*last, last[0].blocks - 1)
                        if r.before in ("x", "ln") and isinstance(i, int) and i == 0 and n in (1, 2):
                            turn_x(r, n + 1)
                        if s == 1 and k == 3:
                            turn(r, i, 0)
                        if k == 0 and not (isinstance(i, int) and r.use[s] + i == 0):
                            pe.wait_ge(ps_free[s], r.use[s] + i)
                        pe.wait_ge(w_lo_ready, u + (n + 1))
                        if r.kind == "z" and r.before is None:
                            pe.wait_ge(T_free, ff_turn + k // 2 + 1)
                            hi, lo = aT_hi, aT_lo
                        else:
                            if r.kind == "glu":
                                pe.wait_ge(s5_done, SEQ // TC)
                            elif r.before == "attention":
                                pe.wait_ge(o_ready, (TOK - 1) * HEADS // 4 + k // 2 + 1)
                            elif r.before in ("x", "ln"):
                                pe.wait_ge(h_ready, r.h0 + k // 2 + 1)
                            hi, lo = hT_hi, hT_lo
                        for t in range(TOK):
                            for kk in range(UK):
                                kt = k * UK + kk
                                tok = slice(t * P, (t + 1) * P)
                                for m, (a_, b_) in enumerate(((hi, w_hi), (hi, w_lo), (lo, w_hi))):
                                    ins = MM(PS[s][:, t, 0:r.width], a_[:, kt, tok], b_[:, n % RING, kk, 0:r.width],
                                             start=kt == 0 and m == 0,
                                             stop=k == r.units - 1 and kk == UK - 1 and m == 2)
                        ins.then_inc(w_used, 1)
                        if q is not None and n == r.per - 3:
                            sum_chunk(q, q_first)
                if closes(r):
                    turn(r, r.n - 1, r.blocks - 1)
                if r.kind == "ff":
                    ff_turn = r.turn


_INS = ["x", "c", "positions", "ada_w", "ada_b", "ln_g", "ln_b", "s5_in_w", "s5_a_re", "s5_a_im", "s5_log_dt", "s5_b_re",
        "s5_b_im", "s5_c_re", "s5_c_im", "s5_d", "s5_glu_w", "s5_glu_b", "dsa_in_w", "dsa_out_w", "ffn_w_in", "ffn_w_out"]


def kernel(**inputs):
    import concourse.bacc as bacc
    from concourse.bass_utils import run_bass_kernel_spmd

    nc = bacc.Bacc("TRN2", target_bir_lowering=False, num_devices=1)
    arrays, args = {}, []
    for name in _INS:
        a = np.ascontiguousarray(inputs[name])
        arrays[f"in_{name}"] = a
        args.append(nc.dram_tensor(f"in_{name}", a.shape, mybir.dt.from_np(a.dtype), kind="ExternalInput").ap())
    arrays["in_consts"] = shape_constants()
    args.append(nc.dram_tensor("in_consts", (P, 98), F32, kind="ExternalInput").ap())
    args.append(nc.dram_tensor("out", (1, SEQ, D), F32, kind="ExternalOutput").ap())
    build(nc, *args)
    r = run_bass_kernel_spmd(nc, [arrays], core_ids=[0])
    return r.results[0]["out"]
```
